# Optimizing a Trainium2 kernel written in Bass

```python
import math
import functools
import jax
import jax.numpy as jnp
from jax import lax
import numpy as np

D_MODEL = 1024
BATCH = 1
SEQ = 512
DEPTH = 2

HEAD_DIM = 64
D_FF = 4 * D_MODEL
RMS_EPS = 1e-6

RWKV_HEADS = 8
RWKV_WIDTH = RWKV_HEADS * HEAD_DIM
RWKV_DECAY_LORA = 64
RWKV_A_LORA = 64
RWKV_GATE_LORA = 128
RWKV_GN_EPS = 6.4e-4
RWKV_SIZES = (RWKV_WIDTH, RWKV_WIDTH, RWKV_WIDTH, RWKV_DECAY_LORA, RWKV_A_LORA, RWKV_GATE_LORA)
RWKV_COLS = sum(RWKV_SIZES)

GDN_HEADS = 8
GDN_WIDTH = GDN_HEADS * HEAD_DIM
GDN_CONV = 4
GDN_CHUNK = 64
GDN_SIZES = (3 * GDN_WIDTH, GDN_HEADS, GDN_HEADS, GDN_WIDTH)
GDN_COLS = sum(GDN_SIZES)

EVEN_COLS = RWKV_COLS + GDN_COLS
EVEN_MIX_WIDTH = RWKV_WIDTH + GDN_WIDTH

DSA_HEADS = 8
DSA_KV_HEADS = 2
DSA_GROUP = DSA_HEADS // DSA_KV_HEADS
DSA_WIDTH = DSA_HEADS * HEAD_DIM
IDX_HEADS = 8
IDX_DIM = 64
DSA_TOPK_MAX = 256
DSA_Q_BLOCK = 128

MOBA_HEADS = 8
MOBA_WIDTH = MOBA_HEADS * HEAD_DIM
MOBA_BLOCK = 256
MOBA_TOPK = 3
MOBA_Q_BLOCK = 32

ODD_SIZES = (DSA_WIDTH, 2 * DSA_KV_HEADS * HEAD_DIM, IDX_HEADS * IDX_DIM, IDX_DIM, IDX_HEADS, MOBA_WIDTH, MOBA_WIDTH, MOBA_WIDTH)
ODD_COLS = sum(ODD_SIZES)
ODD_MIX_WIDTH = DSA_WIDTH + MOBA_WIDTH
ALIBI_HEADS = DSA_HEADS + MOBA_HEADS

kernel_name = 'hybrid_rwkv7_gdn_dsa_moba_trunk'

def split_cols(p, sizes):
    offs = np.cumsum((0,) + tuple(sizes))
    return [p[..., int(offs[i]):int(offs[i + 1])] for i in range(len(sizes))]

def rms_norm(x, g, eps=RMS_EPS):
    xf = x.astype(jnp.float32)
    y = xf * lax.rsqrt(jnp.mean(xf * xf, axis=-1, keepdims=True) + eps)
    return (y * g.astype(jnp.float32)).astype(x.dtype)

def layer_norm(x, w, b, eps=1e-6):
    xf = x.astype(jnp.float32)
    xc = xf - jnp.mean(xf, axis=-1, keepdims=True)
    y = xc * lax.rsqrt(jnp.mean(xc * xc, axis=-1, keepdims=True) + eps)
    return (y * w.astype(jnp.float32) + b.astype(jnp.float32)).astype(x.dtype)

def l2_normalize(x, eps=1e-6):
    xf = x.astype(jnp.float32)
    return (xf * lax.rsqrt(jnp.sum(xf * xf, axis=-1, keepdims=True) + eps)).astype(x.dtype)

def token_shift(x):
    return jnp.pad(x, ((0, 0), (1, 0), (0, 0)))[:, :-1]

def causal_depthwise_conv(x, w):
    K, C = w.shape
    return lax.conv_general_dilated(x, w[:, None, :].astype(x.dtype), window_strides=(1,), padding=[(K - 1, 0)], dimension_numbers=('NWC', 'WIO', 'NWC'), feature_group_count=C)

def alibi_slopes(n):
    return 2.0 ** (-8.0 * jnp.arange(1, n + 1, dtype=jnp.float32) / n)

def rwkv7_scan(r, log_w, k, v, a, b):
    B, T, H, N = r.shape

    def step(S, inp):
        r_t, w_t, k_t, v_t, a_t, b_t = inp
        sa = jnp.einsum('bhvk,bhk->bhv', S, a_t)
        S = S * w_t[:, :, None, :] + sa[..., None] * b_t[:, :, None, :] + v_t[..., None] * k_t[:, :, None, :]
        return S, jnp.einsum('bhvk,bhk->bhv', S, r_t)

    xs = tuple(jnp.moveaxis(t.astype(jnp.float32), 1, 0) for t in (r, jnp.exp(log_w), k, v, a, b))
    S0 = jnp.zeros((B, H, N, N), jnp.float32)
    _, o = lax.scan(step, S0, xs)
    return jnp.moveaxis(o, 0, 1)

def rwkv7_mix(p, mu, w0, w2, a0, a2, g2, k_k, k_a, r_k, lnx_w, lnx_b):
    B, T, _ = p.shape
    H, N = RWKV_HEADS, HEAD_DIM
    f32 = jnp.float32
    p = p + (token_shift(p) - p) * mu
    r, k, v, wd, ad, gd = split_cols(p, RWKV_SIZES)
    w_pre = (w0 + jnp.tanh(wd) @ w2).astype(f32)
    log_decay = -jnp.exp(-jax.nn.softplus(-w_pre) - 0.5)
    a = jax.nn.sigmoid(a0 + ad @ a2)
    g = jax.nn.sigmoid(gd) @ g2
    kk = l2_normalize((k * k_k).reshape(B, T, H, N))
    k = k * (1.0 + (a - 1.0) * k_a)

    def heads(t):
        return t.reshape(B, T, H, N)

    r_h, k_h, v_h, a_h = heads(r), heads(k), heads(v), heads(a)
    o = rwkv7_scan(r_h, heads(log_decay), k_h, v_h, -kk, kk * a_h)
    oc = o - jnp.mean(o, axis=-1, keepdims=True)
    o = oc * lax.rsqrt(jnp.mean(oc * oc, axis=-1, keepdims=True) + RWKV_GN_EPS)
    o = o.reshape(B, T, RWKV_WIDTH) * lnx_w.astype(f32) + lnx_b.astype(f32)
    bonus = jnp.sum((r_h * k_h * r_k).astype(f32), axis=-1, keepdims=True) * v_h.astype(f32)
    o = o + bonus.reshape(B, T, RWKV_WIDTH)
    return (o * g.astype(f32)).astype(p.dtype)

def chunk_gated_delta_rule(q, k, v, g, beta):
    B, T, H, N = q.shape
    C = GDN_CHUNK
    f32 = jnp.float32
    pad = (-T) % C

    def chunks(t):
        t = jnp.pad(t.astype(f32), [(0, 0), (0, pad)] + [(0, 0)] * (t.ndim - 2))
        t = jnp.moveaxis(t, 2, 1)
        return t.reshape((B, H, -1, C) + t.shape[3:])

    q = chunks(q) * (N ** -0.5)
    k, v = chunks(k), chunks(v)
    g = jnp.cumsum(chunks(g), axis=-1)
    beta = chunks(beta)
    causal = jnp.tril(jnp.ones((C, C), dtype=bool))
    strict = jnp.tril(jnp.ones((C, C), dtype=bool), -1)
    decay = jnp.exp(jnp.where(causal, g[..., :, None] - g[..., None, :], -jnp.inf))
    k_beta = k * beta[..., None]
    a_mat = jnp.where(strict, jnp.einsum('bhnik,bhnjk->bhnij', k_beta, k) * decay, 0.0) + jnp.eye(C, dtype=f32)
    tri = functools.partial(lax.linalg.triangular_solve, left_side=True, lower=True, unit_diagonal=True)
    u = tri(a_mat, v * beta[..., None])
    w = tri(a_mat, k_beta * jnp.exp(g)[..., None])
    qk = jnp.where(causal, jnp.einsum('bhnik,bhnjk->bhnij', q, k) * decay, 0.0)

    def step(S, inp):
        q_c, k_c, u_c, w_c, g_c, qk_c = inp
        v_new = u_c - jnp.einsum('bhck,bhkv->bhcv', w_c, S)
        o_c = jnp.einsum('bhck,bhkv->bhcv', q_c * jnp.exp(g_c)[..., None], S) + jnp.einsum('bhij,bhjv->bhiv', qk_c, v_new)
        g_last = g_c[..., -1:]
        S = S * jnp.exp(g_last)[..., None] + jnp.einsum('bhck,bhcv->bhkv', k_c * jnp.exp(g_last - g_c)[..., None], v_new)
        return S, o_c

    xs = tuple(jnp.moveaxis(t, 2, 0) for t in (q, k, u, w, g, qk))
    S0 = jnp.zeros((B, H, N, v.shape[-1]), f32)
    _, o = lax.scan(step, S0, xs)
    o = jnp.moveaxis(o, 0, 2).reshape(B, H, -1, N)[:, :, :T]
    return jnp.moveaxis(o, 1, 2)

def gated_deltanet_mix(p, conv_w, a_log, dt_bias, norm_w):
    B, T, _ = p.shape
    H, N = GDN_HEADS, HEAD_DIM
    f32 = jnp.float32
    qkv, b_in, a_in, z = split_cols(p, GDN_SIZES)
    qkv = jax.nn.silu(causal_depthwise_conv(qkv, conv_w))
    q, k, v = (t.reshape(B, T, H, N) for t in split_cols(qkv, (GDN_WIDTH, GDN_WIDTH, GDN_WIDTH)))
    q, k = l2_normalize(q), l2_normalize(k)
    beta = jax.nn.sigmoid(b_in.astype(f32))
    g = -jnp.exp(a_log.astype(f32)) * jax.nn.softplus(a_in.astype(f32) + dt_bias.astype(f32))
    o = chunk_gated_delta_rule(q, k, v, g, beta)
    o = rms_norm(o, norm_w) * jax.nn.silu(z.astype(f32)).reshape(B, T, H, N)
    return o.reshape(B, T, GDN_WIDTH).astype(p.dtype)

def dsa_attention(q, kv, iq, ik, iw, q_norm, k_norm, ln_w, ln_b, slopes):
    B, T, _ = q.shape
    H, KV, G, N = DSA_HEADS, DSA_KV_HEADS, DSA_GROUP, HEAD_DIM
    f32 = jnp.float32
    top_k = min(DSA_TOPK_MAX, T // 4)
    QB = DSA_Q_BLOCK if T % DSA_Q_BLOCK == 0 else T
    n_qb = T // QB
    q = rms_norm(q.reshape(B, T, H, N), q_norm)
    k_in, v_in = split_cols(kv, (KV * N, KV * N))
    k = rms_norm(k_in.reshape(B, T, KV, N), k_norm)
    v = v_in.reshape(B, T, KV, N)
    iq = iq.reshape(B, T, IDX_HEADS, IDX_DIM)
    ik = layer_norm(ik, ln_w, ln_b)
    iw = iw.astype(f32) * IDX_HEADS ** -0.5
    s_pos = jnp.arange(T)
    b_idx = jnp.arange(B)[:, None, None]
    m = slopes.reshape(KV, G)[None, None, :, :, None]

    def one_block(args):
        q_b, iq_b, iw_b, start = args
        t_pos = start + jnp.arange(QB)
        logits = jnp.einsum('bqhd,bsd->bqhs', iq_b, ik).astype(f32) * IDX_DIM ** -0.5
        score = jnp.einsum('bqh,bqhs->bqs', iw_b, jax.nn.relu(logits))
        score = jnp.where(s_pos[None, None, :] <= t_pos[None, :, None], score, -jnp.inf)
        _, idx = lax.top_k(score, top_k)
        k_sel = k[b_idx, idx]
        v_sel = v[b_idx, idx]
        dist = (t_pos[None, :, None] - idx).astype(f32)
        sc = jnp.einsum('bqgrn,bqsgn->bqgrs', q_b.reshape(B, QB, KV, G, N), k_sel).astype(f32) * N ** -0.5
        sc = sc - m * dist[:, :, None, None, :]
        sc = jnp.where((dist >= 0)[:, :, None, None, :], sc, -jnp.inf)
        pr = jax.nn.softmax(sc, axis=-1).astype(v.dtype)
        o = jnp.einsum('bqgrs,bqsgn->bqgrn', pr, v_sel)
        return o.reshape(B, QB, DSA_WIDTH)

    def blocks(t):
        return jnp.moveaxis(t.reshape((B, n_qb, QB) + t.shape[2:]), 1, 0)

    o = lax.map(one_block, (blocks(q), blocks(iq), blocks(iw), jnp.arange(n_qb) * QB))
    return jnp.moveaxis(o, 0, 1).reshape(B, T, DSA_WIDTH)

def moba_attention(q, k, v, q_norm, k_norm, slopes):
    B, T, _ = q.shape
    H, N, BS, QB = MOBA_HEADS, HEAD_DIM, MOBA_BLOCK, MOBA_Q_BLOCK
    f32 = jnp.float32
    n_kb = -(-T // BS)
    t_pad = n_kb * BS
    n_sel = min(MOBA_TOPK, n_kb - 1)
    pad = ((0, 0), (0, t_pad - T), (0, 0), (0, 0))
    q = jnp.pad(rms_norm(q.reshape(B, T, H, N), q_norm), pad)
    k = jnp.pad(rms_norm(k.reshape(B, T, H, N), k_norm), pad)
    v = jnp.pad(v.reshape(B, T, H, N), pad)
    k_bh = jnp.transpose(k.reshape(B, n_kb, BS, H, N), (0, 3, 1, 2, 4))
    v_bh = jnp.transpose(v.reshape(B, n_kb, BS, H, N), (0, 3, 1, 2, 4))
    k_mean = jnp.mean(k_bh.astype(f32), axis=3)
    scale = N ** -0.5
    b_idx = jnp.arange(B)[:, None, None, None]
    h_idx = jnp.arange(H)[None, None, :, None]

    def one_block(args):
        q_b, start = args
        t_pos = start + jnp.arange(QB)
        own = start // BS
        k_own = lax.dynamic_slice_in_dim(k, own * BS, BS, axis=1)
        v_own = lax.dynamic_slice_in_dim(v, own * BS, BS, axis=1)
        dist = (t_pos[:, None] - (own * BS + jnp.arange(BS))[None, :]).astype(f32)
        sc = jnp.einsum('bqhn,bshn->bqhs', q_b, k_own).astype(f32) * scale - slopes[None, None, :, None] * dist[None, :, None, :]
        sc = jnp.where((dist >= 0)[None, :, None, :], sc, -jnp.inf)
        if n_sel == 0:
            pr = jax.nn.softmax(sc, axis=-1).astype(v.dtype)
            return jnp.einsum('bqhs,bshn->bqhn', pr, v_own)
        gate = jnp.einsum('bqhn,bhjn->bqhj', q_b.astype(f32), k_mean)
        gate = jnp.where(jnp.arange(n_kb) < own, gate, -jnp.inf)
        _, sel = lax.top_k(gate, n_sel)
        k_sel = k_bh[b_idx, h_idx, sel]
        v_sel = v_bh[b_idx, h_idx, sel]
        sel_pos = sel[..., None] * BS + jnp.arange(BS)
        dist_sel = (t_pos[None, :, None, None, None] - sel_pos).astype(f32)
        sc_sel = jnp.einsum('bqhn,bqhjsn->bqhjs', q_b, k_sel).astype(f32) * scale - slopes[None, None, :, None, None] * dist_sel
        sc_sel = jnp.where((sel < own)[..., None], sc_sel, -jnp.inf)
        sc_all = jnp.concatenate([sc, sc_sel.reshape(B, QB, H, n_sel * BS)], axis=-1)
        pr = jax.nn.softmax(sc_all, axis=-1).astype(v.dtype)
        o = jnp.einsum('bqhs,bshn->bqhn', pr[..., :BS], v_own)
        o = o + jnp.einsum('bqhjs,bqhjsn->bqhn', pr[..., BS:].reshape(B, QB, H, n_sel, BS), v_sel)
        return o

    n_qb = t_pad // QB
    q_blocks = jnp.moveaxis(q.reshape(B, n_qb, QB, H, N), 1, 0)
    o = lax.map(one_block, (q_blocks, jnp.arange(n_qb) * QB))
    return jnp.moveaxis(o, 0, 1).reshape(B, t_pad, MOBA_WIDTH)[:, :T]

def even_mixer(h, w_in, w_out, mu, w0, w2, a0, a2, g2, k_k, k_a, r_k, lnx_w, lnx_b, conv_w, a_log, dt_bias, gdn_norm_w):
    p = h @ w_in
    o_a = rwkv7_mix(p[..., :RWKV_COLS], mu, w0, w2, a0, a2, g2, k_k, k_a, r_k, lnx_w, lnx_b)
    o_b = gated_deltanet_mix(p[..., RWKV_COLS:], conv_w, a_log, dt_bias, gdn_norm_w)
    return jnp.concatenate([o_a, o_b], axis=-1) @ w_out

def odd_mixer(h, w_in, w_out, dsa_q_norm, dsa_k_norm, idx_k_ln_w, idx_k_ln_b, moba_q_norm, moba_k_norm):
    p = h @ w_in
    dq, dkv, iq, ik, iw, mq, mk, mv = split_cols(p, ODD_SIZES)
    slopes = alibi_slopes(ALIBI_HEADS)
    o_c = dsa_attention(dq, dkv, iq, ik, iw, dsa_q_norm, dsa_k_norm, idx_k_ln_w, idx_k_ln_b, slopes[0::2])
    o_d = moba_attention(mq, mk, mv, moba_q_norm, moba_k_norm, slopes[1::2])
    return jnp.concatenate([o_c, o_d], axis=-1) @ w_out

def relu2_mlp(h, w1, w2):
    return jnp.square(jax.nn.relu(h @ w1)) @ w2

def setup_inputs(seed: int = 0) -> dict:
    key = jax.random.key(seed)
    keys = iter(jax.random.split(key, 64))
    f32 = jnp.float32

    def normal(shape, scale):
        return jax.random.normal(next(keys), shape, f32) * scale

    def uniform(shape, lo, hi):
        return jax.random.uniform(next(keys), shape, f32, lo, hi)

    ne = (DEPTH + 1) // 2
    no = DEPTH // 2
    dt = jnp.exp(uniform((ne, GDN_HEADS), math.log(1e-3), math.log(1e-1)))
    return {
        'x': normal((BATCH, SEQ, D_MODEL), 1.0),
        'norm1_g': 1.0 + normal((DEPTH, D_MODEL), 0.05),
        'norm2_g': 1.0 + normal((DEPTH, D_MODEL), 0.05),
        'mlp_w1': normal((DEPTH, D_MODEL, D_FF), D_MODEL ** -0.5),
        'mlp_w2': normal((DEPTH, D_FF, D_MODEL), D_FF ** -0.5),
        'ev_w_in': normal((ne, D_MODEL, EVEN_COLS), D_MODEL ** -0.5),
        'ev_w_out': normal((ne, EVEN_MIX_WIDTH, D_MODEL), EVEN_MIX_WIDTH ** -0.5),
        'rwkv_mu': uniform((ne, RWKV_COLS), 0.0, 1.0),
        'rwkv_w0': uniform((ne, RWKV_WIDTH), -6.5, -1.5),
        'rwkv_w2': normal((ne, RWKV_DECAY_LORA, RWKV_WIDTH), 0.5 * RWKV_DECAY_LORA ** -0.5),
        'rwkv_a0': normal((ne, RWKV_WIDTH), 0.1),
        'rwkv_a2': normal((ne, RWKV_A_LORA, RWKV_WIDTH), 0.5 * RWKV_A_LORA ** -0.5),
        'rwkv_g2': normal((ne, RWKV_GATE_LORA, RWKV_WIDTH), RWKV_GATE_LORA ** -0.5),
        'rwkv_k_k': 0.85 + normal((ne, RWKV_WIDTH), 0.05),
        'rwkv_k_a': 1.0 + normal((ne, RWKV_WIDTH), 0.05),
        'rwkv_r_k': normal((ne, RWKV_HEADS, HEAD_DIM), 0.1),
        'rwkv_lnx_w': 1.0 + normal((ne, RWKV_WIDTH), 0.05),
        'rwkv_lnx_b': normal((ne, RWKV_WIDTH), 0.02),
        'gdn_conv_w': normal((ne, GDN_CONV, 3 * GDN_WIDTH), GDN_CONV ** -0.5),
        'gdn_a_log': jnp.log(uniform((ne, GDN_HEADS), 1.0, 16.0)),
        'gdn_dt_bias': dt + jnp.log(-jnp.expm1(-dt)),
        'gdn_norm_w': 1.0 + normal((ne, HEAD_DIM), 0.05),
        'od_w_in': normal((no, D_MODEL, ODD_COLS), D_MODEL ** -0.5),
        'od_w_out': normal((no, ODD_MIX_WIDTH, D_MODEL), ODD_MIX_WIDTH ** -0.5),
        'dsa_q_norm': 1.0 + normal((no, HEAD_DIM), 0.05),
        'dsa_k_norm': 1.0 + normal((no, HEAD_DIM), 0.05),
        'idx_k_ln_w': 1.0 + normal((no, IDX_DIM), 0.05),
        'idx_k_ln_b': normal((no, IDX_DIM), 0.02),
        'moba_q_norm': 1.0 + normal((no, HEAD_DIM), 0.05),
        'moba_k_norm': 1.0 + normal((no, HEAD_DIM), 0.05),
    }

def reference(x, norm1_g, norm2_g, mlp_w1, mlp_w2, ev_w_in, ev_w_out, rwkv_mu, rwkv_w0, rwkv_w2, rwkv_a0, rwkv_a2, rwkv_g2, rwkv_k_k, rwkv_k_a, rwkv_r_k, rwkv_lnx_w, rwkv_lnx_b, gdn_conv_w, gdn_a_log, gdn_dt_bias, gdn_norm_w, od_w_in, od_w_out, dsa_q_norm, dsa_k_norm, idx_k_ln_w, idx_k_ln_b, moba_q_norm, moba_k_norm):
    for i in range(DEPTH):
        j = i // 2
        h = rms_norm(x, norm1_g[i])
        if i % 2 == 0:
            mix = even_mixer(h, ev_w_in[j], ev_w_out[j], rwkv_mu[j], rwkv_w0[j], rwkv_w2[j], rwkv_a0[j], rwkv_a2[j], rwkv_g2[j], rwkv_k_k[j], rwkv_k_a[j], rwkv_r_k[j], rwkv_lnx_w[j], rwkv_lnx_b[j], gdn_conv_w[j], gdn_a_log[j], gdn_dt_bias[j], gdn_norm_w[j])
        else:
            mix = odd_mixer(h, od_w_in[j], od_w_out[j], dsa_q_norm[j], dsa_k_norm[j], idx_k_ln_w[j], idx_k_ln_b[j], moba_q_norm[j], moba_k_norm[j])
        x = x + mix.astype(x.dtype)
        x = x + relu2_mlp(rms_norm(x, norm2_g[i]), mlp_w1[i], mlp_w2[i]).astype(x.dtype)
    return x


_drawn_inputs = setup_inputs


def setup_inputs(seed=0):
    import zlib

    import numpy as np

    out = dict(_drawn_inputs(seed))
    spreads = {}
    factors = {'rwkv_lnx_b': 2.85,
     'dsa_q_norm': 8.0,
     'dsa_k_norm': 8.0,
     'idx_k_ln_b': 2.931,
     'moba_q_norm': 8.0,
     'moba_k_norm': 8.0}
    for name, (base, spread) in spreads.items():
        noise = np.random.default_rng([zlib.crc32(name.encode()), seed]).standard_normal(out[name].shape)
        drawn = base * np.exp(spread * noise) if base else spread * noise
        out[name] = jnp.asarray(drawn.astype(out[name].dtype))
    for name, factor in factors.items():
        out[name] = (out[name] * factor).astype(out[name].dtype)
    return out
```

```python
from contextlib import ExitStack, contextmanager

import numpy as np

import concourse.bass as bass
from concourse import mybir

F32 = mybir.dt.float32
I32 = mybir.dt.int32
ALU = mybir.AluOpType
ACT = mybir.ActivationFunctionType
AX = mybir.AxisListType

P = 128
SEQ = 512
D = 1024
DFF = 4096
HD = 64
KT = D // P
TT = SEQ // P
W = SEQ
NH = 8
PAIRS = NH // 2
PW = 516
CW = P + 1
LEVELS = 7
RMS_EPS = 1e-6
GN_EPS = 6.4e-4
RWKV_COLS = 1792
GDN_QKV = RWKV_COLS
GDN_BA = RWKV_COLS + 3 * 512
GDN_Z = GDN_BA + 2 * NH
OD_K, OD_V, OD_IQ, OD_IK, OD_IW = 512, 640, 768, 1280, 1344
OD_MQ = 1352
OD_MV = OD_MQ + 1024
TOPK = min(256, SEQ // 4)
CAUSAL_FILL = -3.0e38
TAKEN = -3.4e38
FAR = 1.0e30


class Tally:

    def __init__(self, eng, sem):
        self.eng, self.sem, self.n, self.loops = eng, sem, 0, []

    @contextmanager
    def loop(self, reg, per, trips, first=0):
        start = self.n
        self.loops.append((reg, per, first))
        yield
        self.loops.pop()
        assert self.n - start == per, (self.n - start, per)
        self.n = start + per * trips

    def value(self, n=None):
        v = self.n if n is None else n
        for reg, per, first in self.loops:
            v = (reg * per) + (v - first * per)
        return v

    def step(self, ins):
        self.n += 1
        return ins.then_inc(self.sem, 1)

    def settle(self):
        self.eng.wait_ge(self.sem, self.value())

    def link(self, ins):
        self.step(ins)
        self.settle()


def trunk_kernel(nc, a, out):
    ctx = ExitStack()
    with ctx:
        def sem(name):
            return ctx.enter_context(nc.semaphore(name))

        ARENA = 52800
        A = ctx.enter_context(nc.sbuf_tensor("arena", [P, ARENA], F32))
        bank = [ctx.enter_context(nc.psum_tensor(f"bank{i}", [P, 512], F32)) for i in range(8)]

        top = [0]

        def carve(n):
            off = top[0]
            top[0] += n
            assert top[0] <= ARENA, top[0]
            return off

        def flat(off, n):
            return A[:, off:off + n]

        def grid(off, n, w):
            return A[:, off:off + n * w].rearrange("p (n w) -> p n w", n=n)

        def wide(x):
            return x.rearrange("p n w -> p (n w)")

        XT = grid(carve(KT * W), KT, W)
        IDENT, ONES = flat(carve(P), P), flat(carve(P), P)
        HEADS2 = flat(carve(P), P)
        INCL = flat(carve(P), P)
        STRICT = flat(carve(P), P)
        o_merge = carve(LEVELS * P)
        MERGE = grid(o_merge, LEVELS, P)
        SCANM = flat(carve(4 * CW), 4 * CW)
        PC = flat(carve(P), P)
        PC2 = flat(carve(8), 8)
        misc = [carve(576)]
        misc_end = top[0]

        def small(n):
            off = misc[0]
            misc[0] += n
            assert misc[0] <= misc_end
            return flat(off, n)

        def by_chunk(n):
            return small(TT * n).rearrange("p (c h) -> p c h", c=TT)

        OMKA = small(4)
        ALOG, DTB, NEA = small(NH), small(NH), small(NH)
        AB = by_chunk(16)
        BETA, GLOG, GTMP, GCUM = by_chunk(NH), by_chunk(NH), by_chunk(NH), by_chunk(NH)
        EG = by_chunk(NH)
        EREST = by_chunk(NH)
        ESTATE = by_chunk(PAIRS)
        SM, ESM = small(8), small(8)
        NMEAN, VAR, RSTD = small(NH), small(16), small(16)
        SLOPE = small(16)
        QW = small(2)
        IW = by_chunk(NH)
        IWW = small(KT * NH).rearrange("p (k n) -> p k n", k=KT)
        M8 = small(8)
        NMX, RSUM, RINV = small(NH), small(NH), small(NH)

        o_ht = carve(KT * W)
        HT = grid(o_ht, KT, W)
        o_ring = carve(2 * KT * W)
        RING = A[:, o_ring:o_ring + 2 * KT * W].rearrange("p (s k n) -> p s k n", s=2, k=KT)
        work = top[0]

        o_rkv, o_gqkv = carve(12 * W), carve(12 * W)
        o_z, o_kk, o_b, o_g, o_bon = (carve(4 * W) for _ in range(5))
        o_cum = carve(4 * 4 * CW)
        RKV, GQKV = grid(o_rkv, 12, W), grid(o_gqkv, 12, W)
        R, K, V = (grid(o_rkv + i * 4 * W, 4, W) for i in range(3))
        GQ, GK, GV = (grid(o_gqkv + i * 4 * W, 4, W) for i in range(3))
        Z, KK, B, G, BON = (grid(o, 4, W) for o in (o_z, o_kk, o_b, o_g, o_bon))
        CUM = A[:, o_cum:o_cum + 16 * CW].rearrange("p (c k t) -> p c k t", c=4, k=4)
        tail = top[0]
        XIN = grid(o_gqkv, TT, D)
        PR, PR2 = flat(o_z, P), flat(o_z + P, P)
        SQ = [grid(o_g, KT, W)] + [grid(ARENA - 9 * W, KT, W)] * 3
        RS = [flat(o_cum, W)] + [flat(ARENA - W, W)] * 3

        o_stage = [carve(4 * PW), carve(4 * PW)]
        STAGE = [grid(o, 4, PW) for o in o_stage]
        SQA, SQB = (grid(o, 4, W) for o in o_stage)
        CONV = grid(carve(4 * W), 4, W)
        RSB = CONV
        LW2, G2 = flat(carve(W), W), flat(carve(W), W)
        WA, GD = flat(carve(W), W), flat(carve(W), W)
        TMPD = flat(carve(W), W)

        spare = [[o_ht, KT * W], [o_ring, 2 * KT * W], [tail, ARENA - tail]]

        def chunk_buf(w=P):
            for s in spare:
                if s[1] >= 4 * P:
                    s[0] += 4 * P
                    s[1] -= 4 * P
                    return grid(s[0] - 4 * P, 4 * P // w, w)
            raise AssertionError("no room")

        LT, TI, QI, XM = ([chunk_buf() for _ in range(4)] for _ in range(4))
        RD, KD, BD, AD = (chunk_buf() for _ in range(4))
        KC, QC, VRC, VGC = (chunk_buf() for _ in range(4))
        KTOK, BTOK, VR, KGT, VG = (wide(chunk_buf()) for _ in range(5))
        MK, RK, RBM, GRK = ([chunk_buf() for _ in range(2)] for _ in range(4))
        SR, SG = chunk_buf(), chunk_buf()
        DT, GTRI = [XM[2], XM[3]], [XM[0], XM[1]]
        X1R, UN, VN = wide(MK[0]), wide(MK[1]), wide(LT[2])
        OR, OG = wide(LT[0]), wide(LT[1])
        OSQ, OSQG, TMPG, TMPS = wide(TI[0]), wide(TI[1]), wide(TI[2]), TI[3]
        TMPK = wide(XM[0])

        H1 = grid(work, DFF // P, W)
        RELU = grid(work + 32 * W, 4, W)
        assert work + (36 + 9) * W <= ARENA

        L1 = grid(work, 21, W)
        o_vall = work + 21 * W
        VALL = A[:, o_vall:o_vall + 4 * 1024].rearrange("p (s v) -> p s v", s=4)
        o_bias = o_vall + 4096
        BIASW = P * TT * (TT + 1) // 2
        BIAS = grid(o_bias, 2, BIASW)
        o_dist = o_bias + 2 * BIASW
        DIST = flat(o_dist, W)
        SCORE = grid(o_dist + W, 3, W)
        o_att = o_dist + 4 * W
        SQ1 = [grid(o_att, 4, W), grid(o_att + 4 * W, 4, W)]
        RS1 = grid(o_att + 8 * W, 4, W)
        RT = grid(o_att, 4, W)
        QS, KS = flat(o_att + 4 * W, W), flat(o_att + 5 * W, W)
        ZB = grid(o_att + 6 * W, 3, W)
        PTS = grid(o_att + 9 * W, 2, W)
        o_on = o_att + 12 * W
        ON = A[:, o_on:o_on + 4096].rearrange("p (s v) -> p s v", s=4)
        assert o_on + 4096 <= ARENA, o_on
        OUTT = grid(work, TT, D)

        at = dict(norm1=0, norm2=16, mu=32, w0=46, a0=50, k_k=54, k_a=58, r_k=62, lnx_w=66,
                  lnx_b=70, conv=74)
        NPC = 122
        GDNN, DQN, DKN, LNW, LNB, MQN, MKN = range(7)

        def pc(name, i):
            return PC[:, at[name] + i:at[name] + i + 1]

        def pc2(i):
            return PC2[:, i:i + 1]

        def bias_off(i):
            return P * i * (i + 1) // 2

        bank_filled, bank_read = sem("bank_filled"), sem("bank_read")
        q_x, q_lora, q_ab, q_z, q_w, q_a, q_g, q_pair = 2, 11, 13, 14, 18, 22, 26, 30
        q_kk, q_gq, q_gk, q_bon, q_cum = 54, 58, 62, 66, 70
        q_out, q_m1, q_m2 = [71, 170], [80, 179], [112, 211]
        q_norm = [10, 79, 120, 178]
        q_k, q_ik, q_v, q_iw, q_mv, q_pr1 = 121, 123, 124, 125, 126, 130
        q_ikm, q_ikv, q_dqn, q_mqn, q_mkn, q_k2n, q_mix = 146, 147, 148, 152, 156, 160, 162
        q_fin = 219

        (dma_par, dma_x, dma_out, consts, squares, rms, h_ready, w2_used, inverse_begun, topk_rounds,
         pads_zero, lora_shifted, lora_act, cum_ready, stage_in, stage_used, conv_out, conv_used,
         kk_ready, sq_grp, rs_grp, rs_used, bonus_in, gate_in, gate_ln, glog_ready,
         gcum_ready, l0_dve, l0_act, mix_ready, h1_ready) = (sem(n) for n in (
             "dma_par dma_x dma_out consts squares rms h_ready w2_used inverse_begun topk_rounds pads_zero "
             "lora_shifted lora_act cum_ready stage_in stage_used conv_out conv_used kk_ready "
             "sq_grp rs_grp rs_used bonus_in gate_in gate_ln glog_ready gcum_ready "
             "l0_dve l0_act mix_ready h1_ready").split())
        w_full = [sem("w_full0"), sem("w_full1")]
        act_step, dve_step, pool_step = sem("act_step"), sem("dve_step"), sem("pool_step")
        (f_grow, f_kt, f_vg, f_vr, f_kk, f_kq, f_lt, f_mk, f_rk, f_rb, f_ktok, f_btok, f_x1, f_ks,
         f_u, f_y, f_or, f_og, f_qs, f_sr, f_sg, f_tr, f_tg) = (sem(n) for n in (
             "f_grow f_kt f_vg f_vr f_kk f_kq f_lt f_mk f_rk f_rb f_ktok f_btok f_x1 f_ks "
             "f_u f_y f_or f_og f_qs f_sr f_sg f_tr f_tg").split())
        (e_diff, e_exp, e_copy, e_gtri, e_dsub, e_dt, e_dmask, e_rk, e_ba, e_s0, r_kt, r_vg, r_vr,
         r_kk, r_kq, r_lt, r_mk, r_rk, r_rb, r_ktok, r_btok, r_x1, r_ks, r_u, r_y, e_var, e_rstd,
         e_on, e_og, r_tr, r_tg, e_state, e_ln) = (sem(n) for n in (
             "e_diff e_exp e_copy e_gtri e_dsub e_dt e_dmask e_rk e_ba e_s0 r_kt r_vg r_vr "
             "r_kk r_kq r_lt r_mk r_rk r_rb r_ktok r_btok r_x1 r_ks r_u r_y e_var e_rstd "
             "e_on e_og r_tr r_tg e_state e_ln").split())
        inv_x, inv_xs, inv_y, inv_t = sem("inv_x"), sem("inv_xs"), sem("inv_y"), sem("inv_t")
        (n_sq, n_rs, n_used, ik_centred, dist_ready, idx_full, idx_relu, idx_acc, idx_masked,
         bias_ready, at_stage, at_qk, at_z, at_mx, at_p, at_t, at_pt, at_o, at_on) = (
             sem(n) for n in (
                 "n_sq n_rs n_used ik_centred dist_ready idx_full idx_relu idx_acc idx_masked "
                 "bias_ready at_stage at_qk at_z at_mx at_p at_t at_pt at_o at_on").split())

        block = ctx.enter_context(nc.Block())
        ev, od = a["ev_w_in"][0], a["od_w_in"][0]

        def kmaj(w):
            return w.rearrange("(k p) n -> p k n", p=P)

        @block.sync
        def _(sp):
            def load(slot, cols, at=0):
                w = cols.shape[-1]
                sp.dma_start(RING[:, slot, :, at:at + w], kmaj(cols)).then_inc(w_full[slot], 16)

            sp.dma_start(XIN, a["x"][0].rearrange("(t p) d -> p t d", p=P)).then_inc(dma_x, 16)
            load(0, ev[:, 1536:RWKV_COLS])
            load(0, ev[:, GDN_BA:GDN_BA + 16], at=256)
            load(1, ev[:, GDN_Z:GDN_Z + 512])
            sp.wait_ge(bank_filled, q_z)
            load(0, ev[:, 0:512])
            sp.wait_ge(bank_filled, q_w)
            load(1, ev[:, GDN_QKV:GDN_QKV + 512])
            with sp.Fori(1, 3) as i:
                sp.wait_ge(bank_filled, i * 8 + (q_pair - 4))
                load(0, ev[:, bass.ds(i * 512, 512)])
                sp.wait_ge(bank_filled, i * 8 + q_pair)
                load(1, ev[:, bass.ds(i * 512 + GDN_QKV, 512)])

            def w_out_and_mlp(l):
                wout = a["ev_w_out" if l == 0 else "od_w_out"][0]
                w1 = a["mlp_w1"][l]
                w2 = a["mlp_w2"][l].rearrange("(r p) n -> p r n", p=P)
                load(0, wout[:, 0:512])
                if l == 1:
                    sp.wait_ge(bank_filled, q_pr1 + 16)
                load(1, wout[:, 512:1024])
                with sp.Fori(0, 4) as i:
                    sp.wait_ge(bank_filled, i * 8 + (q_m1[l] - 4))
                    load(0, w1[:, bass.ds(i * 1024, 512)])
                    sp.wait_ge(bank_filled, i * 8 + q_m1[l])
                    load(1, w1[:, bass.ds(i * 1024 + 512, 512)])
                sp.wait_ge(bank_filled, q_m2[l] - 4)
                sp.dma_start(RING[:, 0], w2[:, 0:8, 0:512]).then_inc(w_full[0], 16)
                sp.wait_ge(bank_filled, q_m2[l])
                sp.dma_start(RING[:, 1], w2[:, 0:8, 512:1024]).then_inc(w_full[1], 16)
                with sp.Fori(1, 4) as i:
                    sp.wait_ge(w2_used, i * 2 + (6 * l - 1))
                    sp.dma_start(RING[:, 0], w2[:, bass.ds(i * 8, 8), 0:512]).then_inc(w_full[0], 16)
                    sp.wait_ge(w2_used, i * 2 + 6 * l)
                    sp.dma_start(RING[:, 1], w2[:, bass.ds(i * 8, 8), 512:1024]).then_inc(w_full[1], 16)

            sp.wait_ge(f_tg, TT)
            w_out_and_mlp(0)
            sp.wait_ge(bank_filled, q_m2[0] + 4)
            for g in range(2):
                for half in range(2):
                    load(0, od[:, OD_K + g * HD:OD_K + (g + 1) * HD], at=(2 * g + half) * HD)
            for half in range(2):
                load(0, od[:, OD_IK:OD_IK + HD], at=256 + half * HD)
            load(0, od[:, OD_V:OD_V + 128], at=384)
            sp.wait_ge(bank_filled, q_m2[0] + 8)
            load(1, od[:, OD_MV:OD_MV + 512])
            with sp.Fori(0, 2) as i:
                sp.wait_ge(bank_filled, i * 8 + (q_pr1 - 4))
                load(0, od[:, bass.ds(i * 768, 512)])
                sp.wait_ge(bank_filled, i * 8 + q_pr1)
                load(1, od[:, bass.ds(i * 512 + OD_MQ, 512)])
            sp.wait_ge(bank_filled, q_pr1 + 12)
            w_out_and_mlp(1)
            for i in range(TT):
                sp.wait_ge(bank_read, q_fin + 2 * i + 2)
                sp.dma_start(out[0, i * P:(i + 1) * P, :], OUTT[:, i, :]).then_inc(dma_out, 16)
            sp.wait_ge(dma_out, 16 * TT)

        @block.tensor
        def _(pe):
            full = [0, 0]

            def arrived(slot, dmas=1):
                full[slot] += 16 * dmas
                pe.wait_ge(w_full[slot], full[slot])

            def take(q, dyn=0):
                if q >= 8:
                    pe.wait_ge(bank_read, dyn + (q - 7))
                return bank[q % 8]

            def group(slot, act, q, dyn=0, ready=None):
                for b in range(4):
                    o = take(q + b, dyn)
                    for k in range(KT):
                        if ready is not None and b == 0:
                            ready(k)
                        mm = pe.matmul(o[:, :], RING[:, slot, k, b * P:(b + 1) * P], act(k),
                                       start=(k == 0), stop=(k == KT - 1))
                    mm.then_inc(bank_filled, 1)

            def norm(n):
                o = take(q_norm[n])
                for k in range(KT):
                    pe.wait_ge(squares, KT * n + k + 1)
                    mm = pe.matmul(o[:, :], ONES, SQ[n][:, k, :], start=(k == 0), stop=(k == KT - 1))
                mm.then_inc(bank_filled, 1)

            def normed(n):
                return lambda k: pe.wait_ge(h_ready, KT * n + k + 1)

            def h(k):
                return HT[:, k, :]

            pe.wait_ge(consts, 1)
            pe.wait_ge(dma_par, 16 * N_PAR)
            pe.transpose(take(0)[:, 0:NPC], PR[0:NPC, :], IDENT[0:NPC, 0:NPC]).then_inc(bank_filled, 1)
            pe.transpose(take(1)[:, 0:7], PR2[0:7, :], IDENT[0:7, 0:7]).then_inc(bank_filled, 1)
            pe.wait_ge(dma_x, 16)
            for k in range(KT):
                o = take(q_x + k)
                for i in range(TT):
                    mm = pe.transpose(o[:, i * P:(i + 1) * P], XIN[:, i, k * P:(k + 1) * P], IDENT)
                mm.then_inc(bank_filled, 1)
            norm(0)

            arrived(0, 2)
            for b in range(2):
                o = take(q_lora + b)
                for k in range(KT):
                    if b == 0:
                        pe.wait_ge(h_ready, k + 1)
                    mm = pe.matmul(o[:, :], RING[:, 0, k, b * P:(b + 1) * P], h(k),
                                   start=(k == 0), stop=(k == KT - 1))
                mm.then_inc(bank_filled, 1)
            o = take(q_ab)
            for i in range(TT):
                for k in range(KT):
                    mm = pe.matmul(o[:, 16 * i:16 * i + 16], HT[:, k, i * P:(i + 1) * P],
                                   RING[:, 0, k, 256:272], start=(k == 0), stop=(k == KT - 1))
            mm.then_inc(bank_filled, 1)
            arrived(1)
            group(1, h, q_z)

            pe.wait_ge(lora_act, 2)
            for c in range(4):
                pe.matmul(take(q_w + c)[:, :], LW2[0:HD, c * P:(c + 1) * P], WA[0:HD, :],
                          start=True, stop=True).then_inc(bank_filled, 1)
            for c in range(4):
                pe.matmul(take(q_a + c)[:, :], LW2[HD:P, c * P:(c + 1) * P], WA[HD:P, :],
                          start=True, stop=True).then_inc(bank_filled, 1)
            for c in range(4):
                pe.matmul(take(q_g + c)[:, :], G2[:, c * P:(c + 1) * P], GD,
                          start=True, stop=True).then_inc(bank_filled, 1)

            with pe.Fori(0, 3) as i:
                pe.wait_ge(w_full[0], i * 16 + (full[0] + 16))
                group(0, h, q_pair, i * 8)
                pe.wait_ge(w_full[1], i * 16 + (full[1] + 16))
                group(1, h, q_pair + 4, i * 8)
            full[0] += 48
            full[1] += 48

            for n, (q, src) in enumerate(((q_kk, SQA), (q_gq, SQB), (q_gk, SQA), (q_bon, SQB))):
                if n < 3:
                    pe.wait_ge(sq_grp, n + 1)
                else:
                    pe.wait_ge(bonus_in, 4)
                for c in range(4):
                    pe.matmul(take(q + c)[:, :], HEADS2, src[:, c, :],
                              start=True, stop=True).then_inc(bank_filled, 1)
            pe.wait_ge(glog_ready, 1)
            o = take(q_cum)
            pe.matmul(o[:, 0:32], INCL, wide(GLOG), start=True, stop=True)
            pe.matmul(o[:, 32:64], ONES, wide(GLOG), start=True, stop=True).then_inc(bank_filled, 1)

            pe.wait_ge(l0_dve, 1)
            pe.wait_ge(l0_act, 1)

            def half(x, p, j):
                return x[p * HD:(p + 1) * HD, j, :]

            def head_products(banks, lhs, rhs, done):
                for j in range(PAIRS):
                    for p in range(2):
                        mm = pe.matmul(bank[banks[p]][:, j * P:(j + 1) * P], half(lhs, p, j),
                                       half(rhs, p, j), start=True, stop=True)
                mm.then_inc(done, 1)

            def turn(b, src, done):
                for j in range(PAIRS):
                    mm = pe.transpose(bank[b][:, j * P:(j + 1) * P], src[:, j, :], IDENT)
                mm.then_inc(done, 1)

            def turn_wide(b, src, done):
                for j in range(PAIRS):
                    mm = pe.transpose(bank[b][:, j * P:(j + 1) * P], src[:, j * P:(j + 1) * P], IDENT)
                mm.then_inc(done, 1)

            def by_state(b, lhs, state, more):
                for j in range(PAIRS):
                    mm = pe.matmul(bank[b][:, j * P:(j + 1) * P], lhs[:, j, :], state[:, j, :],
                                   start=(j == 0), stop=not more, skip_group_check=True)
                return mm

            def by_heads(b, mats, vals, first, last):
                for hh in range(NH):
                    cols = slice(hh * HD, (hh + 1) * HD)
                    mm = pe.matmul(bank[b][:, cols], mats[hh % 2][:, hh // 2, :], vals[:, cols],
                                   start=(first and hh == 0), stop=last, skip_group_check=True)
                return mm

            with pe.Fori(0, TT) as c:
                n = c + 1
                pe.wait_ge(e_gtri, n)
                for p in range(2):
                    mm = pe.matmul(bank[p][:, :], ONES, wide(GTRI[p]), start=True, stop=True)
                mm.then_inc(f_grow, 1)
                pe.wait_ge(e_copy, n)
                turn(2, KC, f_kt)
                turn(3, VGC, f_vg)
                turn(4, VRC, f_vr)
                head_products((5, 6), KC, KC, f_kk)
                pe.wait_ge(r_kt, n)
                head_products((7, 2), KC, QC, f_kq)
                pe.wait_ge(e_ba, n)
                pe.wait_ge(e_rk, n)
                pe.wait_ge(r_vg, n)
                pe.wait_ge(r_vr, n)
                head_products((3, 4), BD, AD, f_lt)
                pe.wait_ge(e_dsub, n)
                head_products((0, 1), KD, AD, f_mk)
                pe.wait_ge(r_kk, n)
                head_products((5, 6), KD, RD, f_rk)
                pe.wait_ge(r_kq, n)
                head_products((7, 2), BD, RD, f_rb)
                pe.wait_ge(r_lt, n)
                turn(3, KD, f_ktok)
                turn(4, BD, f_btok)
                pe.wait_ge(e_s0, n)
                pe.wait_ge(r_mk, n)
                by_state(0, AD, SR, True)
                by_heads(0, MK, VR, False, True).then_inc(f_x1, 1)
                by_state(1, KC, SG, False).then_inc(f_ks, 1)
                pe.wait_ge(r_x1, n)
                pe.wait_ge(r_ks, n)
                pe.wait_ge(r_rb, n)
                pe.wait_ge(r_btok, n)
                pe.sem_inc(inverse_begun, 1)
                with pe.Fori(0, LEVELS) as lev:
                    for g in range(4):
                        pe.wait_ge(inv_t, c * (4 * LEVELS + 4) + (lev * 4 + (g + 1)))
                        for j in range(PAIRS):
                            mm = pe.matmul(bank[2 * g][:, j * P:(j + 1) * P], LT[g][:, j, :],
                                           TI[g][:, j, :], start=True, stop=True)
                        mm.then_inc(inv_x, 1)
                    for g in range(4):
                        pe.wait_ge(inv_xs, c * (4 * LEVELS) + (lev * 4 + (g + 1)))
                        for j in range(PAIRS):
                            pe.matmul(bank[2 * g][:, j * P:(j + 1) * P], QI[g][:, j, :],
                                      XM[g][:, j, :], start=True, stop=True)
                        for j in range(PAIRS):
                            mm = pe.matmul(bank[2 * g + 1][:, j * P:(j + 1) * P], XM[g][:, j, :],
                                           QI[g][:, j, :], start=True, stop=True)
                        mm.then_inc(inv_y, 1)
                pe.wait_ge(inv_t, c * (4 * LEVELS + 4) + (4 * LEVELS + 4))
                by_heads(0, QI[0:2], X1R, True, True).then_inc(f_u, 1)
                by_heads(1, QI[2:4], VG, True, True).then_inc(f_y, 1)
                by_state(4, QC, SG, False).then_inc(f_qs, 1)
                by_state(2, RD, SR, True)
                by_heads(2, RK, VR, False, False)
                pe.wait_ge(r_u, n)
                by_heads(2, RBM, UN, False, True).then_inc(f_or, 1)
                pe.wait_ge(r_y, n)
                by_heads(3, GRK, VN, True, True).then_inc(f_og, 1)
                for j in range(PAIRS):
                    cols = slice(j * P, (j + 1) * P)
                    pe.matmul(bank[5][:, cols], KTOK[:, cols], VR[:, cols], start=(j == 0),
                              stop=False, skip_group_check=True)
                    mm = pe.matmul(bank[5][:, cols], BTOK[:, cols], UN[:, cols], start=False,
                                   stop=True, skip_group_check=True)
                mm.then_inc(f_sr, 1)
                for j in range(PAIRS):
                    cols = slice(j * P, (j + 1) * P)
                    mm = pe.matmul(bank[6][:, cols], KGT[:, cols], VN[:, cols], start=True, stop=True)
                mm.then_inc(f_sg, 1)
                pe.wait_ge(e_on, n)
                turn_wide(7, OR, f_tr)
                pe.wait_ge(e_og, n)
                turn_wide(0, OG, f_tg)
                pe.wait_ge(r_tg, n)
                pe.wait_ge(e_state, n)

            def mlp(l):
                with pe.Fori(0, 4) as i:
                    for s in range(2):
                        pe.wait_ge(w_full[s], i * 16 + (full[s] + 16))
                        group(s, h, q_m1[l] + 4 * s, i * 8)
                full[0] += 64
                full[1] += 64

                def quarter(kq, first, last):
                    for s in range(2):
                        pe.wait_ge(w_full[s], kq * 16 + (full[s] + 16))
                        for b in range(4):
                            if first:
                                o = take(q_m2[l] + 4 * s + b)
                            else:
                                o = bank[(q_m2[l] + 4 * s + b) % 8]
                            for k in range(KT):
                                if s == 0 and b == 0:
                                    pe.wait_ge(h1_ready, kq * 8 + (4 + 32 * l + k + 1))
                                if first or last:
                                    rhs = H1[:, kq * 8 + k, :]
                                else:
                                    rhs = H1[:, bass.ds(kq * 8 + k, 1), :].rearrange("p a w -> p (a w)")
                                mm = pe.matmul(o[:, :], RING[:, s, k, b * P:(b + 1) * P], rhs,
                                               start=(first and k == 0), stop=(last and k == KT - 1),
                                               skip_group_check=True)
                            if last:
                                mm.then_inc(bank_filled, 1)
                        if not last:
                            mm.then_inc(w2_used, 1)

                quarter(0, True, False)
                with pe.Fori(1, 3) as kq:
                    quarter(kq, False, False)
                quarter(3, False, True)
                full[0] += 64
                full[1] += 64

            def projected(l, act):
                for s in range(2):
                    arrived(s)
                    group(s, act, q_out[l] + 4 * s)
                norm(2 * l + 1)
                for k in range(KT):
                    pe.wait_ge(h_ready, KT * (2 * l + 1) + k + 1)
                mlp(l)

            pe.wait_ge(mix_ready, 2)
            projected(0, lambda k: R[:, k, :] if k < 4 else GQ[:, k - 4, :])

            norm(2)
            arrived(0, 7)
            for b in range(3):
                o = take(q_k + b)
                for k in range(KT):
                    if b == 0:
                        pe.wait_ge(h_ready, KT * 2 + k + 1)
                    mm = pe.matmul(o[:, :], RING[:, 0, k, b * P:(b + 1) * P], h(k),
                                   start=(k == 0), stop=(k == KT - 1))
                mm.then_inc(bank_filled, 1)
            o = take(q_v)
            for i in range(TT):
                for k in range(KT):
                    mm = pe.matmul(o[:, i * P:(i + 1) * P], HT[:, k, i * P:(i + 1) * P],
                                   RING[:, 0, k, 384:512], start=(k == 0), stop=(k == KT - 1))
            mm.then_inc(bank_filled, 1)
            o = take(q_iw)
            for i in range(TT):
                for k in range(KT):
                    mm = pe.matmul(o[:, NH * i:NH * i + NH], HT[:, k, i * P:(i + 1) * P],
                                   IWW[:, k, :], start=(k == 0), stop=(k == KT - 1))
            mm.then_inc(bank_filled, 1)
            arrived(1)
            for i in range(TT):
                o = take(q_mv + i)
                for k in range(KT):
                    mm = pe.matmul(o[:, :], HT[:, k, i * P:(i + 1) * P], RING[:, 1, k, :],
                                   start=(k == 0), stop=(k == KT - 1))
                mm.then_inc(bank_filled, 1)
            with pe.Fori(0, 2) as i:
                for s in range(2):
                    pe.wait_ge(w_full[s], i * 16 + (full[s] + 16))
                    group(s, h, q_pr1 + 4 * s, i * 8)
            full[0] += 32
            full[1] += 32
            pe.matmul(take(q_ikm)[:, :], HEADS2, L1[:, 20, :], start=True, stop=True).then_inc(bank_filled, 1)
            pe.wait_ge(n_sq, 1)
            pe.matmul(take(q_ikv)[:, :], HEADS2, SQ1[0][:, 0, :], start=True, stop=True).then_inc(bank_filled, 1)
            for n, (q, tiles) in enumerate(((q_dqn, 4), (q_mqn, 4), (q_mkn, 4), (q_k2n, 2))):
                pe.wait_ge(n_sq, n + 2)
                for t in range(tiles):
                    pe.matmul(take(q + t)[:, :], HEADS2, SQ1[(n + 1) % 2][:, t, :],
                              start=True, stop=True).then_inc(bank_filled, 1)

            pe.wait_ge(n_used, 5)
            pe.wait_ge(bank_read, q_mix)
            u = 0
            for i in range(1, TT):
                for hh in range(NH):
                    p, j = hh % 2, hh // 2
                    pe.wait_ge(idx_relu, u + 1)
                    pe.matmul(bank[u % 4][:, 0:P * (i + 1)],
                              L1[p * HD:(p + 1) * HD, 16 + j, i * P:(i + 1) * P],
                              L1[p * HD:(p + 1) * HD, 20, 0:P * (i + 1)],
                              start=True, stop=True).then_inc(idx_full, 1)
                    u += 1
            pe.wait_ge(idx_relu, 4 + u)

            with pe.Fori(0, 2) as ty:
                with pe.Fori(0, PAIRS) as j:
                    pair8 = ty * 32 + j * 8
                    pe.wait_ge(at_stage, ty * 4 + j + 1)

                    def scores(u):
                        i, p = u // 2, u % 2
                        pe.wait_ge(at_z, pair8 + (u + 1))
                        pe.matmul(bank[u % 4][:, 0:P * (i + 1)],
                                  QS[p * HD:(p + 1) * HD, i * P:(i + 1) * P],
                                  KS[p * HD:(p + 1) * HD, 0:P * (i + 1)],
                                  start=True, stop=True).then_inc(at_qk, 1)

                    def turned(u):
                        i = u // 2
                        pe.wait_ge(at_p, pair8 + (u + 1))
                        pe.wait_ge(at_pt, pair8 + (u + 1))
                        for s in range(i + 1):
                            mm = pe.transpose(bank[4 + u % 2][:, s * P:(s + 1) * P],
                                              ZB[:, ZSLOT[u], s * P:(s + 1) * P], IDENT)
                        mm.then_inc(at_t, 1)

                    def values(u):
                        i, p = u // 2, u % 2
                        if u == 0:
                            pe.wait_ge(at_on, ty * 4 + j + 1)
                        pe.wait_ge(at_pt, pair8 + (u + 3))
                        for s in range(i + 1):
                            v = VALL[:, s, bass.ds(ty * 512 + j * 128 + p * HD, HD)]
                            mm = pe.matmul(bank[6][:, u * HD:(u + 1) * HD],
                                           PTS[:, u % 2, s * P:(s + 1) * P], v,
                                           start=(s == 0), stop=(s == i))
                        mm.then_inc(at_o, 1)

                    for u in range(4):
                        scores(u)
                    for u in range(8):
                        turned(u)
                        if u + 4 < 8:
                            scores(u + 4)
                        if u >= 1:
                            values(u - 1)
                    values(7)
            pe.wait_ge(at_on, 9)
            for k in range(KT):
                o = bank[(q_mix + k) % 8]
                for i in range(TT):
                    mm = pe.transpose(o[:, i * P:(i + 1) * P], ON[:, i, k * P:(k + 1) * P], IDENT)
                mm.then_inc(bank_filled, 1)
            pe.wait_ge(bank_read, q_mix + 8)
            projected(1, h)
            pe.wait_ge(bank_read, q_m2[1] + 8)
            for i in range(TT):
                for half_ in range(2):
                    o = take(q_fin + 2 * i + half_)
                    for b in range(4):
                        mm = pe.transpose(o[:, b * P:(b + 1) * P],
                                          XT[:, half_ * 4 + b, i * P:(i + 1) * P], IDENT)
                    mm.then_inc(bank_filled, 1)

        @block.scalar
        def _(act):
            t = Tally(act, act_step)

            def filled(q, dyn=0):
                act.wait_ge(bank_filled, dyn + (q + 1))

            def src(q):
                return bank[q % 8]

            def rows(dst, vec):
                act.dma_start(dst, vec).then_inc(dma_par, 16)

            rows(PR[0:16, :], a["norm1_g"].rearrange("l (c p) -> (l c) p", p=P))
            rows(PR[16:32, :], a["norm2_g"].rearrange("l (c p) -> (l c) p", p=P))
            r = 32
            for name in ("rwkv_mu", "rwkv_w0", "rwkv_a0", "rwkv_k_k", "rwkv_k_a", "rwkv_r_k",
                         "rwkv_lnx_w", "rwkv_lnx_b"):
                v = a[name]
                v = v.rearrange("o (c a) n -> (o c) (a n)", a=2) if name == "rwkv_r_k" else \
                    v.rearrange("o (c p) -> (o c) p", p=P)
                rows(PR[r:r + v.shape[0], :], v)
                r += v.shape[0]
            rows(PR[74:122, :], a["gdn_conv_w"][0].rearrange("j (b p) -> (j b) p", p=P))
            for i, name in enumerate(PAR64):
                for half in range(2):
                    rows(PR2[i:i + 1, half * HD:(half + 1) * HD], a[name])
            rows(ALOG, a["gdn_a_log"].broadcast_to([P, NH]))
            rows(DTB, a["gdn_dt_bias"].broadcast_to([P, NH]))
            rows(LW2[0:HD, :], a["rwkv_w2"][0])
            rows(LW2[HD:P, :], a["rwkv_a2"][0])
            rows(G2, a["rwkv_g2"][0])
            rows(IWW, kmaj(od[:, OD_IW:OD_IW + NH]))

            def norm(n, ready):
                for k in range(KT):
                    act.wait_ge(bank_read, ready + k + 1)
                    act.activation(SQ[n][:, k, :], XT[:, k, :], ACT.Square).then_inc(squares, 1)
                filled(q_norm[n])
                act.activation(RS[n], src(q_norm[n])[:, :], ACT.Ln, bias=RMS_EPS, scale=1.0 / D)\
                   .then_inc(bank_read, 1)
                act.wait_ge(bank_read, q_norm[n] + 1)
                act.activation(RS[n], RS[n], ACT.Exp, scale=-0.5).then_inc(rms, 1)

            norm(0, q_x)

            act.wait_ge(pads_zero, 1)
            for b in range(2):
                filled(q_lora + b)
                act.activation(STAGE[0][:, b, 3:3 + W], src(q_lora + b)[:, :], ACT.Copy)\
                   .then_inc(bank_read, 1)
            filled(q_ab)
            act.activation(wide(AB), src(q_ab)[:, 0:64], ACT.Copy).then_inc(bank_read, 1)
            for b in range(4):
                filled(q_z + b)
                act.activation(Z[:, b, :], src(q_z + b)[:, :], ACT.Silu).then_inc(bank_read, 1)
            act.wait_ge(lora_shifted, 2)
            act.activation(WA[0:HD, :], WA[0:HD, :], ACT.Tanh).then_inc(lora_act, 1)
            act.activation(GD, GD, ACT.Sigmoid).then_inc(lora_act, 1)
            act.wait_ge(bank_read, q_ab + 1)
            act.activation(BETA, AB[:, :, 0:NH], ACT.Sigmoid)
            for c in range(4):
                filled(q_w + c)
                act.activation(BON[:, c, :], src(q_w + c)[:, :], ACT.Sigmoid, bias=pc("w0", c))\
                   .then_inc(bank_read, 1)
            for c in range(4):
                filled(q_a + c)
                act.activation(B[:, c, :], src(q_a + c)[:, :], ACT.Sigmoid, bias=pc("a0", c))\
                   .then_inc(bank_read, 1)
            for c in range(4):
                filled(q_g + c)
                act.activation(G[:, c, :], src(q_g + c)[:, :], ACT.Copy).then_inc(bank_read, 1)

            with act.Fori(0, 3) as i:
                for s in range(2):
                    for b in range(4):
                        filled(q_pair + 4 * s + b, i * 8)
                        if s == 0:
                            act.wait_ge(stage_used, i * 4 + (b + 1))
                        act.activation(STAGE[s][:, b, 3:3 + W], src(q_pair + 4 * s + b)[:, :],
                                       ACT.Copy).then_inc(bank_read, 1)
                for b in range(4):
                    act.wait_ge(conv_out, i * 4 + (b + 1))
                    act.activation(GQKV[:, bass.ds(i * 4 + b, 1), :].rearrange("p a w -> p (a w)"),
                                   CONV[:, b, :], ACT.Silu).then_inc(conv_used, 1)

            act.wait_ge(gate_in, 1)
            t.link(act.activation(wide(GLOG), wide(GTMP), ACT.Abs))
            t.link(act.activation(wide(GLOG), wide(GLOG), ACT.Exp, scale=-1.0))
            act.activation(NEA, ALOG, ACT.Exp)
            act.activation(wide(GLOG), wide(GLOG), ACT.Ln, bias=1.0).then_inc(gate_ln, 1)
            act.wait_ge(conv_used, 4 + 12)
            act.wait_ge(stage_used, 4 + 12)
            for n, (q, x, sq) in enumerate(((q_kk, KK, SQA), (q_gq, GQ, SQB), (q_gk, GK, SQA))):
                if n == 0:
                    act.wait_ge(kk_ready, 4)
                if n == 2:
                    act.wait_ge(bank_filled, q_kk + 4)
                act.activation(wide(sq), wide(x), ACT.Square).then_inc(sq_grp, 1)
                if n > 0:
                    act.wait_ge(rs_used, n)
                for c in range(4):
                    filled(q + c)
                    act.activation(RSB[:, c, :], src(q + c)[:, :], ACT.Ln, bias=1e-6)\
                       .then_inc(bank_read, 1)
                act.wait_ge(bank_read, q + 4)
                act.activation(wide(RSB), wide(RSB), ACT.Exp, scale=-0.5).then_inc(rs_grp, 1)
            act.wait_ge(gcum_ready, 1)
            act.activation(wide(EG), wide(GCUM), ACT.Exp)
            act.activation(wide(EREST), wide(EREST), ACT.Exp)
            for p in range(2):
                part = slice(p * HD, (p + 1) * HD)
                last = act.activation(
                    ESTATE[part, :, :],
                    src(q_cum)[part, 32:64].rearrange("p (c j q) -> p c j q", c=TT, q=2)[:, :, :, p],
                    ACT.Exp)
            last.then_inc(l0_act, 1)

            act.wait_ge(l0_dve, 1)
            with act.Fori(0, TT) as c:
                n = c + 1
                act.wait_ge(f_vg, n)
                act.activation(VG, bank[3][:, :], ACT.Copy).then_inc(r_vg, 1)
                act.wait_ge(f_vr, n)
                act.activation(VR, bank[4][:, :], ACT.Copy).then_inc(r_vr, 1)
                act.wait_ge(e_diff, n)
                act.activation(wide(KD), wide(RD), ACT.Exp, scale=-1.0)
                with t.loop(c, 1, TT):
                    t.link(act.activation(wide(BD), wide(RD), ACT.Exp, scale=-1.0))
                act.activation(wide(RD), wide(RD), ACT.Exp)
                act.activation(wide(AD), wide(AD), ACT.Exp)
                act.activation(ESM, SM, ACT.Exp).then_inc(e_exp, 1)
                act.wait_ge(e_dsub, n)
                for p in range(2):
                    last = act.activation(wide(DT[p]), wide(DT[p]), ACT.Exp)
                last.then_inc(e_dt, 1)
                act.wait_ge(f_lt, n)
                for p in range(2):
                    last = act.activation(wide(LT[p]), bank[3 + p][:, :], ACT.Copy)
                last.then_inc(r_lt, 1)
                act.wait_ge(f_ktok, n)
                act.activation(KTOK, bank[3][:, :], ACT.Copy).then_inc(r_ktok, 1)
                act.wait_ge(f_btok, n)
                act.activation(BTOK, bank[4][:, :], ACT.Copy).then_inc(r_btok, 1)
                act.wait_ge(f_x1, n)
                act.activation(X1R, bank[0][:, :], ACT.Copy).then_inc(r_x1, 1)
                act.wait_ge(f_u, n)
                act.activation(UN, bank[0][:, :], ACT.Copy, scale=-1.0).then_inc(r_u, 1)
                for g, eps in ((0, GN_EPS), (1, RMS_EPS)):
                    cols = slice(g * NH, (g + 1) * NH)
                    act.wait_ge(e_var, 2 * c + (g + 1))
                    act.activation(RSTD[:, cols], VAR[:, cols], ACT.Ln, bias=eps, scale=1.0 / HD)\
                       .then_inc(e_ln, 1)
                    act.wait_ge(e_ln, 2 * c + (g + 1))
                    act.activation(RSTD[:, cols], RSTD[:, cols], ACT.Exp, scale=-0.5)\
                       .then_inc(e_rstd, 1)
                here = bass.ds(c * P, P)
                act.wait_ge(f_tr, n)
                act.activation(R[:, :, here], bank[7][:, :].rearrange("p (j t) -> p j t", j=4),
                               ACT.Copy).then_inc(r_tr, 1)
                act.wait_ge(f_tg, n)
                act.activation(GQ[:, :, here], bank[0][:, :].rearrange("p (j t) -> p j t", j=4),
                               ACT.Copy).then_inc(r_tg, 1)

            def mlp(l):
                with act.Fori(0, 4) as i:
                    for b in range(8):
                        filled(q_m1[l] + b, i * 8)
                        act.wait_ge(h1_ready, i * 8 + (32 * l + b + 1))
                        act.activation(RELU[:, b % 4, :], src(q_m1[l] + b)[:, :], ACT.Relu)\
                           .then_inc(bank_read, 1)

            norm(1, q_out[0])
            mlp(0)
            norm(2, q_m2[0])

            for q, tile in ((q_k, 8), (q_k + 1, 10), (q_ik, 20)):
                filled(q)
                act.activation(L1[:, tile, :], src(q)[:, :], ACT.Copy).then_inc(bank_read, 1)
            filled(q_v)
            for g in range(2):
                vin = src(q_v)[:, :].rearrange("p (s v) -> p s v", s=4)[:, :, g * HD:(g + 1) * HD]
                for rep in range(4):
                    cc = (4 * g + rep) * HD
                    last = act.activation(VALL[:, :, cc:cc + HD], vin, ACT.Copy)
            last.then_inc(bank_read, 1)
            filled(q_iw)
            act.activation(wide(IW), src(q_iw)[:, 0:TT * NH], ACT.Copy, scale=float(NH) ** -0.5)\
               .then_inc(bank_read, 1)
            for i in range(TT):
                filled(q_mv + i)
                act.activation(VALL[:, i, 512:1024], src(q_mv + i)[:, :], ACT.Copy).then_inc(bank_read, 1)
            with act.Fori(0, 2) as i:
                for s in range(2):
                    for b in range(4):
                        q = q_pr1 + 4 * s + b
                        filled(q, i * 8)
                        dst = L1[:, bass.ds(i * (16 if s == 0 else 8) + 4 * s + b, 1), :]
                        act.activation(dst.rearrange("p a w -> p (a w)"), src(q)[:, :], ACT.Copy)\
                           .then_inc(bank_read, 1)
            act.wait_ge(ik_centred, 1)
            act.activation(SQ1[0][:, 0, :], L1[:, 20, :], ACT.Square).then_inc(n_sq, 1)
            act.wait_ge(bank_read, q_pr1 + 16)
            for n, (q, tiles, x) in enumerate(((q_ikv, 1, None), (q_dqn, 4, L1[:, 0:4, :]),
                                               (q_mqn, 4, L1[:, 4:8, :]), (q_mkn, 4, L1[:, 12:16, :]),
                                               (q_k2n, 2, L1[:, 8:12:2, :]))):
                if n > 0:
                    if n >= 2:
                        act.wait_ge(bank_filled, q_prev)
                    sq = SQ1[n % 2][:, 0:tiles, :]
                    act.activation(sq, x, ACT.Square).then_inc(n_sq, 1)
                    act.wait_ge(n_used, n)
                q_prev = q
                for c in range(tiles):
                    filled(q + c)
                    act.activation(RS1[:, c, :], src(q + c)[:, :], ACT.Ln, bias=RMS_EPS,
                                   scale=1.0 / HD).then_inc(bank_read, 1)
                act.wait_ge(bank_read, q + tiles)
                act.activation(RS1[:, 0:tiles, :], RS1[:, 0:tiles, :], ACT.Exp, scale=-0.5)\
                   .then_inc(n_rs, 1)

            act.wait_ge(n_used, 5)
            act.sem_inc(idx_relu, 4)
            u = 0
            for i in range(1, TT):
                for hh in range(NH):
                    act.wait_ge(idx_full, u + 1)
                    if u >= 4:
                        act.wait_ge(idx_acc, u - 3)
                    act.activation(RT[:, u % 4, 0:P * (i + 1)], bank[u % 4][:, 0:P * (i + 1)],
                                   ACT.Relu, scale=float(HD) ** -0.5).then_inc(idx_relu, 1)
                    u += 1

            act.wait_ge(idx_acc, u)
            act.sem_inc(at_pt, 2)
            with act.Fori(0, 2) as ty:
                with act.Fori(0, PAIRS) as j:
                    pair8 = ty * 32 + j * 8

                    def probs(u):
                        wdt = P * (u // 2 + 1)
                        act.wait_ge(at_mx, pair8 + (u + 1))
                        if u == 0:
                            act.wait_ge(at_on, ty * 4 + j + 1)
                        act.activation(ZB[:, ZSLOT[u], 0:wdt], ZB[:, ZSLOT[u], 0:wdt], ACT.Exp,
                                       bias=NMX[:, u:u + 1], accum_out=RSUM[:, u:u + 1])\
                           .then_inc(at_p, 1)

                    def out_turned(u):
                        wdt = P * (u // 2 + 1)
                        act.wait_ge(at_t, pair8 + (u + 1))
                        if u >= 2:
                            act.wait_ge(at_o, pair8 + (u - 1))
                        act.activation(PTS[:, u % 2, 0:wdt], bank[4 + u % 2][:, 0:wdt], ACT.Copy)\
                           .then_inc(at_pt, 1)

                    for u in range(8):
                        probs(u)
                        if u >= 1:
                            out_turned(u - 1)
                    out_turned(7)
            norm(3, q_out[1])
            mlp(1)
            for i in range(2 * TT):
                filled(q_fin + i)
                act.activation(OUTT[:, i // 2, (i % 2) * 512:(i % 2 + 1) * 512],
                               src(q_fin + i)[:, :], ACT.Copy).then_inc(bank_read, 1)

        @block.vector
        def _(dve):
            t = Tally(dve, dve_step)
            mul, add, sub = ALU.mult, ALU.add, ALU.subtract

            def filled(q, dyn=0):
                dve.wait_ge(bank_filled, dyn + (q + 1))

            def src(q):
                return bank[q % 8]

            dve.sem_inc(stage_used, 4)
            dve.sem_inc(h1_ready, 4)
            filled(0)
            dve.tensor_copy(PC[:, 0:NPC], bank[0][:, 0:NPC]).then_inc(bank_read, 1)
            filled(1)
            dve.tensor_copy(PC2[:, 0:7], bank[1][:, 0:7]).then_inc(bank_read, 1)
            dve.wait_ge(bank_read, 2)
            dve.tensor_scalar(OMKA, PC[:, at["k_a"]:at["k_a"] + 4], -1.0, 1.0, mul, add)
            for i, col in enumerate((DQN, MQN)):
                dve.tensor_scalar(QW[:, i:i + 1], pc2(col), float(HD) ** -0.5, None, mul)
            for k in range(KT):
                filled(q_x + k)
                dve.tensor_copy(XT[:, k, :], src(q_x + k)[:, :]).then_inc(bank_read, 1)

            def norm(n):
                dve.wait_ge(rms, n + 1)
                for k in range(KT):
                    g = pc("norm1" if n % 2 == 0 else "norm2", (n // 2) * KT + k)
                    dve.scalar_tensor_tensor(out=HT[:, k, :], in0=XT[:, k, :], scalar=g, in1=RS[n],
                                             op0=mul, op1=mul).then_inc(h_ready, 1)

            norm(0)

            def shifted(dst, stage, mu):
                t.link(dve.tensor_tensor(TMPD, stage[:, 2:2 + W], stage[:, 3:3 + W], sub))
                return dve.scalar_tensor_tensor(out=dst, in0=TMPD, scalar=mu, in1=stage[:, 3:3 + W],
                                                op0=mul, op1=add)

            for b, dst in enumerate((WA, GD)):
                dve.wait_ge(bank_read, q_lora + b + 1)
                shifted(dst, STAGE[0][:, b, :], pc("mu", 12 + b)).then_inc(lora_shifted, 1)
                dve.wait_ge(lora_shifted, b + 1)
            dve.sem_inc(conv_used, 4)
            dve.wait_ge(bank_read, q_ab + 1)
            dve.tensor_tensor(GTMP, AB[:, :, NH:2 * NH], DTB.unsqueeze(1).broadcast_to([P, TT, NH]),
                              add).then_inc(gate_in, 1)
            t.link(dve.memset(CUM[:, :, :, 0:1].rearrange("p c k o -> p (c k) o"), 0.0))
            for c in range(4):
                dve.wait_ge(bank_read, q_w + c + 1)
                t.link(dve.tensor_scalar(CUM[:, c, :, 1:CW],
                                         BON[:, c, :].rearrange("p (k t) -> p k t", k=4),
                                         -float(np.exp(-0.5)), None, mul))
                cum = CUM[:, c, :, :].rearrange("p k t -> p (k t)")
                t.link(dve.tensor_tensor_scan(cum, SCANM, cum, 0.0, mul, add))

            with dve.Fori(0, 3) as i:
                with t.loop(i, 4 + 12, 3):
                    for b in range(4):
                        dve.wait_ge(bank_read, i * 8 + (q_pair + b + 1))
                        mu = PC[:, bass.ds(i * 4 + (at["mu"] + b), 1)]
                        dst = RKV[:, bass.ds(i * 4 + b, 1), :].rearrange("p a w -> p (a w)")
                        shifted(dst, STAGE[0][:, b, :], mu).then_inc(stage_used, 1)
                        dve.wait_ge(stage_used, i * 4 + (4 + b + 1))
                    for b in range(4):
                        dve.wait_ge(bank_read, i * 8 + (q_pair + 4 + b + 1))
                        dve.wait_ge(conv_used, i * 4 + (b + 1))
                        for tap in range(4):
                            wgt = PC[:, bass.ds(i * 4 + (at["conv"] + 12 * tap + b), 1)]
                            x = STAGE[1][:, b, tap:tap + W]
                            if tap == 0:
                                ins = dve.tensor_scalar(CONV[:, b, :], x, wgt, None, mul)
                            else:
                                ins = dve.scalar_tensor_tensor(out=CONV[:, b, :], in0=x, scalar=wgt,
                                                               in1=CONV[:, b, :], op0=mul, op1=add)
                            if tap < 3:
                                t.link(ins)
                            else:
                                ins.then_inc(conv_out, 1)
                        dve.wait_ge(conv_out, i * 4 + (b + 1))
            for c in range(4):
                dve.tensor_scalar(KK[:, c, :], K[:, c, :], pc("k_k", c), None, mul).then_inc(kk_ready, 1)
            dve.wait_ge(kk_ready, 4)
            for c in range(4):
                t.link(dve.tensor_scalar(TMPD, B[:, c, :], pc("k_a", c), OMKA[:, c:c + 1], mul, add))
                t.link(dve.tensor_tensor(K[:, c, :], K[:, c, :], TMPD, mul))
            dve.wait_ge(gate_ln, 1)
            t.link(dve.scalar_tensor_tensor(out=wide(GTMP), in0=wide(GTMP), scalar=0.0, in1=wide(GLOG),
                                            op0=ALU.max, op1=add))
            dve.scalar_tensor_tensor(out=GLOG, in0=GTMP, scalar=-1.0,
                                     in1=NEA.unsqueeze(1).broadcast_to([P, TT, NH]),
                                     op0=mul, op1=mul).then_inc(glog_ready, 1)
            dve.wait_ge(rs_grp, 1)
            dve.tensor_tensor(wide(KK), wide(KK), wide(RSB), mul).then_inc(rs_used, 1)
            dve.wait_ge(rs_used, 1)
            t.link(dve.tensor_tensor(wide(B), wide(KK), wide(B), mul))
            dve.wait_ge(rs_grp, 2)
            dve.scalar_tensor_tensor(out=wide(GQ), in0=wide(GQ), scalar=float(HD) ** -0.5,
                                     in1=wide(RSB), op0=mul, op1=mul).then_inc(rs_used, 1)
            dve.wait_ge(bank_filled, q_gq + 4)
            for c in range(4):
                dve.scalar_tensor_tensor(out=SQB[:, c, :], in0=R[:, c, :], scalar=pc("r_k", c),
                                         in1=K[:, c, :], op0=mul, op1=mul).then_inc(bonus_in, 1)
            dve.wait_ge(rs_grp, 3)
            dve.tensor_tensor(wide(GK), wide(GK), wide(RSB), mul).then_inc(rs_used, 1)
            for c in range(4):
                filled(q_bon + c)
                dve.tensor_tensor(BON[:, c, :], src(q_bon + c)[:, :], V[:, c, :], mul)\
                   .then_inc(bank_read, 1)
            filled(q_cum)
            t.link(dve.tensor_copy(wide(GCUM), src(q_cum)[:, 0:32]))
            dve.tensor_tensor(wide(EREST), src(q_cum)[:, 32:64], wide(GCUM), sub).then_inc(gcum_ready, 1)
            dve.wait_ge(l0_act, 1)
            dve.wait_ge(gcum_ready, 1)
            dve.wait_ge(rs_used, 3)
            dve.tensor_copy(VAR[:, 0:1], PC[:, 0:1]).then_inc(l0_dve, 1)
            dve.sem_inc(bank_read, 1)

            def bc(x, n=P):
                return x.unsqueeze(2).broadcast_to([P, x.shape[1], n])

            def by_parity(x, p):
                return x.rearrange("p o (j q) -> p (o j) q", q=2)[:, :, p]

            def bank4(b):
                return bank[b][:, :].rearrange("p (j t) -> p j t", j=4)

            def heads(x):
                return x.rearrange("p (h d) -> p h d", h=NH)

            def mask4(m):
                return m.unsqueeze(1).broadcast_to([P, 4, P])

            dve.wait_ge(l0_dve, 1)
            with dve.Fori(0, TT) as c:
                n = c + 1
                here = bass.ds(c * P, P)
                row = bass.ds(c, 1)

                def row_of(x):
                    return x[:, row, :].rearrange("p a h -> p (a h)")

                with t.loop(c, DVE_CHUNK, TT):
                    mid = CUM[:, :, row, P // 2:P // 2 + 1].rearrange("p c k o -> p c (k o)")
                    chunk_cum = CUM[:, :, row, :].rearrange("p c k t -> p c (k t)")
                    midb = mid.broadcast_to([P, 4, P])
                    t.link(dve.tensor_tensor(RD, chunk_cum[:, :, 1:CW], midb, sub))
                    dve.tensor_tensor(AD, chunk_cum[:, :, 0:P], midb, sub)
                    dve.tensor_copy(SM[:, 0:4].unsqueeze(2), mid)
                    dve.tensor_copy(SM[:, 4:8].unsqueeze(2), RD[:, :, P - 1:P]).then_inc(e_diff, 1)
                    dve.wait_ge(f_grow, n)
                    for p in range(2):
                        gs = by_parity(GCUM[:, row, :], p)
                        t.step(dve.tensor_tensor(DT[p], bank4(p), bc(gs), sub))
                    t.settle()
                    for p in range(2):
                        ins = dve.tensor_scalar(wide(DT[p]), wide(DT[p]), 0.0, None, ALU.min)
                    ins.then_inc(e_dsub, 1)
                    dve.wait_ge(f_kt, n)
                    dve.tensor_tensor(heads(KGT), heads(bank[2][:, :]), bc(row_of(EREST), HD), mul)\
                       .then_inc(r_kt, 1)
                    dve.wait_ge(e_exp, n)
                    dve.tensor_tensor(RD, RD, R[:, :, here], mul)
                    dve.tensor_tensor(KD, KD, K[:, :, here], mul).then_inc(e_rk, 1)
                    dve.tensor_tensor(SR, SR, bc(ESM[:, 0:4]), mul).then_inc(e_s0, 1)
                    dve.wait_ge(e_dmask, n)
                    dve.wait_ge(f_kk, n)
                    for p in range(2):
                        ins = dve.tensor_tensor(LT[2 + p], bank4(5 + p), LT[2 + p], mul)
                    ins.then_inc(r_kk, 1)
                    dve.wait_ge(f_kq, n)
                    for p in range(2):
                        ins = dve.tensor_tensor(GRK[p], bank4((7, 2)[p]), GRK[p], mul)
                    ins.then_inc(r_kq, 1)
                    for f, dst, banks, m, r_ in ((f_mk, MK, (0, 1), STRICT, r_mk),
                                                 (f_rk, RK, (5, 6), INCL, r_rk),
                                                 (f_rb, RBM, (7, 2), INCL, r_rb)):
                        dve.wait_ge(f, n)
                        for p in range(2):
                            ins = dve.tensor_tensor(dst[p], bank4(banks[p]), mask4(m), mul)
                        ins.then_inc(r_, 1)
                    dve.wait_ge(f_ks, n)
                    dve.wait_ge(r_vg, n)
                    t.link(dve.tensor_tensor(heads(TMPK), heads(bank[1][:, :]), bc(row_of(EG), HD), mul))
                    dve.tensor_tensor(VG, VG, TMPK, sub).then_inc(r_ks, 1)
                    with dve.Fori(0, LEVELS) as lev:
                        for g in range(4):
                            dve.wait_ge(inv_x, c * (4 * LEVELS) + (lev * 4 + (g + 1)))
                            m = MERGE[:, bass.ds(lev, 1), :].broadcast_to([P, 4, P])
                            dve.tensor_tensor(XM[g], bank4(2 * g), m, mul).then_inc(inv_xs, 1)
                        for g in range(4):
                            dve.wait_ge(inv_y, c * (4 * LEVELS) + (lev * 4 + (g + 1)))
                            dve.tensor_tensor(TI[g], TI[g], bank4(2 * g), sub)
                            dve.tensor_tensor(QI[g], QI[g], bank4(2 * g + 1), sub).then_inc(inv_t, 1)
                    dve.wait_ge(inv_t, c * (4 * LEVELS + 4) + (4 * LEVELS + 4))
                    dve.wait_ge(f_y, n)
                    dve.tensor_tensor(heads(VN), heads(bank[1][:, :]), bc(row_of(BETA), HD), mul)\
                       .then_inc(r_y, 1)
                    dve.wait_ge(f_or, n)
                    o_r = heads(bank[2][:, :])
                    t.link(dve.tensor_reduce(NMEAN, o_r, AX.X, add, negate=True))
                    t.link(dve.tensor_scalar(NMEAN, NMEAN, 1.0 / HD, None, mul))
                    t.link(dve.tensor_tensor(heads(OR), o_r, bc(NMEAN, HD), add))
                    t.link(dve.tensor_tensor(OSQ, OR, OR, mul))
                    dve.tensor_reduce(VAR[:, 0:NH], heads(OSQ), AX.X, add).then_inc(e_var, 1)
                    dve.wait_ge(f_og, n)
                    dve.wait_ge(f_qs, n)
                    t.link(dve.tensor_tensor(heads(TMPG), heads(bank[4][:, :]), bc(row_of(EG), HD), mul))
                    t.link(dve.tensor_tensor(OG, TMPG, bank[3][:, :], add))
                    t.link(dve.tensor_tensor(OSQG, OG, OG, mul))
                    dve.tensor_reduce(VAR[:, NH:2 * NH], heads(OSQG), AX.X, add).then_inc(e_var, 1)
                    dve.wait_ge(e_rstd, 2 * c + 1)
                    dve.tensor_tensor(heads(OR), heads(OR), bc(RSTD[:, 0:NH], HD), mul).then_inc(e_on, 1)
                    dve.wait_ge(e_rstd, 2 * c + 2)
                    dve.tensor_tensor(heads(OG), heads(OG), bc(RSTD[:, NH:2 * NH], HD), mul).then_inc(e_og, 1)
                    dve.wait_ge(f_sr, n)
                    t.link(dve.tensor_tensor(TMPS, bank4(5), mask4(HEADS2), mul))
                    t.link(dve.tensor_tensor(SR, SR, TMPS, add))
                    t.link(dve.tensor_tensor(SR, SR, bc(ESM[:, 4:8]), mul))
                    dve.wait_ge(f_sg, n)
                    t.link(dve.tensor_tensor(TMPS, bank4(6), mask4(HEADS2), mul))
                    t.link(dve.tensor_tensor(SG, SG, bc(row_of(ESTATE)), mul))
                    dve.tensor_tensor(SG, SG, TMPS, add).then_inc(e_state, 1)
                    dve.wait_ge(e_state, n)
                    dve.wait_ge(f_tg, n)
            dve.wait_ge(r_tg, TT)
            for j in range(4):
                t.step(dve.tensor_scalar(R[:, j, :], R[:, j, :], pc("lnx_w", j), pc("lnx_b", j), mul, add))
            t.settle()
            t.link(dve.tensor_tensor(wide(R), wide(R), wide(BON), add))
            dve.tensor_tensor(wide(R), wide(R), wide(G), mul).then_inc(mix_ready, 1)
            dve.scalar_tensor_tensor(out=wide(GQ), in0=wide(GQ), scalar=pc2(GDNN), in1=wide(Z),
                                     op0=mul, op1=mul).then_inc(mix_ready, 1)

            def residual(q):
                for k in range(KT):
                    filled(q + k)
                    dve.tensor_tensor(XT[:, k, :], XT[:, k, :], src(q + k)[:, :], add).then_inc(bank_read, 1)

            def mlp(l):
                with dve.Fori(0, 4) as i:
                    for b in range(8):
                        dve.wait_ge(bank_read, i * 8 + (q_m1[l] + b + 1))
                        x = RELU[:, b % 4, :]
                        dst = H1[:, bass.ds(i * 8 + b, 1), :].rearrange("p a w -> p (a w)")
                        dve.tensor_tensor(dst, x, x, mul).then_inc(h1_ready, 1)
                residual(q_m2[l])

            residual(q_out[0])
            norm(1)
            mlp(0)
            norm(2)

            IK = L1[:, 20, :]
            filled(q_ikm)
            dve.wait_ge(bank_read, q_ikm)
            dve.scalar_tensor_tensor(out=IK, in0=src(q_ikm)[:, :], scalar=-1.0 / HD, in1=IK,
                                     op0=mul, op1=add).then_inc(ik_centred, 1)
            dve.wait_ge(ik_centred, 1)
            dve.sem_inc(bank_read, 1)
            dve.wait_ge(n_rs, 1)
            t.link(dve.scalar_tensor_tensor(out=IK, in0=IK, scalar=pc2(LNW), in1=RS1[:, 0, :],
                                            op0=mul, op1=mul))
            dve.tensor_scalar(IK, IK, pc2(LNB), None, add).then_inc(n_used, 1)
            for n, (lo, wgt) in enumerate(((0, QW[:, 0:1]), (4, QW[:, 1:2]), (12, pc2(MKN)))):
                dve.wait_ge(n_rs, n + 2)
                dve.scalar_tensor_tensor(out=wide(L1[:, lo:lo + 4, :]), in0=wide(L1[:, lo:lo + 4, :]),
                                         scalar=wgt, in1=wide(RS1), op0=mul, op1=mul).then_inc(n_used, 1)
            dve.wait_ge(n_rs, 5)
            for g in range(2):
                dve.scalar_tensor_tensor(out=L1[:, 9 + 2 * g, :], in0=L1[:, 8 + 2 * g, :],
                                         scalar=pc2(DKN), in1=RS1[:, g, :], op0=mul, op1=mul)
            t.step(dve.tensor_copy(NMX[:, 0:1], pc2(0)))
            t.settle()
            for g in range(2):
                ins = dve.tensor_copy(L1[:, 8 + 2 * g, :], L1[:, 9 + 2 * g, :])
            ins.then_inc(n_used, 1)

            u = 0
            for i in range(1, TT):
                for hh in range(NH):
                    wdt = P * (i + 1)
                    dve.wait_ge(idx_relu, 4 + u + 1)
                    wgt = IW[:, i, hh:hh + 1]
                    s = SCORE[:, i - 1, 0:wdt]
                    if hh == 0:
                        dve.tensor_scalar(s, RT[:, u % 4, 0:wdt], wgt, None, mul).then_inc(idx_acc, 1)
                    else:
                        dve.scalar_tensor_tensor(out=s, in0=RT[:, u % 4, 0:wdt], scalar=wgt, in1=s,
                                                 op0=mul, op1=add).then_inc(idx_acc, 1)
                    u += 1
                    dve.wait_ge(idx_acc, u)
            rounds = TOPK // 8
            for i in range(1, TT):
                s = SCORE[:, i - 1, 0:P * (i + 1)]
                dve.wait_ge(idx_masked, i)
                with dve.Fori(0, rounds) as r:
                    with t.loop(r, 2, rounds):
                        t.link(dve.max(M8, s))
                        dve.sem_inc(topk_rounds, 1)
                        t.link(dve.match_replace(s, M8, s, TAKEN))
            dve.wait_ge(dist_ready, 1)
            for i in range(TT):
                wdt = P * (i + 1)
                d = DIST[:, W - wdt:W]
                lo = bias_off(i)
                t.step(dve.tensor_copy(BIAS[:, 1, lo:lo + wdt], d))
                if i == 0:
                    t.step(dve.tensor_copy(BIAS[:, 0, lo:lo + wdt], d))
                else:
                    s = SCORE[:, i - 1, 0:wdt]
                    t.link(dve.tensor_scalar(s, s, 0.5 * (CAUSAL_FILL + TAKEN), FAR, ALU.is_gt, mul))
                    t.step(dve.tensor_tensor(BIAS[:, 0, lo:lo + wdt], s, d, ALU.max))
            t.settle()

            dve.sem_inc(at_z, 4)
            dve.sem_inc(at_on, 1)
            with dve.Fori(0, 2) as ty:
                with dve.Fori(0, PAIRS) as j:
                    pair8 = ty * 32 + j * 8
                    with t.loop(ty, 4, 2), t.loop(j, 1, PAIRS):
                        for u in range(8):
                            i, p = u // 2, u % 2
                            wdt = P * (i + 1)
                            z = ZB[:, ZSLOT[u], 0:wdt]
                            dve.wait_ge(at_qk, pair8 + (u + 1))
                            if u >= 3:
                                dve.wait_ge(at_t, pair8 + (u - 2))
                            elif u == 0:
                                dve.wait_ge(at_on, ty * 4 + j + 1)
                            slope = SLOPE[:, bass.ds(ty * 8 + j * 2 + p, 1)]
                            dist = BIAS[:, bass.ds(ty, 1), bias_off(i):bias_off(i) + wdt]\
                                .rearrange("p a w -> p (a w)")
                            dve.scalar_tensor_tensor(out=z, in0=dist, scalar=slope,
                                                     in1=bank[u % 4][:, 0:wdt], op0=mul, op1=add)\
                               .then_inc(at_z, 1)
                            dve.wait_ge(at_z, pair8 + (4 + u + 1))
                            dve.tensor_reduce(NMX[:, u:u + 1], z, AX.X, ALU.max, negate=True)\
                               .then_inc(at_mx, 1)
                        dve.wait_ge(at_p, pair8 + 8)
                        t.link(dve.reciprocal(RINV, RSUM))
                        dve.wait_ge(at_o, pair8 + 8)
                        dst = ON[:, :, bass.ds(ty * 512 + j * 128, 128)].rearrange("p i (q d) -> p i q d", q=2)
                        dve.tensor_tensor(dst, bank[6][:, :].rearrange("p (i q d) -> p i q d", i=4, q=2),
                                          RINV.rearrange("p (i q) -> p i q", i=4).unsqueeze(3)
                                          .broadcast_to([P, 4, 2, HD]), mul).then_inc(at_on, 1)
            for k in range(KT):
                filled(q_mix + k)
                dve.tensor_copy(HT[:, k, :], src(q_mix + k)[:, :]).then_inc(bank_read, 1)
            residual(q_out[1])
            norm(3)
            mlp(1)

        @block.gpsimd
        def _(pool):
            t = Tally(pool, pool_step)
            mul = ALU.mult

            def select(x, base, pattern, cm, fill, op=ALU.is_ge):
                t.link(pool.affine_select(out=x, in_=x, pattern=pattern, compare_op=op, fill=fill,
                                          base=base, channel_multiplier=cm))

            t.step(pool.memset(IDENT, 0.0))
            t.step(pool.memset(ONES, 1.0))
            t.step(pool.memset(INCL, 1.0))
            t.step(pool.memset(STRICT, 1.0))
            t.step(pool.memset(HEADS2, 0.0))
            t.step(pool.memset(wide(MERGE), 0.0))
            t.step(pool.memset(SCANM, 1.0))
            t.settle()
            select(IDENT, 0, [[-1, P]], 1, 1.0, ALU.not_equal)
            select(INCL, 0, [[1, P]], -1, 0.0)
            select(STRICT, -1, [[1, P]], -1, 0.0)
            for p in range(2):
                t.link(pool.memset(HEADS2[p * HD:(p + 1) * HD, p * HD:(p + 1) * HD], 1.0))
            t.link(pool.memset(SCANM.rearrange("p (k t) -> p k t", k=4)[:, :, 0:1], 0.0))
            for lev in range(LEVELS):
                b = 1 << lev
                low = MERGE[:, lev, :].rearrange("p (n q w) -> p n q w", q=2, w=b)[:, :, 0, :]
                t.link(pool.memset(low, 1.0))
                select(low, -b, [[-2 * b, P // (2 * b)], [0, b]], 1, 0.0)
                select(low, 2 * b - 1, [[2 * b, P // (2 * b)], [0, b]], -1, 0.0)
            for g in range(16):
                col = (g % 2) * NH + g // 2
                t.step(pool.memset(SLOPE[:, col:col + 1], -float(np.float32(2.0) ** np.float32(-0.5 * (g + 1)))))
            t.settle()
            pool.memset(M8, 0.0).then_inc(consts, 1)
            for s in range(2):
                t.step(pool.memset(STAGE[s][:, :, 0:3], 0.0))
            t.settle()
            pool.memset(NMX, 0.0).then_inc(pads_zero, 1)

            pool.wait_ge(l0_dve, 1)
            pool.memset(wide(SR), 0.0)
            pool.memset(wide(SG), 0.0)
            with pool.Fori(0, TT) as c:
                n = c + 1
                here = bass.ds(c * P, P)
                row = bass.ds(c, 1)

                def by_parity(x, p):
                    return x[:, row, :].rearrange("p o (j q) -> p (o j) q", q=2)[:, :, p]\
                        .unsqueeze(2).broadcast_to([P, 4, P])

                for p in range(2):
                    ins = pool.tensor_tensor(GTRI[p], INCL.unsqueeze(1).broadcast_to([P, 4, P]),
                                             by_parity(GLOG, p), mul)
                ins.then_inc(e_gtri, 1)
                pool.tensor_copy(KC, GK[:, :, here])
                pool.tensor_copy(QC, GQ[:, :, here])
                pool.tensor_copy(VGC, GV[:, :, here])
                pool.tensor_copy(VRC, V[:, :, here]).then_inc(e_copy, 1)
                pool.wait_ge(e_exp, n)
                pool.tensor_tensor(BD, BD, B[:, :, here], mul)
                pool.tensor_tensor(AD, AD, KK[:, :, here], mul).then_inc(e_ba, 1)
                pool.wait_ge(e_dt, n)
                for p in range(2):
                    pool.tensor_tensor(LT[2 + p], DT[p], by_parity(BETA, p), mul)
                    ins = pool.tensor_tensor(GRK[p], DT[p], INCL.unsqueeze(1).broadcast_to([P, 4, P]), mul)
                ins.then_inc(e_dmask, 1)
                for g in range(4):
                    pool.tensor_copy(TI[g], IDENT.unsqueeze(1).broadcast_to([P, 4, P]))
                    pool.tensor_copy(QI[g], IDENT.unsqueeze(1).broadcast_to([P, 4, P])).then_inc(inv_t, 1)
                pool.wait_ge(f_tg, n)
                pool.wait_ge(e_state, n)

            pool.wait_ge(bank_read, q_ikm)
            t.link(pool.iota(DIST.bitcast(I32), [[-1, W]], base=W - P, channel_multiplier=1))
            t.link(pool.tensor_copy(DIST, DIST.bitcast(I32)))
            pool.affine_select(out=DIST, in_=DIST, pattern=[[-1, W]], compare_op=ALU.is_ge, fill=FAR,
                               base=W - P, channel_multiplier=1).then_inc(dist_ready, 1)
            for i in range(1, TT):
                pool.wait_ge(idx_acc, NH * i)
                d = SCORE[:, i - 1, P * i:P * (i + 1)]
                pool.affine_select(out=d, in_=d, pattern=[[-1, P]], compare_op=ALU.is_ge,
                                   fill=CAUSAL_FILL, base=0, channel_multiplier=1).then_inc(idx_masked, 1)
            with pool.Fori(0, 2) as ty:
                with pool.Fori(0, PAIRS) as j:
                    pool.wait_ge(at_z, ty * 32 + j * 8 + 4)
                    q = L1[:, bass.ds(ty * 4 + j, 1), :].rearrange("p a w -> p (a w)")
                    k = L1[:, bass.ds(ty * 4 + j + 8, 1), :].rearrange("p a w -> p (a w)")
                    pool.tensor_copy(QS, q)
                    pool.tensor_copy(KS, k).then_inc(at_stage, 1)


PAR64 = ("gdn_norm_w", "dsa_q_norm", "dsa_k_norm", "idx_k_ln_w", "idx_k_ln_b", "moba_q_norm",
         "moba_k_norm")
N_PAR = 2 + 8 + 1 + 2 * len(PAR64) + 6
ZSLOT = [u % 3 for u in range(8)]
DVE_CHUNK = 16

_INS = ("x norm1_g norm2_g mlp_w1 mlp_w2 ev_w_in ev_w_out rwkv_mu rwkv_w0 rwkv_w2 rwkv_a0 rwkv_a2 "
        "rwkv_g2 rwkv_k_k rwkv_k_a rwkv_r_k rwkv_lnx_w rwkv_lnx_b gdn_conv_w gdn_a_log gdn_dt_bias "
        "gdn_norm_w od_w_in od_w_out dsa_q_norm dsa_k_norm idx_k_ln_w idx_k_ln_b moba_q_norm "
        "moba_k_norm").split()


def kernel(**inputs):
    import concourse.bacc as _bacc
    from concourse.bass_utils import run_bass_kernel_spmd as _run

    nc = _bacc.Bacc("TRN2", target_bir_lowering=False, num_devices=1)
    arrays, aps = {}, {}
    for name in _INS:
        x = np.ascontiguousarray(inputs[name])
        arrays[f"in_{name}_dram"] = x
        aps[name] = nc.dram_tensor(f"in_{name}_dram", x.shape, mybir.dt.from_np(x.dtype),
                                   kind="ExternalInput").ap()
    out = nc.dram_tensor("out_0_dram", (1, SEQ, D), F32, kind="ExternalOutput").ap()
    trunk_kernel(nc, aps, out)
    r = _run(nc, [arrays], core_ids=[0])
    return r.results[0]["out_0_dram"]
```

```python
from contextlib import ExitStack, contextmanager

import numpy as np

import concourse.bass as bass
from concourse import mybir

F32 = mybir.dt.float32
F32R = mybir.dt.float32r
I32 = mybir.dt.int32
ALU = mybir.AluOpType
ACT = mybir.ActivationFunctionType
AX = mybir.AxisListType

P = 128
SEQ = 512
D = 1024
DFF = 4096
HD = 64
KT = D // P
TT = SEQ // P
W = SEQ
NH = 8
PAIRS = NH // 2
PW = 516
CW = P + 1
UW = 256
LEVELS = 6
RMS_EPS = 1e-6
GN_EPS = 6.4e-4
RWKV_COLS = 1792
GDN_QKV = RWKV_COLS
GDN_BA = RWKV_COLS + 3 * 512
GDN_Z = GDN_BA + 2 * NH
OD_K, OD_V, OD_IQ, OD_IK, OD_IW = 512, 640, 768, 1280, 1344
OD_MQ = 1352
OD_MV = OD_MQ + 1024
TOPK = min(256, SEQ // 4)
CAUSAL_FILL = -3.0e38
TAKEN = -3.4e38
FAR = 1.0e30


class Tally:

    def __init__(self, eng, sem):
        self.eng, self.sem, self.n, self.loops = eng, sem, 0, []

    @contextmanager
    def loop(self, reg, per, trips, first=0):
        start = self.n
        self.loops.append((reg, per, first))
        yield
        self.loops.pop()
        assert self.n - start == per, (self.n - start, per)
        self.n = start + per * trips

    def value(self, n=None):
        v = self.n if n is None else n
        for reg, per, first in self.loops:
            v = (reg * per) + (v - first * per)
        return v

    def step(self, ins):
        self.n += 1
        return ins.then_inc(self.sem, 1)

    def settle(self):
        self.eng.wait_ge(self.sem, self.value())

    def link(self, ins):
        self.step(ins)
        self.settle()


def trunk_kernel(nc, a, out):
    ctx = ExitStack()
    with ctx:
        def sem(name):
            return ctx.enter_context(nc.semaphore(name))

        ARENA, PARTS = 53000, 28224
        lower = ctx.enter_context(nc.sbuf_tensor("lower", [P, PARTS], F32))
        with nc.sbuf_tensor("upper", [P, ARENA - PARTS], F32) as upper:
            pass

        def parts(name, a_, n, w):
            return ctx.enter_context(nc.sbuf_tensor(name, [P, a_, n, w], F32R))

        AH, AL, HL, HH = (parts(n_, 1, KT, W)[:, 0] for n_ in ("a_hi", "a_lo", "h_lo", "h_hi"))
        WH, WL = parts("w_hi", 2, KT, UW), parts("w_lo", 2, KT, UW)
        IWH, IWL = (parts(n_, 1, KT, NH)[:, 0] for n_ in ("iw_hi", "iw_lo"))
        bank = [ctx.enter_context(nc.psum_tensor(f"bank{i}", [P, 512], F32)) for i in range(8)]

        top = [0]

        def carve(n):
            off = top[0]
            top[0] += n
            assert top[0] <= ARENA, top[0]
            return off

        def flat(off, n):
            if off >= PARTS:
                return upper[:, off - PARTS:off - PARTS + n]
            assert off + n <= PARTS, (off, n)
            return lower[:, off:off + n]

        def grid(off, n, w):
            return flat(off, n * w).rearrange("p (n w) -> p n w", n=n)

        def wide(x):
            return x.rearrange("p n w -> p (n w)")

        XT = grid(carve(KT * W), KT, W)
        IDENT, ONES = flat(carve(P), P), flat(carve(P), P)
        HEADS2 = flat(carve(P), P)
        INCL = flat(carve(P), P)
        STRICT = flat(carve(P), P)
        o_merge = carve(LEVELS * P)
        MERGE = grid(o_merge, LEVELS, P)
        SCANM = flat(carve(4 * CW), 4 * CW)
        PC = flat(carve(P), P)
        PC2 = flat(carve(8), 8)
        misc = [carve(576)]
        misc_end = top[0]

        def small(n):
            off = misc[0]
            misc[0] += n
            assert misc[0] <= misc_end
            return flat(off, n)

        def by_chunk(n):
            return small(TT * n).rearrange("p (c h) -> p c h", c=TT)

        OMKA = small(4)
        ALOG, DTB, NEA = small(NH), small(NH), small(NH)
        AB = by_chunk(16)
        BETA, GLOG, GTMP, GCUM = by_chunk(NH), by_chunk(NH), by_chunk(NH), by_chunk(NH)
        EG = by_chunk(NH)
        EREST = by_chunk(NH)
        ESTATE = by_chunk(PAIRS)
        SM, ESM = small(8), small(8)
        NMEAN, VAR, RSTD = small(NH), small(16), small(16)
        SLOPE = small(16)
        QW = small(2)
        IW = by_chunk(NH)
        IWW = small(KT * NH).rearrange("p (k n) -> p k n", k=KT)
        M8 = small(8 * (TT - 1)).rearrange("p (i n) -> p i n", i=TT - 1)
        NMX, RSUM, RINV = small(NH), small(NH), small(NH)

        o_ht = carve(KT * W)
        HT = grid(o_ht, KT, W)
        o_ring = carve(2 * KT * W)
        RING = flat(o_ring, 2 * KT * W).rearrange("p (s k n) -> p s k n", s=2, k=KT)
        work = top[0]

        o_rkv, o_z, o_lw2 = carve(12 * W), carve(4 * W), carve(W)
        top[0] = PARTS
        o_gqkv = carve(12 * W)
        o_g, o_bon, o_kk, o_b = (carve(4 * W) for _ in range(4))
        o_cum = carve(4 * 4 * CW)
        RKV, GQKV = grid(o_rkv, 12, W), grid(o_gqkv, 12, W)
        R, K, V = (grid(o_rkv + i * 4 * W, 4, W) for i in range(3))
        GQ, GK, GV = (grid(o_gqkv + i * 4 * W, 4, W) for i in range(3))
        Z, KK, B, G, BON = (grid(o, 4, W) for o in (o_z, o_kk, o_b, o_g, o_bon))
        CUM = flat(o_cum, 16 * CW).rearrange("p (c k t) -> p c k t", c=4, k=4)
        tail = top[0]
        XIN = grid(o_gqkv, TT, D)
        PR, PR2 = flat(o_z, P), flat(o_z + P, P)
        SQ = [grid(o_g, KT, W)] + [grid(o_ring + 4 * W, KT, W)] * 3
        RS = [flat(o_cum, W)] + [flat(o_ring + 12 * W, W)] * 3

        o_stage = [carve(4 * PW), carve(4 * PW)]
        STAGE = [grid(o, 4, PW) for o in o_stage]
        SQA, SQB = (grid(o, 4, W) for o in o_stage)
        CONV = grid(carve(4 * W), 4, W)
        RSB = CONV
        LW2, G2 = flat(o_lw2, W), flat(carve(W), W)
        WA, GD = flat(carve(W), W), flat(carve(W), W)
        TMPD = flat(carve(W), W)

        spare = [[o_ht, KT * W], [o_ring, 2 * KT * W], [tail, ARENA - tail]]

        def chunk_buf(w=P):
            for s in spare:
                if s[1] >= 4 * P:
                    s[0] += 4 * P
                    s[1] -= 4 * P
                    return grid(s[0] - 4 * P, 4 * P // w, w)
            raise AssertionError("no room")

        LT, TI, QI, XM = ([chunk_buf() for _ in range(4)] for _ in range(4))
        RD, KD, BD, AD = (chunk_buf() for _ in range(4))
        KC, QC, VRC, VGC = (chunk_buf() for _ in range(4))
        KTOK, BTOK, VR, KGT, VG = (wide(chunk_buf()) for _ in range(5))
        MK, RK, RBM, GRK = ([chunk_buf() for _ in range(2)] for _ in range(4))
        SR, SG = chunk_buf(), chunk_buf()
        DT, GTRI = [XM[2], XM[3]], [XM[0], XM[1]]
        X1R, UN, VN = wide(MK[0]), wide(MK[1]), wide(LT[2])
        OR, OG = wide(LT[0]), wide(LT[1])
        OSQ, OSQG, TMPG, TMPS = wide(TI[0]), wide(TI[1]), wide(TI[2]), TI[3]
        TMPK = wide(XM[0])

        RAW = flat(o_ht, 2 * KT * UW).rearrange("p (s k n) -> p s k n", s=2, k=KT)
        SQT = grid(o_ring, 4, W)

        L1 = grid(o_ring, 21, W)
        o_vall = o_ring + 21 * W
        VALL = grid(o_vall, TT, 1024)
        o_score = o_vall + 4096
        SCORE = grid(o_score, 3, W)
        RS1 = grid(o_score, 4, W)
        DIST = flat(o_merge, W)
        o_bias = PARTS
        BIASW = P * TT * (TT + 1) // 2
        BIAS = grid(o_bias, 2, BIASW)
        o_att = o_bias + 2 * BIASW
        SQ1 = [grid(o_att, 4, W), grid(o_att + 4 * W, 4, W)]
        RT = grid(o_att, 4, W)
        QS, KS = flat(o_att + 4 * W, W), flat(o_att + 5 * W, W)
        ZB = grid(o_att + 6 * W, 3, W)
        PTS = grid(o_att + 9 * W, 2, W)
        o_on = PARTS + 2 * KT * W
        assert o_att + 11 * W <= o_on
        ON = grid(o_on, TT, 1024)
        OUTT = grid(work, TT, D)

        at = dict(norm1=0, norm2=16, mu=32, w0=46, a0=50, k_k=54, k_a=58, r_k=62, lnx_w=66,
                  lnx_b=70, conv=74)
        NPC = 122
        GDNN, DQN, DKN, LNW, LNB, MQN, MKN = range(7)

        def pc(name, i):
            return PC[:, at[name] + i:at[name] + i + 1]

        def pc2(i):
            return PC2[:, i:i + 1]

        def bias_off(i):
            return P * i * (i + 1) // 2

        bank_filled, bank_read = sem("bank_filled"), sem("bank_read")
        q_x, q_lora, q_ab, q_z, q_w, q_a, q_g, q_pair = 2, 11, 13, 14, 18, 22, 26, 30
        q_kk, q_gq, q_gk, q_bon, q_cum = 54, 58, 62, 66, 70
        q_out, q_m1, q_m2 = [71, 222], [80, 231], [88, 239]
        q_norm = [10, 79, 144, 230]
        q_k, q_ik, q_v, q_iq, q_iw, q_ikm, q_ikv, q_mv = 145, 147, 148, 149, 153, 154, 159, [155, 160]
        q_idx, q_dq, q_dqn, q_mqn, q_mkn, q_k2n, q_mix = 164, 188, 200, 204, 208, 212, 214
        q_fin = 295
        u_out, u_mlp, u_kv, u_iq, u_mv, u_dq, u_mqk = [0, 48], [4, 52], 36, 38, 40, 42, 44

        (dma_par, dma_x, dma_out, consts, squares, rms, h_ready, below_begun, inverse_begun, topk_rounds,
         pads_zero, lora_shifted, lora_act, cum_ready, stage_in, stage_used, conv_out, conv_used,
         kk_ready, sq_grp, rs_grp, rs_used, bonus_in, gate_in, gate_ln, glog_ready,
         gcum_ready, l0_dve, l0_act, mix_ready, h1_ready, h_hi, h_lo, mix_hi, mix_lo, hi_ready,
         lo_ready, iw_split) = (sem(n) for n in (
             "dma_par dma_x dma_out consts squares rms h_ready below_begun inverse_begun topk_rounds pads_zero "
             "lora_shifted lora_act cum_ready stage_in stage_used conv_out conv_used kk_ready "
             "sq_grp rs_grp rs_used bonus_in gate_in gate_ln glog_ready gcum_ready "
             "l0_dve l0_act mix_ready h1_ready h_hi h_lo mix_hi mix_lo hi_ready lo_ready "
             "iw_split").split())
        w_full = [sem("w_full0"), sem("w_full1")]
        raw_full = [sem("raw_full0"), sem("raw_full1")]
        act_step, dve_step, pool_step = sem("act_step"), sem("dve_step"), sem("pool_step")
        (f_grow, f_kt, f_vg, f_vr, f_kk, f_kq, f_lt, f_mk, f_rk, f_rb, f_ktok, f_btok, f_x1, f_ks,
         f_u, f_y, f_or, f_og, f_qs, f_sr, f_sg, f_tr, f_tg) = (sem(n) for n in (
             "f_grow f_kt f_vg f_vr f_kk f_kq f_lt f_mk f_rk f_rb f_ktok f_btok f_x1 f_ks "
             "f_u f_y f_or f_og f_qs f_sr f_sg f_tr f_tg").split())
        (e_diff, e_exp, e_copy, e_gtri, e_dsub, e_dt, e_dmask, e_rk, e_ba, e_s0, r_kt, r_vg, r_vr,
         r_kk, r_kq, r_lt, r_mk, r_rk, r_rb, r_ktok, r_btok, r_x1, r_ks, r_u, r_y, e_var, e_rstd,
         e_on, e_og, r_tr, r_tg, e_state, e_ln) = (sem(n) for n in (
             "e_diff e_exp e_copy e_gtri e_dsub e_dt e_dmask e_rk e_ba e_s0 r_kt r_vg r_vr "
             "r_kk r_kq r_lt r_mk r_rk r_rb r_ktok r_btok r_x1 r_ks r_u r_y e_var e_rstd "
             "e_on e_og r_tr r_tg e_state e_ln").split())
        inv_x, inv_xs, inv_y, inv_t, inv_turned, inv_q, inv_first = (sem(n) for n in (
            "inv_x inv_xs inv_y inv_t inv_turned inv_q inv_first").split())
        (f_u1, f_y1, f_zr, f_zg, r_u1, r_y1, r_zr, r_zg) = (sem(n) for n in (
            "f_u1 f_y1 f_zr f_zg r_u1 r_y1 r_zr r_zg").split())
        MERGES = 4 * (LEVELS - 1)
        (n_sq, n_rs, n_used, ik_centred, dist_ready, idx_acc, idx_masked,
         bias_ready, at_stage, at_qk, at_z, at_mx, at_p, at_t, at_pt, at_o, at_on) = (
             sem(n) for n in (
                 "n_sq n_rs n_used ik_centred dist_ready idx_acc idx_masked "
                 "bias_ready at_stage at_qk at_z at_mx at_p at_t at_pt at_o at_on").split())

        block = ctx.enter_context(nc.Block())
        ev, od = a["ev_w_in"][0], a["od_w_in"][0]

        def raw_count(u):
            return 16 * (u // 2 + 1) + ((48, 32)[u % 2] if u >= u_kv else 0)

        def as_f32(x):
            return x.bitcast(F32)

        def kmaj(w):
            return w.rearrange("(k p) n -> p k n", p=P)

        @block.sync
        def _(sp):
            def load(slot, cols, at=0):
                w = cols.shape[-1]
                sp.dma_start(RING[:, slot, :, at:at + w], kmaj(cols)).then_inc(w_full[slot], 16)

            sp.dma_start(XIN, a["x"][0].rearrange("(t p) d -> p t d", p=P)).then_inc(dma_x, 16)
            load(0, ev[:, 1536:RWKV_COLS])
            load(0, ev[:, GDN_BA:GDN_BA + 16], at=256)
            load(1, ev[:, GDN_Z:GDN_Z + 512])
            sp.wait_ge(bank_filled, q_z)
            load(0, ev[:, 0:512])
            sp.wait_ge(bank_filled, q_w)
            load(1, ev[:, GDN_QKV:GDN_QKV + 512])
            with sp.Fori(1, 3) as i:
                sp.wait_ge(bank_filled, i * 8 + (q_pair - 4))
                load(0, ev[:, bass.ds(i * 512, 512)])
                sp.wait_ge(bank_filled, i * 8 + q_pair)
                load(1, ev[:, bass.ds(i * 512 + GDN_QKV, 512)])

            def unit(u, dyn=0):
                if u >= 2:
                    sp.wait_ge(lo_ready, dyn + (u - 1))

            def load_raw(u, cols, at=0):
                sp.dma_start(RAW[:, u % 2, :, at:at + cols.shape[-1]], kmaj(cols))\
                  .then_inc(raw_full[u % 2], 16)

            def w_out(l):
                wout = a["ev_w_out" if l == 0 else "od_w_out"][0]
                for v in range(4):
                    unit(u_out[l] + v)
                    load_raw(u_out[l] + v, wout[:, v * UW:(v + 1) * UW])

            def mlp(l):
                w1, w2 = a["mlp_w1"][l], a["mlp_w2"][l].rearrange("(r p) n -> p r n", p=P)
                with sp.Fori(0, 4) as i:
                    for v in range(8):
                        u = u_mlp[l] + v
                        unit(u, i * 8)
                        if v < 4:
                            load_raw(u, w1[:, bass.ds(i * 1024 + v * UW, UW)])
                        else:
                            sp.dma_start(RAW[:, u % 2], w2[:, bass.ds(i * 8, 8), (v - 4) * UW:(v - 3) * UW])\
                              .then_inc(raw_full[u % 2], 16)

            sp.wait_ge(f_tg, TT)
            sp.wait_ge(e_state, TT)
            w_out(0)
            mlp(0)
            unit(u_kv)
            for g in range(2):
                for half in range(2):
                    load_raw(u_kv, od[:, OD_K + g * HD:OD_K + (g + 1) * HD], at=(2 * g + half) * HD)
            unit(u_kv + 1)
            for half in range(2):
                load_raw(u_kv + 1, od[:, OD_IK:OD_IK + HD], at=half * HD)
            load_raw(u_kv + 1, od[:, OD_V:OD_V + 128], at=128)
            for u0, col in ((u_iq, OD_IQ), (u_mv, OD_MV), (u_dq, 0), (u_mqk, OD_MQ), (u_mqk + 2, OD_MQ + 512)):
                for v in range(2):
                    unit(u0 + v)
                    load_raw(u0 + v, od[:, col + v * UW:col + (v + 1) * UW])
            w_out(1)
            mlp(1)
            for i in range(TT):
                sp.wait_ge(bank_read, q_fin + 2 * i + 2)
                sp.dma_start(out[0, i * P:(i + 1) * P, :], OUTT[:, i, :]).then_inc(dma_out, 16)
            sp.wait_ge(dma_out, 16 * TT)

        @block.tensor
        def _(pe):
            full = [0, 0]

            def arrived(slot, dmas=1):
                full[slot] += 16 * dmas
                pe.wait_ge(w_full[slot], full[slot])

            def take(q, dyn=0):
                if q >= 8:
                    pe.wait_ge(bank_read, dyn + (q - 7))
                return bank[q % 8]

            def group(slot, act, q, dyn=0, ready=None):
                for b in range(4):
                    o = take(q + b, dyn)
                    for k in range(KT):
                        if ready is not None and b == 0:
                            ready(k)
                        mm = pe.matmul(o[:, :], RING[:, slot, k, b * P:(b + 1) * P], act(k),
                                       start=(k == 0), stop=(k == KT - 1))
                    mm.then_inc(bank_filled, 1)

            def norm(n):
                o = take(q_norm[n])
                for k in range(KT):
                    pe.wait_ge(squares, KT * n + k + 1)
                    mm = pe.matmul(o[:, :], ONES, SQ[n][:, k, :], start=(k == 0), stop=(k == KT - 1))
                mm.then_inc(bank_filled, 1)

            def normed(n):
                return lambda k: pe.wait_ge(h_ready, KT * n + k + 1)

            def h(k):
                return HT[:, k, :]

            pe.wait_ge(consts, 1)
            pe.wait_ge(dma_par, 16 * N_PAR)
            pe.transpose(take(0)[:, 0:NPC], PR[0:NPC, :], IDENT[0:NPC, 0:NPC]).then_inc(bank_filled, 1)
            pe.transpose(take(1)[:, 0:7], PR2[0:7, :], IDENT[0:7, 0:7]).then_inc(bank_filled, 1)
            pe.wait_ge(dma_x, 16)
            for k in range(KT):
                o = take(q_x + k)
                for i in range(TT):
                    mm = pe.transpose(o[:, i * P:(i + 1) * P], XIN[:, i, k * P:(k + 1) * P], IDENT)
                mm.then_inc(bank_filled, 1)
            norm(0)

            arrived(0, 2)
            for b in range(2):
                o = take(q_lora + b)
                for k in range(KT):
                    if b == 0:
                        pe.wait_ge(h_ready, k + 1)
                    mm = pe.matmul(o[:, :], RING[:, 0, k, b * P:(b + 1) * P], h(k),
                                   start=(k == 0), stop=(k == KT - 1))
                mm.then_inc(bank_filled, 1)
            o = take(q_ab)
            for i in range(TT):
                for k in range(KT):
                    mm = pe.matmul(o[:, 16 * i:16 * i + 16], HT[:, k, i * P:(i + 1) * P],
                                   RING[:, 0, k, 256:272], start=(k == 0), stop=(k == KT - 1))
            mm.then_inc(bank_filled, 1)
            arrived(1)
            group(1, h, q_z)

            pe.wait_ge(lora_act, 2)
            for c in range(4):
                pe.matmul(take(q_w + c)[:, :], LW2[0:HD, c * P:(c + 1) * P], WA[0:HD, :],
                          start=True, stop=True).then_inc(bank_filled, 1)
            for c in range(4):
                pe.matmul(take(q_a + c)[:, :], LW2[HD:P, c * P:(c + 1) * P], WA[HD:P, :],
                          start=True, stop=True).then_inc(bank_filled, 1)
            for c in range(4):
                pe.matmul(take(q_g + c)[:, :], G2[:, c * P:(c + 1) * P], GD,
                          start=True, stop=True).then_inc(bank_filled, 1)

            with pe.Fori(0, 3) as i:
                pe.wait_ge(w_full[0], i * 16 + (full[0] + 16))
                group(0, h, q_pair, i * 8)
                pe.wait_ge(w_full[1], i * 16 + (full[1] + 16))
                group(1, h, q_pair + 4, i * 8)
            full[0] += 48
            full[1] += 48

            for n, (q, src) in enumerate(((q_kk, SQA), (q_gq, SQB), (q_gk, SQA), (q_bon, SQB))):
                if n < 3:
                    pe.wait_ge(sq_grp, n + 1)
                else:
                    pe.wait_ge(bonus_in, 4)
                for c in range(4):
                    pe.matmul(take(q + c)[:, :], HEADS2, src[:, c, :],
                              start=True, stop=True).then_inc(bank_filled, 1)
            pe.wait_ge(glog_ready, 1)
            o = take(q_cum)
            pe.matmul(o[:, 0:32], INCL, wide(GLOG), start=True, stop=True)
            pe.matmul(o[:, 32:64], ONES, wide(GLOG), start=True, stop=True).then_inc(bank_filled, 1)

            pe.wait_ge(l0_dve, 1)
            pe.wait_ge(l0_act, 1)

            def half(x, p, j):
                return x[p * HD:(p + 1) * HD, j, :]

            def head_products(banks, lhs, rhs, done):
                for j in range(PAIRS):
                    for p in range(2):
                        mm = pe.matmul(bank[banks[p]][:, j * P:(j + 1) * P], half(lhs, p, j),
                                       half(rhs, p, j), start=True, stop=True)
                mm.then_inc(done, 1)

            def turn(b, src, done):
                for j in range(PAIRS):
                    mm = pe.transpose(bank[b][:, j * P:(j + 1) * P], src[:, j, :], IDENT)
                mm.then_inc(done, 1)

            def turn_wide(b, src, done):
                for j in range(PAIRS):
                    mm = pe.transpose(bank[b][:, j * P:(j + 1) * P], src[:, j * P:(j + 1) * P], IDENT)
                mm.then_inc(done, 1)

            def by_state(b, lhs, state, more):
                for j in range(PAIRS):
                    mm = pe.matmul(bank[b][:, j * P:(j + 1) * P], lhs[:, j, :], state[:, j, :],
                                   start=(j == 0), stop=not more, skip_group_check=True)
                return mm

            def by_heads(b, mats, vals, first, last):
                for hh in range(NH):
                    cols = slice(hh * HD, (hh + 1) * HD)
                    mm = pe.matmul(bank[b][:, cols], mats[hh % 2][:, hh // 2, :], vals[:, cols],
                                   start=(first and hh == 0), stop=last, skip_group_check=True)
                return mm

            TOP, LOW = slice(0, HD), slice(HD, P)

            def below(b, mats, vals, rows, first):
                pe.sem_inc(below_begun, 1)
                for hh in range(NH):
                    cols = slice(hh * HD, (hh + 1) * HD)
                    mm = pe.matmul(bank[b][LOW, cols], mats[hh % 2][rows, hh // 2, LOW],
                                   vals[rows, cols], start=(first and hh == 0), stop=True,
                                   skip_group_check=True)
                return mm

            with pe.Fori(0, TT) as c:
                n = c + 1
                pe.wait_ge(e_gtri, n)
                for p in range(2):
                    mm = pe.matmul(bank[p][:, :], ONES, wide(GTRI[p]), start=True, stop=True)
                mm.then_inc(f_grow, 1)
                pe.wait_ge(e_copy, n)
                turn(2, KC, f_kt)
                turn(3, VGC, f_vg)
                turn(4, VRC, f_vr)
                head_products((5, 6), KC, KC, f_kk)
                pe.wait_ge(r_kt, n)
                head_products((7, 2), KC, QC, f_kq)
                pe.wait_ge(e_ba, n)
                pe.wait_ge(e_rk, n)
                pe.wait_ge(r_vg, n)
                pe.wait_ge(r_vr, n)
                head_products((3, 4), BD, AD, f_lt)
                pe.wait_ge(e_dsub, n)
                head_products((0, 1), KD, AD, f_mk)
                pe.wait_ge(r_kk, n)
                head_products((5, 6), KD, RD, f_rk)
                pe.wait_ge(r_kq, n)
                head_products((7, 2), BD, RD, f_rb)
                pe.wait_ge(r_lt, n)
                turn(3, KD, f_ktok)
                turn(4, BD, f_btok)
                pe.wait_ge(e_s0, n)
                pe.wait_ge(r_mk, n)
                by_state(0, AD, SR, True)
                by_heads(0, MK, VR, False, True).then_inc(f_x1, 1)
                by_state(1, KC, SG, False).then_inc(f_ks, 1)
                pe.wait_ge(r_x1, n)
                pe.wait_ge(r_ks, n)
                pe.wait_ge(r_rb, n)
                pe.wait_ge(r_btok, n)
                pe.sem_inc(inverse_begun, 1)
                for g in range(4):
                    pe.wait_ge(inv_q, c * (MERGES + 4) + (g + 1))
                    for j in range(PAIRS):
                        mm = pe.transpose(bank[2 * g][:, j * P:(j + 1) * P], QI[g][:, j, :], IDENT)
                    mm.then_inc(inv_first, 1)
                with pe.Fori(0, LEVELS - 1) as lev:
                    def merged(g, sem_, per, more=0):
                        pe.wait_ge(sem_, c * per + (lev * 4 + (g + 1 + more)))

                    for g in range(4):
                        merged(g, inv_t, MERGES + 4)
                        for j in range(PAIRS):
                            mm = pe.matmul(bank[2 * g][:, j * P:(j + 1) * P], LT[g][:, j, :],
                                           TI[g][:, j, :], start=True, stop=True)
                        mm.then_inc(inv_x, 1)
                    for g in range(4):
                        merged(g, inv_xs, MERGES)
                        merged(g, inv_q, MERGES + 4)
                        for j in range(PAIRS):
                            mm = pe.matmul(bank[2 * g][:, j * P:(j + 1) * P], QI[g][:, j, :],
                                           XM[g][:, j, :], start=True, stop=True)
                        mm.then_inc(inv_y, 1)
                    for g in range(4):
                        merged(g, inv_t, MERGES + 4, 4)
                        for j in range(PAIRS):
                            mm = pe.transpose(bank[2 * g + 1][:, j * P:(j + 1) * P], TI[g][:, j, :], IDENT)
                        mm.then_inc(inv_turned, 1)
                pe.wait_ge(inv_q, c * (MERGES + 4) + (MERGES + 4))
                by_heads(0, QI[0:2], X1R, True, True).then_inc(f_u1, 1)
                by_heads(1, QI[2:4], VG, True, True).then_inc(f_y1, 1)
                by_state(4, QC, SG, False).then_inc(f_qs, 1)
                by_state(2, RD, SR, True)
                by_heads(2, RK, VR, False, False)
                pe.wait_ge(r_u1, n)
                below(5, LT[0:2], X1R, TOP, True).then_inc(f_zr, 1)
                pe.wait_ge(r_y1, n)
                below(6, LT[2:4], VG, TOP, True).then_inc(f_zg, 1)
                pe.wait_ge(r_zr, n)
                below(0, QI[0:2], X1R, LOW, False).then_inc(f_u, 1)
                pe.wait_ge(r_zg, n)
                below(1, QI[2:4], VG, LOW, False).then_inc(f_y, 1)
                pe.wait_ge(r_u, n)
                by_heads(2, RBM, UN, False, True).then_inc(f_or, 1)
                pe.wait_ge(r_y, n)
                by_heads(3, GRK, VN, True, True).then_inc(f_og, 1)
                for j in range(PAIRS):
                    cols = slice(j * P, (j + 1) * P)
                    pe.matmul(bank[5][:, cols], KTOK[:, cols], VR[:, cols], start=(j == 0),
                              stop=False, skip_group_check=True)
                    mm = pe.matmul(bank[5][:, cols], BTOK[:, cols], UN[:, cols], start=False,
                                   stop=True, skip_group_check=True)
                mm.then_inc(f_sr, 1)
                for j in range(PAIRS):
                    cols = slice(j * P, (j + 1) * P)
                    mm = pe.matmul(bank[6][:, cols], KGT[:, cols], VN[:, cols], start=True, stop=True)
                mm.then_inc(f_sg, 1)
                pe.wait_ge(e_on, n)
                turn_wide(7, OR, f_tr)
                pe.wait_ge(e_og, n)
                turn_wide(0, OG, f_tg)
                pe.wait_ge(r_tg, n)
                pe.wait_ge(e_state, n)

            def products(o, pairs, waits=None):
                n_ = len(pairs)
                for i_, (k, wh, wl, xh, xl) in enumerate(pairs):
                    if waits is not None:
                        waits[0](k)
                    pe.matmul(o, wh, xh, start=(i_ == 0), stop=False)
                    pe.matmul(o, wl, xh, start=False, stop=False)
                for i_, (k, wh, wl, xh, xl) in enumerate(pairs):
                    if waits is not None:
                        waits[1](k)
                    mm = pe.matmul(o, wh, xl, start=False, stop=(i_ == n_ - 1))
                return mm

            def split_unit(u, q, xh, xl, dyn_u=0, dyn_q=0, waits=None, order=range(KT)):
                pe.wait_ge(lo_ready, dyn_u + (u + 1))
                for b in range(2):
                    cols = slice(b * P, (b + 1) * P)
                    products(take(q + b, dyn_q)[:, :],
                             [(k, WH[:, u % 2, k, cols], WL[:, u % 2, k, cols], xh[:, k, :], xl[:, k, :])
                              for k in order], waits if b == 0 else None).then_inc(bank_filled, 1)

            def normed_split(n):
                return (lambda k: pe.wait_ge(h_hi, KT * (n - 1) + k + 1),
                        lambda k: pe.wait_ge(h_lo, KT * (n - 1) + k + 1))

            def mlp(l):
                for k in range(KT):
                    normed_split(2 * l + 1)[1](k)
                with pe.Fori(0, 4) as i:
                    for v in range(4):
                        split_unit(u_mlp[l] + v, q_m1[l] + 2 * v, HH, HL, i * 8, i * 16)
                    hidden = (lambda k: pe.wait_ge(h1_ready, i * 8 + (32 * l + 4 + k + 1)),
                              lambda k: pe.wait_ge(h1_ready, i * 8 + (32 * l + 4 + k + 1)))
                    for v in range(4):
                        split_unit(u_mlp[l] + 4 + v, q_m2[l] + 2 * v, AH, AL, i * 8, i * 16,
                                   hidden if v == 0 else None)

            def projected(l, xh, xl, waits, order):
                for v in range(4):
                    split_unit(u_out[l] + v, q_out[l] + 2 * v, xh, xl, waits=waits if v == 0 else None,
                               order=order)
                norm(2 * l + 1)
                mlp(l)

            mixed = (lambda k: pe.wait_ge(mix_hi, 1 if k >= 4 else 2),
                     lambda k: pe.wait_ge(mix_lo, 1 if k >= 4 else 2))
            projected(0, HH, HL, mixed, [4, 5, 6, 7, 0, 1, 2, 3])

            norm(2)
            split_unit(u_kv, q_k, HH, HL, waits=normed_split(2))
            u = u_kv + 1
            pe.wait_ge(lo_ready, u + 1)
            products(take(q_ik)[:, :], [(k, WH[:, u % 2, k, 0:P], WL[:, u % 2, k, 0:P], HH[:, k, :],
                                         HL[:, k, :]) for k in range(KT)]).then_inc(bank_filled, 1)

            def token_major(o, i, wh, wl):
                rows = slice(i * P, (i + 1) * P)
                return products(o, [(k, HH[:, k, rows], HL[:, k, rows], wh[:, k, :], wl[:, k, :])
                                    for k in range(KT)])

            o = take(q_v)
            for i in range(TT):
                mm = token_major(o[:, i * P:(i + 1) * P], i, WH[:, u % 2, :, P:2 * P], WL[:, u % 2, :, P:2 * P])
            mm.then_inc(bank_filled, 1)
            for v in range(2):
                split_unit(u_iq + v, q_iq + 2 * v, HH, HL)
            o = take(q_iw)
            pe.wait_ge(iw_split, 2)
            for i in range(TT):
                mm = token_major(o[:, NH * i:NH * i + NH], i, IWH, IWL)
            mm.then_inc(bank_filled, 1)

            def mv(v):
                u = u_mv + v
                pe.wait_ge(lo_ready, u + 1)
                for i in range(TT):
                    token_major(take(q_mv[v] + i)[:, 0:UW], i, WH[:, u % 2], WL[:, u % 2])\
                        .then_inc(bank_filled, 1)

            pe.wait_ge(bank_read, q_ik + 1)
            pe.matmul(take(q_ikm)[:, :], HEADS2, L1[:, 20, :], start=True, stop=True).then_inc(bank_filled, 1)
            mv(0)
            pe.wait_ge(n_sq, 1)
            pe.matmul(take(q_ikv)[:, :], HEADS2, SQ1[0][:, 0, :], start=True, stop=True).then_inc(bank_filled, 1)
            mv(1)
            pe.wait_ge(n_used, 1)
            u = 0
            for i in range(1, TT):
                for hh in range(NH):
                    p, j = hh % 2, hh // 2
                    pe.matmul(take(q_idx + u)[:, 0:P * (i + 1)],
                              L1[p * HD:(p + 1) * HD, 16 + j, i * P:(i + 1) * P],
                              L1[p * HD:(p + 1) * HD, 20, 0:P * (i + 1)],
                              start=True, stop=True).then_inc(bank_filled, 1)
                    u += 1
            for v in range(6):
                split_unit(u_dq + v, q_dq + 2 * v, HH, HL)
            for n, (q, tiles) in enumerate(((q_dqn, 4), (q_mqn, 4), (q_mkn, 4), (q_k2n, 2))):
                pe.wait_ge(n_sq, n + 2)
                for t in range(tiles):
                    pe.matmul(take(q + t)[:, :], HEADS2, SQ1[(n + 1) % 2][:, t, :],
                              start=True, stop=True).then_inc(bank_filled, 1)
            pe.wait_ge(n_used, 5)
            pe.wait_ge(bank_read, q_mix)

            with pe.Fori(0, 2) as ty:
                with pe.Fori(0, PAIRS) as j:
                    pair8 = ty * 32 + j * 8
                    pe.wait_ge(at_stage, ty * 4 + j + 1)

                    def scores(u):
                        i, p = u // 2, u % 2
                        pe.wait_ge(at_z, pair8 + (u + 1))
                        pe.matmul(bank[u % 4][:, 0:P * (i + 1)],
                                  QS[p * HD:(p + 1) * HD, i * P:(i + 1) * P],
                                  KS[p * HD:(p + 1) * HD, 0:P * (i + 1)],
                                  start=True, stop=True).then_inc(at_qk, 1)

                    def turned(u):
                        i = u // 2
                        pe.wait_ge(at_p, pair8 + (u + 1))
                        pe.wait_ge(at_pt, pair8 + (u + 1))
                        for s in range(i + 1):
                            mm = pe.transpose(bank[4 + u % 2][:, s * P:(s + 1) * P],
                                              ZB[:, ZSLOT[u], s * P:(s + 1) * P], IDENT)
                        mm.then_inc(at_t, 1)

                    def values(u):
                        i, p = u // 2, u % 2
                        if u == 0:
                            pe.wait_ge(at_on, ty * 4 + j + 1)
                        pe.wait_ge(at_pt, pair8 + (u + 3))
                        for s in range(i + 1):
                            v = VALL[:, s, bass.ds(ty * 512 + j * 128 + p * HD, HD)]
                            mm = pe.matmul(bank[6][:, u * HD:(u + 1) * HD],
                                           PTS[:, u % 2, s * P:(s + 1) * P], v,
                                           start=(s == 0), stop=(s == i))
                        mm.then_inc(at_o, 1)

                    for u in range(4):
                        scores(u)
                    for u in range(8):
                        turned(u)
                        if u + 4 < 8:
                            scores(u + 4)
                        if u >= 1:
                            values(u - 1)
                    values(7)
            pe.wait_ge(at_on, 9)
            for k in range(KT):
                o = bank[(q_mix + k) % 8]
                for i in range(TT):
                    mm = pe.transpose(o[:, i * P:(i + 1) * P], ON[:, i, k * P:(k + 1) * P], IDENT)
                mm.then_inc(bank_filled, 1)
            projected(1, AH, AL, (lambda k: pe.wait_ge(mix_hi, 2 + k + 1),
                                  lambda k: pe.wait_ge(bank_read, q_mix + k + 1)), range(KT))
            pe.wait_ge(bank_read, q_fin)
            for i in range(TT):
                for half_ in range(2):
                    o = take(q_fin + 2 * i + half_)
                    for b in range(4):
                        mm = pe.transpose(o[:, b * P:(b + 1) * P],
                                          XT[:, half_ * 4 + b, i * P:(i + 1) * P], IDENT)
                    mm.then_inc(bank_filled, 1)

        @block.scalar
        def _(act):
            t = Tally(act, act_step)

            def filled(q, dyn=0):
                act.wait_ge(bank_filled, dyn + (q + 1))

            def src(q):
                return bank[q % 8]

            def rows(dst, vec):
                act.dma_start(dst, vec).then_inc(dma_par, 16)

            rows(PR[0:16, :], a["norm1_g"].rearrange("l (c p) -> (l c) p", p=P))
            rows(PR[16:32, :], a["norm2_g"].rearrange("l (c p) -> (l c) p", p=P))
            r = 32
            for name in ("rwkv_mu", "rwkv_w0", "rwkv_a0", "rwkv_k_k", "rwkv_k_a", "rwkv_r_k",
                         "rwkv_lnx_w", "rwkv_lnx_b"):
                v = a[name]
                v = v.rearrange("o (c a) n -> (o c) (a n)", a=2) if name == "rwkv_r_k" else \
                    v.rearrange("o (c p) -> (o c) p", p=P)
                rows(PR[r:r + v.shape[0], :], v)
                r += v.shape[0]
            rows(PR[74:122, :], a["gdn_conv_w"][0].rearrange("j (b p) -> (j b) p", p=P))
            for i, name in enumerate(PAR64):
                for half in range(2):
                    rows(PR2[i:i + 1, half * HD:(half + 1) * HD], a[name])
            rows(ALOG, a["gdn_a_log"].broadcast_to([P, NH]))
            rows(DTB, a["gdn_dt_bias"].broadcast_to([P, NH]))
            rows(LW2[0:HD, :], a["rwkv_w2"][0])
            rows(LW2[HD:P, :], a["rwkv_a2"][0])
            rows(G2, a["rwkv_g2"][0])
            rows(IWW, kmaj(od[:, OD_IW:OD_IW + NH]))

            def norm(n, ready, between=lambda k: None):
                for k in range(KT):
                    act.wait_ge(bank_read, ready + k + 1)
                    act.activation(SQ[n][:, k, :], XT[:, k, :], ACT.Square).then_inc(squares, 1)
                    between(k)
                filled(q_norm[n])
                act.activation(RS[n], src(q_norm[n])[:, :], ACT.Ln, bias=RMS_EPS, scale=1.0 / D)\
                   .then_inc(bank_read, 1)
                act.wait_ge(bank_read, q_norm[n] + 1)
                act.activation(RS[n], RS[n], ACT.Exp, scale=-0.5).then_inc(rms, 1)

            def weight_hi(u, dyn=0, q_done=None, dyn_q=0):
                act.wait_ge(raw_full[u % 2], dyn + raw_count(u))
                if q_done is not None:
                    filled(q_done, dyn_q)
                act.activation(WH[:, u % 2], RAW[:, u % 2], ACT.Copy).then_inc(hi_ready, 1)

            def h_split(n):
                for k in range(KT):
                    act.wait_ge(h_ready, KT * n + k + 1)
                    act.activation(HH[:, k, :], SQ[n][:, k, :], ACT.Copy).then_inc(h_hi, 1)

            norm(0, q_x)

            act.wait_ge(pads_zero, 1)
            for b in range(2):
                filled(q_lora + b)
                act.activation(STAGE[0][:, b, 3:3 + W], src(q_lora + b)[:, :], ACT.Copy)\
                   .then_inc(bank_read, 1)
            filled(q_ab)
            act.activation(wide(AB), src(q_ab)[:, 0:64], ACT.Copy).then_inc(bank_read, 1)
            for b in range(4):
                filled(q_z + b)
                act.activation(Z[:, b, :], src(q_z + b)[:, :], ACT.Silu).then_inc(bank_read, 1)
            act.wait_ge(lora_shifted, 2)
            act.activation(WA[0:HD, :], WA[0:HD, :], ACT.Tanh).then_inc(lora_act, 1)
            act.activation(GD, GD, ACT.Sigmoid).then_inc(lora_act, 1)
            act.wait_ge(bank_read, q_ab + 1)
            act.activation(BETA, AB[:, :, 0:NH], ACT.Sigmoid)
            for c in range(4):
                filled(q_w + c)
                act.activation(BON[:, c, :], src(q_w + c)[:, :], ACT.Sigmoid, bias=pc("w0", c))\
                   .then_inc(bank_read, 1)
            for c in range(4):
                filled(q_a + c)
                act.activation(B[:, c, :], src(q_a + c)[:, :], ACT.Sigmoid, bias=pc("a0", c))\
                   .then_inc(bank_read, 1)
            for c in range(4):
                filled(q_g + c)
                act.activation(G[:, c, :], src(q_g + c)[:, :], ACT.Copy).then_inc(bank_read, 1)

            with act.Fori(0, 3) as i:
                for s in range(2):
                    for b in range(4):
                        filled(q_pair + 4 * s + b, i * 8)
                        if s == 0:
                            act.wait_ge(stage_used, i * 4 + (b + 1))
                        act.activation(STAGE[s][:, b, 3:3 + W], src(q_pair + 4 * s + b)[:, :],
                                       ACT.Copy).then_inc(bank_read, 1)
                for b in range(4):
                    act.wait_ge(conv_out, i * 4 + (b + 1))
                    act.activation(GQKV[:, bass.ds(i * 4 + b, 1), :].rearrange("p a w -> p (a w)"),
                                   CONV[:, b, :], ACT.Silu).then_inc(conv_used, 1)

            act.wait_ge(gate_in, 1)
            t.link(act.activation(wide(GLOG), wide(GTMP), ACT.Abs))
            t.link(act.activation(wide(GLOG), wide(GLOG), ACT.Exp, scale=-1.0))
            act.activation(NEA, ALOG, ACT.Exp)
            act.activation(wide(GLOG), wide(GLOG), ACT.Ln, bias=1.0).then_inc(gate_ln, 1)
            act.wait_ge(conv_used, 4 + 12)
            act.wait_ge(stage_used, 4 + 12)
            for n, (q, x, sq) in enumerate(((q_kk, KK, SQA), (q_gq, GQ, SQB), (q_gk, GK, SQA))):
                if n == 0:
                    act.wait_ge(kk_ready, 4)
                if n == 2:
                    act.wait_ge(bank_filled, q_kk + 4)
                act.activation(wide(sq), wide(x), ACT.Square).then_inc(sq_grp, 1)
                if n > 0:
                    act.wait_ge(rs_used, n)
                for c in range(4):
                    filled(q + c)
                    act.activation(RSB[:, c, :], src(q + c)[:, :], ACT.Ln, bias=1e-6)\
                       .then_inc(bank_read, 1)
                act.wait_ge(bank_read, q + 4)
                act.activation(wide(RSB), wide(RSB), ACT.Exp, scale=-0.5).then_inc(rs_grp, 1)
            act.wait_ge(gcum_ready, 1)
            act.activation(wide(EG), wide(GCUM), ACT.Exp)
            act.activation(wide(EREST), wide(EREST), ACT.Exp)
            for p in range(2):
                part = slice(p * HD, (p + 1) * HD)
                last = act.activation(
                    ESTATE[part, :, :],
                    src(q_cum)[part, 32:64].rearrange("p (c j q) -> p c j q", c=TT, q=2)[:, :, :, p],
                    ACT.Exp)
            last.then_inc(l0_act, 1)

            act.wait_ge(l0_dve, 1)
            with act.Fori(0, TT) as c:
                n = c + 1
                act.wait_ge(f_vg, n)
                act.activation(VG, bank[3][:, :], ACT.Copy).then_inc(r_vg, 1)
                act.wait_ge(f_vr, n)
                act.activation(VR, bank[4][:, :], ACT.Copy).then_inc(r_vr, 1)
                act.wait_ge(e_diff, n)
                act.activation(wide(KD), wide(RD), ACT.Exp, scale=-1.0)
                with t.loop(c, 1, TT):
                    t.link(act.activation(wide(BD), wide(RD), ACT.Exp, scale=-1.0))
                act.activation(wide(RD), wide(RD), ACT.Exp)
                act.activation(wide(AD), wide(AD), ACT.Exp)
                act.activation(ESM, SM, ACT.Exp).then_inc(e_exp, 1)
                act.wait_ge(e_dsub, n)
                for p in range(2):
                    last = act.activation(wide(DT[p]), wide(DT[p]), ACT.Exp)
                last.then_inc(e_dt, 1)
                act.wait_ge(f_lt, n)
                for p in range(2):
                    last = act.activation(wide(LT[p]), bank[3 + p][:, :], ACT.Copy)
                last.then_inc(r_lt, 1)
                act.wait_ge(f_ktok, n)
                act.activation(KTOK, bank[3][:, :], ACT.Copy).then_inc(r_ktok, 1)
                act.wait_ge(f_btok, n)
                act.activation(BTOK, bank[4][:, :], ACT.Copy).then_inc(r_btok, 1)
                act.wait_ge(f_x1, n)
                act.activation(X1R, bank[0][:, :], ACT.Copy).then_inc(r_x1, 1)
                with act.Fori(0, LEVELS - 1) as lev:
                    for g in range(4):
                        act.wait_ge(inv_turned, c * MERGES + (lev * 4 + (g + 1)))
                        act.activation(wide(QI[g]), bank[2 * g + 1][:, :], ACT.Copy).then_inc(inv_q, 1)
                act.wait_ge(f_u1, n)
                act.activation(X1R[0:HD, :], bank[0][0:HD, :], ACT.Copy).then_inc(r_u1, 1)
                act.wait_ge(f_zr, n)
                act.activation(X1R[HD:P, :], bank[5][HD:P, :], ACT.Copy, scale=-1.0).then_inc(r_zr, 1)
                act.wait_ge(f_u, n)
                act.activation(UN, bank[0][:, :], ACT.Copy, scale=-1.0).then_inc(r_u, 1)
                for g, eps in ((0, GN_EPS), (1, RMS_EPS)):
                    cols = slice(g * NH, (g + 1) * NH)
                    act.wait_ge(e_var, 2 * c + (g + 1))
                    act.activation(RSTD[:, cols], VAR[:, cols], ACT.Ln, bias=eps, scale=1.0 / HD)\
                       .then_inc(e_ln, 1)
                    act.wait_ge(e_ln, 2 * c + (g + 1))
                    act.activation(RSTD[:, cols], RSTD[:, cols], ACT.Exp, scale=-0.5)\
                       .then_inc(e_rstd, 1)
                here = bass.ds(c * P, P)
                act.wait_ge(f_tr, n)
                act.activation(R[:, :, here], bank[7][:, :].rearrange("p (j t) -> p j t", j=4),
                               ACT.Copy).then_inc(r_tr, 1)
                act.wait_ge(f_tg, n)
                act.activation(GQ[:, :, here], bank[0][:, :].rearrange("p (j t) -> p j t", j=4),
                               ACT.Copy).then_inc(r_tg, 1)

            def norm_and_weights(l, n):
                def between(k):
                    if k % 2 == 1:
                        weight_hi(u_out[l] + k // 2 + 2, q_done=q_out[l] + k)

                norm(n, q_out[l], between)
                h_split(n)

            def mlp(l):
                def quarter(i, units):
                    for v in range(8):
                        if v < 4:
                            for b in (2 * v, 2 * v + 1):
                                if b == 0:
                                    act.wait_ge(bank_read, i * 16 + q_m1[l])
                                filled(q_m1[l] + b, i * 16)
                                act.wait_ge(h1_ready, i * 8 + (32 * l + b + 1))
                                act.activation(SQT[:, b % 4, :], src(q_m1[l] + b)[:, :], ACT.Relu)\
                                   .then_inc(bank_read, 1)
                        if v < units:
                            weight_hi(u_mlp[l] + 2 + v, i * 64, q_m1[l] + 2 * v + 1, i * 16)

                with act.Fori(0, 3) as i:
                    quarter(i, 8)
                quarter(3, 6)

            act.wait_ge(e_state, TT)
            weight_hi(0)
            weight_hi(1)
            act.wait_ge(mix_ready, 1)
            act.activation(HH[:, 4:8, :], GQ, ACT.Copy).then_inc(mix_hi, 1)
            act.wait_ge(mix_ready, 2)
            act.activation(HH[:, 0:4, :], R, ACT.Copy).then_inc(mix_hi, 1)
            norm_and_weights(0, 1)
            act.activation(IWH, IWW, ACT.Copy).then_inc(iw_split, 1)
            mlp(0)
            norm(2, q_norm[2] - 8,
                 lambda k: weight_hi(u_kv + (k - 5) // 2, q_done=q_norm[2] - 8 + k) if k in (5, 7) else None)
            h_split(2)

            for q, tile in ((q_k, 8), (q_k + 1, 10), (q_ik, 20)):
                filled(q)
                act.activation(L1[:, tile, :], src(q)[:, :], ACT.Copy).then_inc(bank_read, 1)
                if q == q_k + 1:
                    weight_hi(u_iq, q_done=q)
            filled(q_v)
            for g in range(2):
                vin = src(q_v)[:, :].rearrange("p (s v) -> p s v", s=4)[:, :, g * HD:(g + 1) * HD]
                for rep in range(4):
                    cc = (4 * g + rep) * HD
                    last = act.activation(VALL[:, :, cc:cc + HD], vin, ACT.Copy)
            last.then_inc(bank_read, 1)
            weight_hi(u_iq + 1, q_done=q_v)

            def evacuate(q, tile):
                filled(q)
                act.activation(L1[:, tile, :], src(q)[:, :], ACT.Copy).then_inc(bank_read, 1)

            for v in range(2):
                for b in range(2):
                    evacuate(q_iq + 2 * v + b, 16 + 2 * v + b)
                weight_hi(u_mv + v, q_done=q_iq + 2 * v + 1)
            filled(q_iw)
            act.activation(wide(IW), src(q_iw)[:, 0:TT * NH], ACT.Copy, scale=float(NH) ** -0.5)\
               .then_inc(bank_read, 1)
            act.wait_ge(ik_centred, 1)
            act.activation(SQ1[0][:, 0, :], L1[:, 20, :], ACT.Square).then_inc(n_sq, 1)

            def mv(v):
                act.wait_ge(bank_read, q_mv[v])
                for i in range(TT):
                    filled(q_mv[v] + i)
                    act.activation(VALL[:, i, 512 + v * UW:512 + (v + 1) * UW],
                                   src(q_mv[v] + i)[:, 0:UW], ACT.Copy).then_inc(bank_read, 1)
                weight_hi(u_dq + v, q_done=q_mv[v] + 3)

            def inverse_rms(q, tiles):
                for c in range(tiles):
                    filled(q + c)
                    act.activation(RS1[:, c, :], src(q + c)[:, :], ACT.Ln, bias=RMS_EPS,
                                   scale=1.0 / HD).then_inc(bank_read, 1)
                act.wait_ge(bank_read, q + tiles)
                act.activation(RS1[:, 0:tiles, :], RS1[:, 0:tiles, :], ACT.Exp, scale=-0.5)\
                   .then_inc(n_rs, 1)

            mv(0)
            inverse_rms(q_ikv, 1)
            mv(1)
            u = 0
            for i in range(1, TT):
                for hh in range(NH):
                    filled(q_idx + u)
                    if u >= 4:
                        act.wait_ge(idx_acc, u - 3)
                    act.activation(RT[:, u % 4, 0:P * (i + 1)], src(q_idx + u)[:, 0:P * (i + 1)],
                                   ACT.Relu, scale=float(HD) ** -0.5).then_inc(bank_read, 1)
                    u += 1
            for v in range(6):
                for b in range(2):
                    evacuate(q_dq + 2 * v + b, (0, 4, 12)[v // 2] + 2 * (v % 2) + b)
                weight_hi(u_dq + 2 + v, q_done=q_dq + 2 * v + 1)
            act.wait_ge(bank_read, q_dqn)
            act.wait_ge(idx_acc, u)
            act.wait_ge(bias_ready, 1)
            for n, (q, tiles, x) in enumerate(((q_dqn, 4, L1[:, 0:4, :]), (q_mqn, 4, L1[:, 4:8, :]),
                                               (q_mkn, 4, L1[:, 12:16, :]), (q_k2n, 2, L1[:, 8:12:2, :])), 1):
                if n >= 2:
                    act.wait_ge(bank_filled, q_prev)
                act.activation(SQ1[n % 2][:, 0:tiles, :], x, ACT.Square).then_inc(n_sq, 1)
                act.wait_ge(n_used, n)
                q_prev = q
                inverse_rms(q, tiles)

            act.wait_ge(n_used, 5)
            act.sem_inc(at_pt, 2)
            with act.Fori(0, 2) as ty:
                with act.Fori(0, PAIRS) as j:
                    pair8 = ty * 32 + j * 8

                    def probs(u):
                        wdt = P * (u // 2 + 1)
                        act.wait_ge(at_mx, pair8 + (u + 1))
                        if u == 0:
                            act.wait_ge(at_on, ty * 4 + j + 1)
                        act.activation(ZB[:, ZSLOT[u], 0:wdt], ZB[:, ZSLOT[u], 0:wdt], ACT.Exp,
                                       bias=NMX[:, u:u + 1], accum_out=RSUM[:, u:u + 1])\
                           .then_inc(at_p, 1)

                    def out_turned(u):
                        wdt = P * (u // 2 + 1)
                        act.wait_ge(at_t, pair8 + (u + 1))
                        if u >= 2:
                            act.wait_ge(at_o, pair8 + (u - 1))
                        act.activation(PTS[:, u % 2, 0:wdt], bank[4 + u % 2][:, 0:wdt], ACT.Copy)\
                           .then_inc(at_pt, 1)

                    for u in range(8):
                        probs(u)
                        if u >= 1:
                            out_turned(u - 1)
                    out_turned(7)
            for k in range(KT):
                filled(q_mix + k)
                act.activation(AH[:, k, :], src(q_mix + k)[:, :], ACT.Copy).then_inc(mix_hi, 1)
            norm_and_weights(1, 3)
            mlp(1)
            for i in range(2 * TT):
                filled(q_fin + i)
                act.activation(OUTT[:, i // 2, (i % 2) * 512:(i % 2 + 1) * 512],
                               src(q_fin + i)[:, :], ACT.Copy).then_inc(bank_read, 1)

        @block.vector
        def _(dve):
            t = Tally(dve, dve_step)
            mul, add, sub = ALU.mult, ALU.add, ALU.subtract

            def filled(q, dyn=0):
                dve.wait_ge(bank_filled, dyn + (q + 1))

            def src(q):
                return bank[q % 8]

            dve.sem_inc(stage_used, 4)
            dve.sem_inc(h1_ready, 4)
            filled(0)
            dve.tensor_copy(PC[:, 0:NPC], bank[0][:, 0:NPC]).then_inc(bank_read, 1)
            filled(1)
            dve.tensor_copy(PC2[:, 0:7], bank[1][:, 0:7]).then_inc(bank_read, 1)
            dve.wait_ge(bank_read, 2)
            dve.tensor_scalar(OMKA, PC[:, at["k_a"]:at["k_a"] + 4], -1.0, 1.0, mul, add)
            for i, col in enumerate((DQN, MQN)):
                dve.tensor_scalar(QW[:, i:i + 1], pc2(col), float(HD) ** -0.5, None, mul)
            for k in range(KT):
                filled(q_x + k)
                dve.tensor_copy(XT[:, k, :], src(q_x + k)[:, :]).then_inc(bank_read, 1)

            def norm(n):
                dst = HT if n == 0 else SQ[n]
                dve.wait_ge(rms, n + 1)
                for k in range(KT):
                    g = pc("norm1" if n % 2 == 0 else "norm2", (n // 2) * KT + k)
                    dve.scalar_tensor_tensor(out=dst[:, k, :], in0=XT[:, k, :], scalar=g, in1=RS[n],
                                             op0=mul, op1=mul).then_inc(h_ready, 1)
                if n > 0:
                    for k in range(KT):
                        dve.wait_ge(h_hi, KT * (n - 1) + k + 1)
                        dve.tensor_tensor(HL[:, k, :], dst[:, k, :], as_f32(HH[:, k, :]), sub)\
                           .then_inc(h_lo, 1)

            norm(0)

            def shifted(dst, stage, mu):
                t.link(dve.tensor_tensor(TMPD, stage[:, 2:2 + W], stage[:, 3:3 + W], sub))
                return dve.scalar_tensor_tensor(out=dst, in0=TMPD, scalar=mu, in1=stage[:, 3:3 + W],
                                                op0=mul, op1=add)

            for b, dst in enumerate((WA, GD)):
                dve.wait_ge(bank_read, q_lora + b + 1)
                shifted(dst, STAGE[0][:, b, :], pc("mu", 12 + b)).then_inc(lora_shifted, 1)
                dve.wait_ge(lora_shifted, b + 1)
            dve.sem_inc(conv_used, 4)
            dve.wait_ge(bank_read, q_ab + 1)
            dve.tensor_tensor(GTMP, AB[:, :, NH:2 * NH], DTB.unsqueeze(1).broadcast_to([P, TT, NH]),
                              add).then_inc(gate_in, 1)
            t.link(dve.memset(CUM[:, :, :, 0:1].rearrange("p c k o -> p (c k) o"), 0.0))
            for c in range(4):
                dve.wait_ge(bank_read, q_w + c + 1)
                t.link(dve.tensor_scalar(CUM[:, c, :, 1:CW],
                                         BON[:, c, :].rearrange("p (k t) -> p k t", k=4),
                                         -float(np.exp(-0.5)), None, mul))
                cum = CUM[:, c, :, :].rearrange("p k t -> p (k t)")
                t.link(dve.tensor_tensor_scan(cum, SCANM, cum, 0.0, mul, add))

            with dve.Fori(0, 3) as i:
                with t.loop(i, 4 + 12, 3):
                    for b in range(4):
                        dve.wait_ge(bank_read, i * 8 + (q_pair + b + 1))
                        mu = PC[:, bass.ds(i * 4 + (at["mu"] + b), 1)]
                        dst = RKV[:, bass.ds(i * 4 + b, 1), :].rearrange("p a w -> p (a w)")
                        shifted(dst, STAGE[0][:, b, :], mu).then_inc(stage_used, 1)
                        dve.wait_ge(stage_used, i * 4 + (4 + b + 1))
                    for b in range(4):
                        dve.wait_ge(bank_read, i * 8 + (q_pair + 4 + b + 1))
                        dve.wait_ge(conv_used, i * 4 + (b + 1))
                        for tap in range(4):
                            wgt = PC[:, bass.ds(i * 4 + (at["conv"] + 12 * tap + b), 1)]
                            x = STAGE[1][:, b, tap:tap + W]
                            if tap == 0:
                                ins = dve.tensor_scalar(CONV[:, b, :], x, wgt, None, mul)
                            else:
                                ins = dve.scalar_tensor_tensor(out=CONV[:, b, :], in0=x, scalar=wgt,
                                                               in1=CONV[:, b, :], op0=mul, op1=add)
                            if tap < 3:
                                t.link(ins)
                            else:
                                ins.then_inc(conv_out, 1)
                        dve.wait_ge(conv_out, i * 4 + (b + 1))
            for c in range(4):
                dve.tensor_scalar(KK[:, c, :], K[:, c, :], pc("k_k", c), None, mul).then_inc(kk_ready, 1)
            dve.wait_ge(kk_ready, 4)
            for c in range(4):
                t.link(dve.tensor_scalar(TMPD, B[:, c, :], pc("k_a", c), OMKA[:, c:c + 1], mul, add))
                t.link(dve.tensor_tensor(K[:, c, :], K[:, c, :], TMPD, mul))
            dve.wait_ge(gate_ln, 1)
            t.link(dve.scalar_tensor_tensor(out=wide(GTMP), in0=wide(GTMP), scalar=0.0, in1=wide(GLOG),
                                            op0=ALU.max, op1=add))
            dve.scalar_tensor_tensor(out=GLOG, in0=GTMP, scalar=-1.0,
                                     in1=NEA.unsqueeze(1).broadcast_to([P, TT, NH]),
                                     op0=mul, op1=mul).then_inc(glog_ready, 1)
            dve.wait_ge(rs_grp, 1)
            dve.tensor_tensor(wide(KK), wide(KK), wide(RSB), mul).then_inc(rs_used, 1)
            dve.wait_ge(rs_used, 1)
            t.link(dve.tensor_tensor(wide(B), wide(KK), wide(B), mul))
            dve.wait_ge(rs_grp, 2)
            dve.scalar_tensor_tensor(out=wide(GQ), in0=wide(GQ), scalar=float(HD) ** -0.5,
                                     in1=wide(RSB), op0=mul, op1=mul).then_inc(rs_used, 1)
            dve.wait_ge(bank_filled, q_gq + 4)
            for c in range(4):
                dve.scalar_tensor_tensor(out=SQB[:, c, :], in0=R[:, c, :], scalar=pc("r_k", c),
                                         in1=K[:, c, :], op0=mul, op1=mul).then_inc(bonus_in, 1)
            dve.wait_ge(rs_grp, 3)
            dve.tensor_tensor(wide(GK), wide(GK), wide(RSB), mul).then_inc(rs_used, 1)
            for c in range(4):
                filled(q_bon + c)
                dve.tensor_tensor(BON[:, c, :], src(q_bon + c)[:, :], V[:, c, :], mul)\
                   .then_inc(bank_read, 1)
            filled(q_cum)
            t.link(dve.tensor_copy(wide(GCUM), src(q_cum)[:, 0:32]))
            dve.tensor_tensor(wide(EREST), src(q_cum)[:, 32:64], wide(GCUM), sub).then_inc(gcum_ready, 1)
            dve.wait_ge(l0_act, 1)
            dve.wait_ge(gcum_ready, 1)
            dve.wait_ge(rs_used, 3)
            dve.tensor_copy(VAR[:, 0:1], PC[:, 0:1]).then_inc(l0_dve, 1)
            dve.sem_inc(bank_read, 1)

            def bc(x, n=P):
                return x.unsqueeze(2).broadcast_to([P, x.shape[1], n])

            def by_parity(x, p):
                return x.rearrange("p o (j q) -> p (o j) q", q=2)[:, :, p]

            def bank4(b):
                return bank[b][:, :].rearrange("p (j t) -> p j t", j=4)

            def heads(x):
                return x.rearrange("p (h d) -> p h d", h=NH)

            def mask4(m):
                return m.unsqueeze(1).broadcast_to([P, 4, P])

            dve.wait_ge(l0_dve, 1)
            with dve.Fori(0, TT) as c:
                n = c + 1
                here = bass.ds(c * P, P)
                row = bass.ds(c, 1)

                def row_of(x):
                    return x[:, row, :].rearrange("p a h -> p (a h)")

                with t.loop(c, DVE_CHUNK, TT):
                    mid = CUM[:, :, row, P // 2:P // 2 + 1].rearrange("p c k o -> p c (k o)")
                    chunk_cum = CUM[:, :, row, :].rearrange("p c k t -> p c (k t)")
                    midb = mid.broadcast_to([P, 4, P])
                    t.link(dve.tensor_tensor(RD, chunk_cum[:, :, 1:CW], midb, sub))
                    dve.tensor_tensor(AD, chunk_cum[:, :, 0:P], midb, sub)
                    dve.tensor_copy(SM[:, 0:4].unsqueeze(2), mid)
                    dve.tensor_copy(SM[:, 4:8].unsqueeze(2), RD[:, :, P - 1:P]).then_inc(e_diff, 1)
                    dve.wait_ge(f_grow, n)
                    for p in range(2):
                        gs = by_parity(GCUM[:, row, :], p)
                        t.step(dve.tensor_tensor(DT[p], bank4(p), bc(gs), sub))
                    t.settle()
                    for p in range(2):
                        ins = dve.tensor_scalar(wide(DT[p]), wide(DT[p]), 0.0, None, ALU.min)
                    ins.then_inc(e_dsub, 1)
                    dve.wait_ge(f_kt, n)
                    dve.tensor_tensor(heads(KGT), heads(bank[2][:, :]), bc(row_of(EREST), HD), mul)\
                       .then_inc(r_kt, 1)
                    dve.wait_ge(e_exp, n)
                    dve.tensor_tensor(RD, RD, R[:, :, here], mul)
                    dve.tensor_tensor(KD, KD, K[:, :, here], mul).then_inc(e_rk, 1)
                    dve.tensor_tensor(SR, SR, bc(ESM[:, 0:4]), mul).then_inc(e_s0, 1)
                    dve.wait_ge(e_dmask, n)
                    dve.wait_ge(f_kk, n)
                    for p in range(2):
                        ins = dve.tensor_tensor(LT[2 + p], bank4(5 + p), LT[2 + p], mul)
                    ins.then_inc(r_kk, 1)
                    dve.wait_ge(f_kq, n)
                    for p in range(2):
                        ins = dve.tensor_tensor(GRK[p], bank4((7, 2)[p]), GRK[p], mul)
                    ins.then_inc(r_kq, 1)
                    for f, dst, banks, m, r_ in ((f_mk, MK, (0, 1), STRICT, r_mk),
                                                 (f_rk, RK, (5, 6), INCL, r_rk),
                                                 (f_rb, RBM, (7, 2), INCL, r_rb)):
                        dve.wait_ge(f, n)
                        for p in range(2):
                            ins = dve.tensor_tensor(dst[p], bank4(banks[p]), mask4(m), mul)
                        ins.then_inc(r_, 1)
                    dve.wait_ge(f_ks, n)
                    dve.wait_ge(r_vg, n)
                    t.link(dve.tensor_tensor(heads(TMPK), heads(bank[1][:, :]), bc(row_of(EG), HD), mul))
                    dve.tensor_tensor(VG, VG, TMPK, sub).then_inc(r_ks, 1)
                    for g in range(4):
                        dve.wait_ge(inv_first, c * 4 + (g + 1))
                        dve.tensor_copy(TI[g], bank4(2 * g)).then_inc(inv_t, 1)
                    with dve.Fori(0, LEVELS - 1) as lev:
                        for g in range(4):
                            dve.wait_ge(inv_x, c * MERGES + (lev * 4 + (g + 1)))
                            m = MERGE[:, bass.ds(lev + 1, 1), :].broadcast_to([P, 4, P])
                            dve.tensor_tensor(XM[g], bank4(2 * g), m, mul).then_inc(inv_xs, 1)
                        for g in range(4):
                            dve.wait_ge(inv_y, c * MERGES + (lev * 4 + (g + 1)))
                            dve.tensor_tensor(TI[g], TI[g], bank4(2 * g), sub).then_inc(inv_t, 1)
                    dve.wait_ge(f_y1, n)
                    dve.tensor_copy(VG[0:HD, :], bank[1][0:HD, :]).then_inc(r_y1, 1)
                    dve.wait_ge(f_zg, n)
                    dve.tensor_scalar(VG[HD:P, :], bank[6][HD:P, :], -1.0, None, mul).then_inc(r_zg, 1)
                    dve.wait_ge(f_y, n)
                    dve.tensor_tensor(heads(VN), heads(bank[1][:, :]), bc(row_of(BETA), HD), mul)\
                       .then_inc(r_y, 1)
                    dve.wait_ge(f_or, n)
                    o_r = heads(bank[2][:, :])
                    t.link(dve.tensor_reduce(NMEAN, o_r, AX.X, add, negate=True))
                    t.link(dve.tensor_scalar(NMEAN, NMEAN, 1.0 / HD, None, mul))
                    t.link(dve.tensor_tensor(heads(OR), o_r, bc(NMEAN, HD), add))
                    t.link(dve.tensor_tensor(OSQ, OR, OR, mul))
                    dve.tensor_reduce(VAR[:, 0:NH], heads(OSQ), AX.X, add).then_inc(e_var, 1)
                    dve.wait_ge(f_og, n)
                    dve.wait_ge(f_qs, n)
                    t.link(dve.tensor_tensor(heads(TMPG), heads(bank[4][:, :]), bc(row_of(EG), HD), mul))
                    t.link(dve.tensor_tensor(OG, TMPG, bank[3][:, :], add))
                    t.link(dve.tensor_tensor(OSQG, OG, OG, mul))
                    dve.tensor_reduce(VAR[:, NH:2 * NH], heads(OSQG), AX.X, add).then_inc(e_var, 1)
                    dve.wait_ge(e_rstd, 2 * c + 1)
                    dve.tensor_tensor(heads(OR), heads(OR), bc(RSTD[:, 0:NH], HD), mul).then_inc(e_on, 1)
                    dve.wait_ge(e_rstd, 2 * c + 2)
                    dve.tensor_tensor(heads(OG), heads(OG), bc(RSTD[:, NH:2 * NH], HD), mul).then_inc(e_og, 1)
                    dve.wait_ge(f_sr, n)
                    t.link(dve.tensor_tensor(TMPS, bank4(5), mask4(HEADS2), mul))
                    t.link(dve.tensor_tensor(SR, SR, TMPS, add))
                    t.link(dve.tensor_tensor(SR, SR, bc(ESM[:, 4:8]), mul))
                    dve.wait_ge(f_sg, n)
                    t.link(dve.tensor_tensor(TMPS, bank4(6), mask4(HEADS2), mul))
                    t.link(dve.tensor_tensor(SG, SG, bc(row_of(ESTATE)), mul))
                    dve.tensor_tensor(SG, SG, TMPS, add).then_inc(e_state, 1)
                    dve.wait_ge(e_state, n)
                    dve.wait_ge(f_tg, n)
            dve.wait_ge(r_tg, TT)
            dve.scalar_tensor_tensor(out=wide(GQ), in0=wide(GQ), scalar=pc2(GDNN), in1=wide(Z),
                                     op0=mul, op1=mul).then_inc(mix_ready, 1)
            for j in range(4):
                t.step(dve.tensor_scalar(R[:, j, :], R[:, j, :], pc("lnx_w", j), pc("lnx_b", j), mul, add))
            t.settle()
            t.link(dve.tensor_tensor(wide(R), wide(R), wide(BON), add))
            dve.tensor_tensor(wide(R), wide(R), wide(G), mul).then_inc(mix_ready, 1)
            dve.wait_ge(mix_lo, 1)
            dve.wait_ge(mix_hi, 2)
            dve.tensor_tensor(HL[:, 0:4, :], R, as_f32(HH[:, 0:4, :]), sub).then_inc(mix_lo, 1)

            def residual(q):
                for k in range(KT):
                    filled(q + k)
                    dve.tensor_tensor(XT[:, k, :], XT[:, k, :], src(q + k)[:, :], add).then_inc(bank_read, 1)

            def mlp(l):
                with dve.Fori(0, 4) as i, t.loop(i, 16, 4):
                    for b in range(8):
                        dve.wait_ge(bank_read, i * 16 + (q_m1[l] + b + 1))
                        sq = SQT[:, b % 4, :]
                        t.link(dve.tensor_tensor(sq, sq, sq, mul))
                        t.link(dve.tensor_copy(AH[:, b, :], sq))
                        dve.tensor_tensor(AL[:, b, :], sq, as_f32(AH[:, b, :]), sub).then_inc(h1_ready, 1)
                    for k in range(KT):
                        filled(q_m2[l] + k, i * 16)
                        dve.tensor_tensor(XT[:, k, :], XT[:, k, :], src(q_m2[l] + k)[:, :], add)\
                           .then_inc(bank_read, 1)

            residual(q_out[0])
            norm(1)
            mlp(0)
            norm(2)

            IK = L1[:, 20, :]
            filled(q_ikm)
            dve.wait_ge(bank_read, q_ikm)
            dve.scalar_tensor_tensor(out=IK, in0=src(q_ikm)[:, :], scalar=-1.0 / HD, in1=IK,
                                     op0=mul, op1=add).then_inc(ik_centred, 1)
            dve.wait_ge(ik_centred, 1)
            dve.sem_inc(bank_read, 1)
            dve.wait_ge(n_rs, 1)
            t.link(dve.scalar_tensor_tensor(out=IK, in0=IK, scalar=pc2(LNW), in1=RS1[:, 0, :],
                                            op0=mul, op1=mul))
            dve.tensor_scalar(IK, IK, pc2(LNB), None, add).then_inc(n_used, 1)
            u = 0
            for i in range(1, TT):
                for hh in range(NH):
                    wdt = P * (i + 1)
                    dve.wait_ge(bank_read, q_idx + u + 1)
                    wgt = IW[:, i, hh:hh + 1]
                    s = SCORE[:, i - 1, 0:wdt]
                    if hh == 0:
                        dve.tensor_scalar(s, RT[:, u % 4, 0:wdt], wgt, None, mul).then_inc(idx_acc, 1)
                    else:
                        dve.scalar_tensor_tensor(out=s, in0=RT[:, u % 4, 0:wdt], scalar=wgt, in1=s,
                                                 op0=mul, op1=add).then_inc(idx_acc, 1)
                    u += 1
                    dve.wait_ge(idx_acc, u)
            rounds = TOPK // 8
            scores = [SCORE[:, i - 1, 0:P * (i + 1)] for i in range(1, TT)]
            dve.wait_ge(idx_masked, TT - 1)
            with dve.Fori(0, rounds) as r:
                with t.loop(r, 2 * (TT - 1), rounds):
                    for i, sc in enumerate(scores):
                        t.step(dve.max(M8[:, i, :], sc))
                    t.settle()
                    dve.sem_inc(topk_rounds, 1)
                    for i, sc in enumerate(scores):
                        t.step(dve.match_replace(sc, M8[:, i, :], sc, TAKEN))
                    t.settle()
            dve.wait_ge(dist_ready, 1)
            for i in range(TT):
                wdt = P * (i + 1)
                d = DIST[:, W - wdt:W]
                lo = bias_off(i)
                t.step(dve.tensor_copy(BIAS[:, 1, lo:lo + wdt], d))
                if i == 0:
                    t.step(dve.tensor_copy(BIAS[:, 0, lo:lo + wdt], d))
                else:
                    s = SCORE[:, i - 1, 0:wdt]
                    t.link(dve.tensor_scalar(s, s, 0.5 * (CAUSAL_FILL + TAKEN), FAR, ALU.is_gt, mul))
                    t.step(dve.tensor_tensor(BIAS[:, 0, lo:lo + wdt], s, d, ALU.max))
            t.settle()
            dve.tensor_copy(NMX[:, 1:2], pc2(0)).then_inc(bias_ready, 1)

            for n, (lo, wgt) in enumerate(((0, QW[:, 0:1]), (4, QW[:, 1:2]), (12, pc2(MKN)))):
                dve.wait_ge(n_rs, n + 2)
                dve.scalar_tensor_tensor(out=wide(L1[:, lo:lo + 4, :]), in0=wide(L1[:, lo:lo + 4, :]),
                                         scalar=wgt, in1=wide(RS1), op0=mul, op1=mul).then_inc(n_used, 1)
            dve.wait_ge(n_rs, 5)
            for g in range(2):
                dve.scalar_tensor_tensor(out=L1[:, 9 + 2 * g, :], in0=L1[:, 8 + 2 * g, :],
                                         scalar=pc2(DKN), in1=RS1[:, g, :], op0=mul, op1=mul)
            t.step(dve.tensor_copy(NMX[:, 0:1], pc2(0)))
            t.settle()
            for g in range(2):
                ins = dve.tensor_copy(L1[:, 8 + 2 * g, :], L1[:, 9 + 2 * g, :])
            ins.then_inc(n_used, 1)

            dve.sem_inc(at_z, 4)
            dve.sem_inc(at_on, 1)
            with dve.Fori(0, 2) as ty:
                with dve.Fori(0, PAIRS) as j:
                    pair8 = ty * 32 + j * 8
                    with t.loop(ty, 4, 2), t.loop(j, 1, PAIRS):
                        for u in range(8):
                            i, p = u // 2, u % 2
                            wdt = P * (i + 1)
                            z = ZB[:, ZSLOT[u], 0:wdt]
                            dve.wait_ge(at_qk, pair8 + (u + 1))
                            if u >= 3:
                                dve.wait_ge(at_t, pair8 + (u - 2))
                            elif u == 0:
                                dve.wait_ge(at_on, ty * 4 + j + 1)
                            slope = SLOPE[:, bass.ds(ty * 8 + j * 2 + p, 1)]
                            dist = BIAS[:, bass.ds(ty, 1), bias_off(i):bias_off(i) + wdt]\
                                .rearrange("p a w -> p (a w)")
                            dve.scalar_tensor_tensor(out=z, in0=dist, scalar=slope,
                                                     in1=bank[u % 4][:, 0:wdt], op0=mul, op1=add)\
                               .then_inc(at_z, 1)
                            dve.wait_ge(at_z, pair8 + (4 + u + 1))
                            dve.tensor_reduce(NMX[:, u:u + 1], z, AX.X, ALU.max, negate=True)\
                               .then_inc(at_mx, 1)
                        dve.wait_ge(at_p, pair8 + 8)
                        t.link(dve.reciprocal(RINV, RSUM))
                        dve.wait_ge(at_o, pair8 + 8)
                        dst = ON[:, :, bass.ds(ty * 512 + j * 128, 128)].rearrange("p i (q d) -> p i q d", q=2)
                        dve.tensor_tensor(dst, bank[6][:, :].rearrange("p (i q d) -> p i q d", i=4, q=2),
                                          RINV.rearrange("p (i q) -> p i q", i=4).unsqueeze(3)
                                          .broadcast_to([P, 4, 2, HD]), mul).then_inc(at_on, 1)
            for k in range(KT):
                dve.wait_ge(mix_hi, 2 + k + 1)
                dve.tensor_tensor(AL[:, k, :], src(q_mix + k)[:, :], as_f32(AH[:, k, :]), sub)\
                   .then_inc(bank_read, 1)
            residual(q_out[1])
            norm(3)
            mlp(1)

        @block.gpsimd
        def _(pool):
            t = Tally(pool, pool_step)
            mul = ALU.mult

            def select(x, base, pattern, cm, fill, op=ALU.is_ge):
                t.link(pool.affine_select(out=x, in_=x, pattern=pattern, compare_op=op, fill=fill,
                                          base=base, channel_multiplier=cm))

            t.step(pool.memset(IDENT, 0.0))
            t.step(pool.memset(ONES, 1.0))
            t.step(pool.memset(INCL, 1.0))
            t.step(pool.memset(STRICT, 1.0))
            t.step(pool.memset(HEADS2, 0.0))
            t.step(pool.memset(wide(MERGE), 0.0))
            t.step(pool.memset(SCANM, 1.0))
            t.settle()
            select(IDENT, 0, [[-1, P]], 1, 1.0, ALU.not_equal)
            select(INCL, 0, [[1, P]], -1, 0.0)
            select(STRICT, -1, [[1, P]], -1, 0.0)
            for p in range(2):
                t.link(pool.memset(HEADS2[p * HD:(p + 1) * HD, p * HD:(p + 1) * HD], 1.0))
            t.link(pool.memset(SCANM.rearrange("p (k t) -> p k t", k=4)[:, :, 0:1], 0.0))
            first = MERGE[:, 0, :].rearrange("p (n q) -> p n q", q=2)[:, :, 1]
            t.link(pool.memset(first, -1.0))
            select(first, 0, [[-2, P // 2]], 1, 0.0, ALU.is_equal)
            for lev in range(1, LEVELS):
                b = 1 << lev
                low = MERGE[:, lev, :].rearrange("p (n q w) -> p n q w", q=2, w=b)[:, :, 0, :]
                t.link(pool.memset(low, 1.0))
                select(low, -b, [[-2 * b, P // (2 * b)], [0, b]], 1, 0.0)
                select(low, 2 * b - 1, [[2 * b, P // (2 * b)], [0, b]], -1, 0.0)
            for g in range(16):
                col = (g % 2) * NH + g // 2
                t.step(pool.memset(SLOPE[:, col:col + 1], -float(np.float32(2.0) ** np.float32(-0.5 * (g + 1)))))
            t.settle()
            pool.memset(wide(M8), 0.0).then_inc(consts, 1)
            for s in range(2):
                t.step(pool.memset(STAGE[s][:, :, 0:3], 0.0))
            t.settle()
            pool.memset(NMX, 0.0).then_inc(pads_zero, 1)

            pool.wait_ge(l0_dve, 1)
            pool.memset(wide(SR), 0.0)
            pool.memset(wide(SG), 0.0)
            with pool.Fori(0, TT) as c:
                n = c + 1
                here = bass.ds(c * P, P)
                row = bass.ds(c, 1)

                def by_parity(x, p):
                    return x[:, row, :].rearrange("p o (j q) -> p (o j) q", q=2)[:, :, p]\
                        .unsqueeze(2).broadcast_to([P, 4, P])

                for p in range(2):
                    ins = pool.tensor_tensor(GTRI[p], INCL.unsqueeze(1).broadcast_to([P, 4, P]),
                                             by_parity(GLOG, p), mul)
                ins.then_inc(e_gtri, 1)
                pool.tensor_copy(KC, GK[:, :, here])
                pool.tensor_copy(QC, GQ[:, :, here])
                pool.tensor_copy(VGC, GV[:, :, here])
                pool.tensor_copy(VRC, V[:, :, here]).then_inc(e_copy, 1)
                pool.wait_ge(e_exp, n)
                pool.tensor_tensor(BD, BD, B[:, :, here], mul)
                pool.tensor_tensor(AD, AD, KK[:, :, here], mul).then_inc(e_ba, 1)
                pool.wait_ge(e_dt, n)
                for p in range(2):
                    pool.tensor_tensor(LT[2 + p], DT[p], by_parity(BETA, p), mul)
                    ins = pool.tensor_tensor(GRK[p], DT[p], INCL.unsqueeze(1).broadcast_to([P, 4, P]), mul)
                ins.then_inc(e_dmask, 1)
                with t.loop(c, 4, TT):
                    for g in range(4):
                        pool.wait_ge((r_lt, r_kk)[g // 2], n)
                        t.link(pool.tensor_tensor(QI[g], LT[g], MERGE[:, 0:1, :].broadcast_to([P, 4, P]), mul))
                        pool.tensor_tensor(QI[g], QI[g], IDENT.unsqueeze(1).broadcast_to([P, 4, P]),
                                           ALU.add).then_inc(inv_q, 1)
                pool.wait_ge(f_tg, n)
                pool.wait_ge(e_state, n)

            def weight_lo(u, dyn=0):
                pool.wait_ge(hi_ready, dyn + (u + 1))
                pool.tensor_tensor(WL[:, u % 2], RAW[:, u % 2], as_f32(WH[:, u % 2]), ALU.subtract)\
                    .then_inc(lo_ready, 1)

            def weights(first, last):
                with pool.Fori(0, (last - first) // 2) as i:
                    weight_lo(first, i * 2)
                    weight_lo(first + 1, i * 2)

            weights(0, 2)
            pool.wait_ge(mix_hi, 1)
            pool.tensor_tensor(HL[:, 4:8, :], GQ, as_f32(HH[:, 4:8, :]), ALU.subtract).then_inc(mix_lo, 1)
            weights(2, u_mlp[0] + 2)
            pool.wait_ge(iw_split, 1)
            pool.tensor_tensor(IWL, IWW, as_f32(IWH), ALU.subtract).then_inc(iw_split, 1)
            weights(u_mlp[0] + 2, u_kv)
            t.link(pool.iota(DIST.bitcast(I32), [[-1, W]], base=W - P, channel_multiplier=1))
            t.link(pool.tensor_copy(DIST, DIST.bitcast(I32)))
            pool.affine_select(out=DIST, in_=DIST, pattern=[[-1, W]], compare_op=ALU.is_ge, fill=FAR,
                               base=W - P, channel_multiplier=1).then_inc(dist_ready, 1)
            weights(u_kv, u_mqk)
            for i in range(1, TT):
                pool.wait_ge(idx_acc, NH * i)
                d = SCORE[:, i - 1, P * i:P * (i + 1)]
                pool.affine_select(out=d, in_=d, pattern=[[-1, P]], compare_op=ALU.is_ge,
                                   fill=CAUSAL_FILL, base=0, channel_multiplier=1).then_inc(idx_masked, 1)
            weights(u_mqk, u_out[1] + 2)
            pool.wait_ge(n_used, 5)
            with pool.Fori(0, 2) as ty:
                with pool.Fori(0, PAIRS) as j:
                    pool.wait_ge(at_z, ty * 32 + j * 8 + 4)
                    q = L1[:, bass.ds(ty * 4 + j, 1), :].rearrange("p a w -> p (a w)")
                    k = L1[:, bass.ds(ty * 4 + j + 8, 1), :].rearrange("p a w -> p (a w)")
                    pool.tensor_copy(QS, q)
                    pool.tensor_copy(KS, k).then_inc(at_stage, 1)
            weights(u_out[1] + 2, u_mlp[1] + 32)


PAR64 = ("gdn_norm_w", "dsa_q_norm", "dsa_k_norm", "idx_k_ln_w", "idx_k_ln_b", "moba_q_norm",
         "moba_k_norm")
N_PAR = 2 + 8 + 1 + 2 * len(PAR64) + 6
ZSLOT = [u % 3 for u in range(8)]
DVE_CHUNK = 16

_INS = ("x norm1_g norm2_g mlp_w1 mlp_w2 ev_w_in ev_w_out rwkv_mu rwkv_w0 rwkv_w2 rwkv_a0 rwkv_a2 "
        "rwkv_g2 rwkv_k_k rwkv_k_a rwkv_r_k rwkv_lnx_w rwkv_lnx_b gdn_conv_w gdn_a_log gdn_dt_bias "
        "gdn_norm_w od_w_in od_w_out dsa_q_norm dsa_k_norm idx_k_ln_w idx_k_ln_b moba_q_norm "
        "moba_k_norm").split()


def kernel(**inputs):
    import concourse.bacc as _bacc
    from concourse.bass_utils import run_bass_kernel_spmd as _run

    nc = _bacc.Bacc("TRN2", target_bir_lowering=False, num_devices=1)
    arrays, aps = {}, {}
    for name in _INS:
        x = np.ascontiguousarray(inputs[name])
        arrays[f"in_{name}_dram"] = x
        aps[name] = nc.dram_tensor(f"in_{name}_dram", x.shape, mybir.dt.from_np(x.dtype),
                                   kind="ExternalInput").ap()
    out = nc.dram_tensor("out_0_dram", (1, SEQ, D), F32, kind="ExternalOutput").ap()
    trunk_kernel(nc, aps, out)
    r = _run(nc, [arrays], core_ids=[0])
    return r.results[0]["out_0_dram"]
```

```python
from contextlib import ExitStack, contextmanager

import numpy as np

import concourse.bass as bass
from concourse import mybir

F32 = mybir.dt.float32
F32R = mybir.dt.float32r
I32 = mybir.dt.int32
ALU = mybir.AluOpType
ACT = mybir.ActivationFunctionType
AX = mybir.AxisListType

P = 128
SEQ = 512
D = 1024
DFF = 4096
HD = 64
KT = D // P
TT = SEQ // P
W = SEQ
NH = 8
PAIRS = NH // 2
PW = 516
CW = P + 1
UW = 256
USLOT = UW + NH
LEVELS = 6
RMS_EPS = 1e-6
GN_EPS = 6.4e-4
RWKV_COLS = 1792
GDN_QKV = RWKV_COLS
GDN_BA = RWKV_COLS + 3 * 512
GDN_Z = GDN_BA + 2 * NH
OD_K, OD_V, OD_IQ, OD_IK, OD_IW = 512, 640, 768, 1280, 1344
OD_MQ = 1352
OD_MV = OD_MQ + 1024
TOPK = min(256, SEQ // 4)
CAUSAL_FILL = -3.0e38
TAKEN = -3.4e38
FAR = 1.0e30


class Tally:

    def __init__(self, eng, sem):
        self.eng, self.sem, self.n, self.loops = eng, sem, 0, []

    @contextmanager
    def loop(self, reg, per, trips, first=0):
        start = self.n
        self.loops.append((reg, per, first))
        yield
        self.loops.pop()
        assert self.n - start == per, (self.n - start, per)
        self.n = start + per * trips

    def value(self, n=None):
        v = self.n if n is None else n
        for reg, per, first in self.loops:
            v = (reg * per) + (v - first * per)
        return v

    def step(self, ins):
        self.n += 1
        return ins.then_inc(self.sem, 1)

    def settle(self):
        self.eng.wait_ge(self.sem, self.value())

    def link(self, ins):
        self.step(ins)
        self.settle()


def trunk_kernel(nc, a, out):
    ctx = ExitStack()
    with ctx:
        def sem(name):
            return ctx.enter_context(nc.semaphore(name))

        ARENA, PARTS = 53000, 28224
        lower = ctx.enter_context(nc.sbuf_tensor("lower", [P, PARTS], F32))
        with nc.sbuf_tensor("upper", [P, ARENA - PARTS], F32) as upper:
            pass

        def parts(name, a_, n, w):
            return ctx.enter_context(nc.sbuf_tensor(name, [P, a_, n, w], F32R))

        AH, AL, HL, HH = (parts(n_, 1, KT, W)[:, 0] for n_ in ("a_hi", "a_lo", "h_lo", "h_hi"))
        WH, WL = parts("w_hi", 2, KT, USLOT), parts("w_lo", 2, KT, USLOT)
        bank = [ctx.enter_context(nc.psum_tensor(f"bank{i}", [P, 512], F32)) for i in range(8)]

        top = [0]

        def carve(n):
            off = top[0]
            top[0] += n
            assert top[0] <= ARENA, top[0]
            return off

        def flat(off, n):
            if off >= PARTS:
                return upper[:, off - PARTS:off - PARTS + n]
            assert off + n <= PARTS, (off, n)
            return lower[:, off:off + n]

        def grid(off, n, w):
            return flat(off, n * w).rearrange("p (n w) -> p n w", n=n)

        def wide(x):
            return x.rearrange("p n w -> p (n w)")

        XT = grid(carve(KT * W), KT, W)
        IDENT, ONES = flat(carve(P), P), flat(carve(P), P)
        HEADS2 = flat(carve(P), P)
        INCL = flat(carve(P), P)
        STRICT = flat(carve(P), P)
        o_merge = carve(LEVELS * P)
        MERGE = grid(o_merge, LEVELS, P)
        SCANM = flat(carve(4 * CW), 4 * CW)
        PC = flat(carve(P), P)
        PC2 = flat(carve(8), 8)
        misc = [carve(576)]
        misc_end = top[0]

        def small(n):
            off = misc[0]
            misc[0] += n
            assert misc[0] <= misc_end
            return flat(off, n)

        def by_chunk(n):
            return small(TT * n).rearrange("p (c h) -> p c h", c=TT)

        OMKA = small(4)
        ALOG, DTB, NEA = small(NH), small(NH), small(NH)
        AB = by_chunk(16)
        BETA, GLOG, GTMP, GCUM = by_chunk(NH), by_chunk(NH), by_chunk(NH), by_chunk(NH)
        EG = by_chunk(NH)
        EREST = by_chunk(NH)
        ESTATE = by_chunk(PAIRS)
        SM, ESM = small(8), small(8)
        NMEAN, VAR, RSTD = small(NH), small(16), small(16)
        SLOPE = small(16)
        QW = small(2)
        IW = by_chunk(NH)
        M8 = small(8 * (TT - 1)).rearrange("p (i n) -> p i n", i=TT - 1)
        NMX, RSUM, RINV = small(2 * NH), small(2 * NH), small(2 * NH)

        o_ht = carve(2 * KT * USLOT)
        HT = grid(o_ht, KT, W)
        o_ring = carve(2 * KT * W)
        RING = flat(o_ring, 2 * KT * W).rearrange("p (s k n) -> p s k n", s=2, k=KT)
        work = top[0]

        o_rkv, o_z, o_lw2 = carve(12 * W), carve(4 * W), carve(W)
        top[0] = PARTS
        o_gqkv = carve(12 * W)
        o_g, o_bon, o_kk, o_b = (carve(4 * W) for _ in range(4))
        o_cum = carve(4 * 4 * CW)
        RKV, GQKV = grid(o_rkv, 12, W), grid(o_gqkv, 12, W)
        R, K, V = (grid(o_rkv + i * 4 * W, 4, W) for i in range(3))
        GQ, GK, GV = (grid(o_gqkv + i * 4 * W, 4, W) for i in range(3))
        Z, KK, B, G, BON = (grid(o, 4, W) for o in (o_z, o_kk, o_b, o_g, o_bon))
        CUM = flat(o_cum, 16 * CW).rearrange("p (c k t) -> p c k t", c=4, k=4)
        tail = top[0]
        XIN = grid(o_gqkv, TT, D)
        PR, PR2 = flat(o_z, P), flat(o_z + P, P)
        SQ = [grid(o_g, KT, W)] + [grid(o_ring + 4 * W, KT, W)] * 3
        RS = [flat(o_cum, W)] + [flat(o_ring + 12 * W, W)] * 3

        o_stage = [carve(4 * PW), carve(4 * PW)]
        STAGE = [grid(o, 4, PW) for o in o_stage]
        SQA, SQB = (grid(o, 4, W) for o in o_stage)
        CONV = grid(carve(4 * W), 4, W)
        SQC = CONV
        LW2, G2 = flat(o_lw2, W), flat(carve(W), W)
        WA, GD = flat(carve(W), W), flat(carve(W), W)
        TMPD = flat(carve(W), W)

        spare = [[o_ht, KT * W], [o_ring, 2 * KT * W], [tail, ARENA - tail]]

        def chunk_buf(w=P):
            for s in spare:
                if s[1] >= 4 * P:
                    s[0] += 4 * P
                    s[1] -= 4 * P
                    return grid(s[0] - 4 * P, 4 * P // w, w)
            raise AssertionError("no room")

        QI, XM = ([chunk_buf() for _ in range(4)] for _ in range(2))
        KC, QC, VRC, VGC = (chunk_buf() for _ in range(4))
        LT, TI = ([chunk_buf() for _ in range(4)] for _ in range(2))
        RD, KD, BD, AD = (chunk_buf() for _ in range(4))
        KTOK, BTOK, VR, KGT, VG = (wide(chunk_buf()) for _ in range(5))
        MK, RK, RBM, GRK = ([chunk_buf() for _ in range(2)] for _ in range(4))
        SR, SG = chunk_buf(), chunk_buf()
        DT, GTRI = [XM[2], XM[3]], [XM[0], XM[1]]
        X1R, UN, VN = wide(MK[0]), wide(MK[1]), wide(LT[2])
        OR, OG = wide(LT[0]), wide(LT[1])
        OSQ, OSQG, TMPG, TMPS = wide(TI[0]), wide(TI[1]), wide(TI[2]), TI[3]
        TMPK = wide(XM[0])

        RAW = flat(o_ht, 2 * KT * USLOT).rearrange("p (s k n) -> p s k n", s=2, k=KT)
        SQT = grid(o_ring, 4, W)

        L1 = grid(o_ring, 21, W)
        o_vall = o_ring + 21 * W
        VALL = grid(o_vall, TT, 1024)
        o_score = o_vall + 4096
        SCORE = grid(o_score, 3, W)
        DIST = flat(o_merge, W)
        o_bias = PARTS
        BIASW = P * TT * (TT + 1) // 2
        BIAS = grid(o_bias, 2, BIASW)
        o_att = o_bias + 2 * BIASW
        SQ1, SQK = [grid(o_att, 4, W), grid(o_att + 4 * W, 4, W)], grid(o_att + 9 * W, 2, W)
        RT = grid(o_att, 4, W)
        QS, KS = grid(o_score, 2, W), grid(o_score + 2 * W, 2, W)
        PTS = grid(o_att + 8 * W, 3, W)
        ZB = grid(PARTS + 3 * KT * W, 8, W)
        o_on = PARTS + 2 * KT * W
        assert o_att + 11 * W <= o_on
        ON = grid(o_on, TT, 1024)
        OUTT = grid(work, TT, D)

        at = dict(norm1=0, norm2=16, mu=32, w0=46, a0=50, k_k=54, k_a=58, r_k=62, lnx_w=66,
                  lnx_b=70, conv=74)
        NPC = 122
        GDNN, DQN, DKN, LNW, LNB, MQN, MKN = range(7)

        def pc(name, i):
            return PC[:, at[name] + i:at[name] + i + 1]

        def pc2(i):
            return PC2[:, i:i + 1]

        def bias_off(i):
            return P * i * (i + 1) // 2

        bank_filled, bank_read = sem("bank_filled"), sem("bank_read")
        q_x, q_par, q_lora, q_ab, q_z, q_w, q_a, q_g, q_pair = 0, 8, 11, 13, 14, 18, 22, 26, 30
        q_kk, q_gq, q_gk, q_bon, q_cum = 54, 58, 62, 66, 70
        q_out, q_m1, q_m2 = [71, 222], [80, 231], [88, 239]
        q_norm = [10, 79, 144, 230]
        q_k, q_ik, q_v, q_iq, q_ikm, q_ikv, q_mv = 145, 147, 148, 150, 154, 159, [155, 160]
        q_idx, q_dq, q_k2n, q_mq, q_dqn, q_mk, q_mqn, q_mkn, q_mix = (
            164, 188, 192, 194, 198, 202, 206, 210, 214)
        q_fin = 295
        VIW = P + NH
        u_out, u_mlp, u_kv, u_iq, u_mv, u_dq, u_mqk = [0, 48], [4, 52], 36, 38, 40, 42, 44

        (dma_par, dma_late, dma_x, dma_out, consts, squares, rms, h_ready, below_begun, inverse_begun, topk_rounds,
         pads_zero, lora_shifted, lora_act, cum_ready, stage_in, stage_used, conv_out, conv_used,
         kk_ready, sq_grp, rs_grp, bonus_in, gate_in, gate_ln, glog_ready,
         gcum_ready, l0_dve, l0_act, mix_ready, h1_ready, h_hi, h_lo, mix_hi, mix_lo, hi_ready,
         lo_ready) = (sem(n) for n in (
             "dma_par dma_late dma_x dma_out consts squares rms h_ready below_begun inverse_begun topk_rounds pads_zero "
             "lora_shifted lora_act cum_ready stage_in stage_used conv_out conv_used kk_ready "
             "sq_grp rs_grp bonus_in gate_in gate_ln glog_ready gcum_ready "
             "l0_dve l0_act mix_ready h1_ready h_hi h_lo mix_hi mix_lo hi_ready lo_ready").split())
        w_full = [sem("w_full0"), sem("w_full1")]
        raw_full = [sem("raw_full0"), sem("raw_full1")]
        act_step, dve_step, pool_step = sem("act_step"), sem("dve_step"), sem("pool_step")
        (f_grow, f_kt, f_vg, f_vr, f_kk, f_kq, f_lt, f_mk, f_rk, f_rb, f_ktok, f_btok, f_x1, f_ks,
         f_u, f_y, f_or, f_og, f_qs, f_sr, f_sg, f_tr, f_tg) = (sem(n) for n in (
             "f_grow f_kt f_vg f_vr f_kk f_kq f_lt f_mk f_rk f_rb f_ktok f_btok f_x1 f_ks "
             "f_u f_y f_or f_og f_qs f_sr f_sg f_tr f_tg").split())
        (e_diff, e_exp, e_copy, e_gtri, e_dsub, e_dt, e_dmask, e_rk, e_ba, e_s0, r_kt, r_vg, r_vr,
         r_kk, r_kq, r_lt, r_mk, r_rk, r_rb, r_ktok, r_btok, r_x1, r_ks, r_u, r_y, e_var, e_rstd,
         e_on, e_og, r_tr, r_tg, e_state, e_ln) = (sem(n) for n in (
             "e_diff e_exp e_copy e_gtri e_dsub e_dt e_dmask e_rk e_ba e_s0 r_kt r_vg r_vr "
             "r_kk r_kq r_lt r_mk r_rk r_rb r_ktok r_btok r_x1 r_ks r_u r_y e_var e_rstd "
             "e_on e_og r_tr r_tg e_state e_ln").split())
        inv_x, inv_xs, inv_y, inv_t, inv_turned, inv_q, inv_first, inv_q0, inv_q1 = (sem(n) for n in (
            "inv_x inv_xs inv_y inv_t inv_turned inv_q inv_first inv_q0 inv_q1").split())
        (f_u1, f_y1, f_zr, f_zg, r_u1, r_y1, r_zr, r_zg) = (sem(n) for n in (
            "f_u1 f_y1 f_zr f_zg r_u1 r_y1 r_zr r_zg").split())
        MERGES = 4 * (LEVELS - 1)
        (n_sq, n_rs, n_used, ik_centred, dist_ready, idx_acc, idx_masked,
         at_stage, at_qk, at_z, at_mx, at_p, at_t, at_pt, at_o, at_on) = (
             sem(n) for n in (
                 "n_sq n_rs n_used ik_centred dist_ready idx_acc idx_masked "
                 "at_stage at_qk at_z at_mx at_p at_t at_pt at_o at_on").split())

        block = ctx.enter_context(nc.Block())
        ev, od = a["ev_w_in"][0], a["od_w_in"][0]

        def raw_count(u):
            return 16 * (u // 2 + 1) + (48 if u >= u_kv else 0)

        def unit_cols(u):
            return USLOT if u == u_kv + 1 else UW

        def as_f32(x):
            return x.bitcast(F32)

        x_rows = a["x"][0].rearrange("(t p) d -> p t d", p=P)

        def kmaj(w):
            return w.rearrange("(k p) n -> p k n", p=P)

        @block.sync
        def _(sp):
            def load(slot, cols, at=0):
                w = cols.shape[-1]
                sp.dma_start(RING[:, slot, :, at:at + w], kmaj(cols)).then_inc(w_full[slot], 16)

            sp.dma_start(XIN[:, 0:2, :], x_rows[:, 0:2, :]).then_inc(dma_x, 16)
            load(0, ev[:, 1536:RWKV_COLS])
            load(0, ev[:, GDN_BA:GDN_BA + 16], at=256)
            load(1, ev[:, GDN_Z:GDN_Z + 512])
            sp.wait_ge(bank_filled, q_z)
            load(0, ev[:, 0:512])
            sp.wait_ge(bank_filled, q_w)
            load(1, ev[:, GDN_QKV:GDN_QKV + 512])
            with sp.Fori(1, 3) as i:
                sp.wait_ge(bank_filled, i * 8 + (q_pair - 4))
                load(0, ev[:, bass.ds(i * 512, 512)])
                sp.wait_ge(bank_filled, i * 8 + q_pair)
                load(1, ev[:, bass.ds(i * 512 + GDN_QKV, 512)])

            def unit(u, dyn=0):
                if u >= 2:
                    sp.wait_ge(lo_ready, dyn + (u - 1))

            def load_raw(u, cols, at=0):
                sp.dma_start(RAW[:, u % 2, :, at:at + cols.shape[-1]], kmaj(cols))\
                  .then_inc(raw_full[u % 2], 16)

            def w_out(l):
                wout = a["ev_w_out" if l == 0 else "od_w_out"][0]
                for v in range(4):
                    unit(u_out[l] + v)
                    load_raw(u_out[l] + v, wout[:, v * UW:(v + 1) * UW])

            def mlp(l):
                w1, w2 = a["mlp_w1"][l], a["mlp_w2"][l].rearrange("(r p) n -> p r n", p=P)
                with sp.Fori(0, 4) as i:
                    for v in range(8):
                        u = u_mlp[l] + v
                        unit(u, i * 8)
                        if v < 4:
                            load_raw(u, w1[:, bass.ds(i * 1024 + v * UW, UW)])
                        else:
                            sp.dma_start(RAW[:, u % 2, :, 0:UW], w2[:, bass.ds(i * 8, 8), (v - 4) * UW:(v - 3) * UW])\
                              .then_inc(raw_full[u % 2], 16)

            sp.wait_ge(f_y, TT)
            sp.wait_ge(f_qs, TT)
            w_out(0)
            mlp(0)
            unit(u_kv)
            for g in range(2):
                for half in range(2):
                    load_raw(u_kv, od[:, OD_K + g * HD:OD_K + (g + 1) * HD], at=(2 * g + half) * HD)
            unit(u_kv + 1)
            for half in range(2):
                load_raw(u_kv + 1, od[:, OD_IK:OD_IK + HD], at=half * HD)
            load_raw(u_kv + 1, od[:, OD_V:OD_V + 128], at=128)
            load_raw(u_kv + 1, od[:, OD_IW:OD_IW + NH], at=UW)
            for u0, col in ((u_iq, OD_IQ), (u_mv, OD_MV), (u_dq, 0), (u_mqk, OD_MQ), (u_mqk + 2, OD_MQ + 512)):
                for v in range(2):
                    unit(u0 + v)
                    load_raw(u0 + v, od[:, col + v * UW:col + (v + 1) * UW])
            w_out(1)
            mlp(1)
            for i in range(TT):
                sp.wait_ge(bank_read, q_fin + 2 * i + 2)
                sp.dma_start(out[0, i * P:(i + 1) * P, :], OUTT[:, i, :]).then_inc(dma_out, 16)
            sp.wait_ge(dma_out, 16 * TT)

        @block.tensor
        def _(pe):
            full = [0, 0]

            def arrived(slot, dmas=1):
                full[slot] += 16 * dmas
                pe.wait_ge(w_full[slot], full[slot])

            def take(q, dyn=0):
                if q >= 8:
                    pe.wait_ge(bank_read, dyn + (q - 7))
                return bank[q % 8]

            def group(slot, act, q, dyn=0, ready=None):
                for b in range(4):
                    o = take(q + b, dyn)
                    for k in range(KT):
                        if ready is not None and b == 0:
                            ready(k)
                        mm = pe.matmul(o[:, :], RING[:, slot, k, b * P:(b + 1) * P], act(k),
                                       start=(k == 0), stop=(k == KT - 1))
                    mm.then_inc(bank_filled, 1)

            def norm(n):
                o = take(q_norm[n])
                for k in range(KT):
                    pe.wait_ge(squares, KT * n + k + 1)
                    mm = pe.matmul(o[:, :], ONES, SQ[n][:, k, :], start=(k == 0), stop=(k == KT - 1))
                mm.then_inc(bank_filled, 1)

            def normed(n):
                return lambda k: pe.wait_ge(h_ready, KT * n + k + 1)

            def h(k):
                return HT[:, k, :]

            pe.wait_ge(consts, 1)
            pe.wait_ge(dma_x, 32)
            for k in range(KT):
                o = take(q_x + k)
                for i in range(TT):
                    mm = pe.transpose(o[:, i * P:(i + 1) * P], XIN[:, i, k * P:(k + 1) * P], IDENT)
                mm.then_inc(bank_filled, 1)
            pe.wait_ge(dma_par, 16 * N_PAR)
            pe.transpose(take(q_par)[:, 0:NPC], PR[0:NPC, :], IDENT[0:NPC, 0:NPC]).then_inc(bank_filled, 1)
            pe.transpose(take(q_par + 1)[:, 0:7], PR2[0:7, :], IDENT[0:7, 0:7]).then_inc(bank_filled, 1)
            norm(0)

            arrived(0, 2)
            for b in range(2):
                o = take(q_lora + b)
                for k in range(KT):
                    if b == 0:
                        pe.wait_ge(h_ready, k + 1)
                    mm = pe.matmul(o[:, :], RING[:, 0, k, b * P:(b + 1) * P], h(k),
                                   start=(k == 0), stop=(k == KT - 1))
                mm.then_inc(bank_filled, 1)
            o = take(q_ab)
            for i in range(TT):
                for k in range(KT):
                    mm = pe.matmul(o[:, 16 * i:16 * i + 16], HT[:, k, i * P:(i + 1) * P],
                                   RING[:, 0, k, 256:272], start=(k == 0), stop=(k == KT - 1))
            mm.then_inc(bank_filled, 1)
            arrived(1)
            group(1, h, q_z)

            pe.wait_ge(lora_act, 2)
            pe.wait_ge(dma_late, 16 * 5)
            for c in range(4):
                pe.matmul(take(q_w + c)[:, :], LW2[0:HD, c * P:(c + 1) * P], WA[0:HD, :],
                          start=True, stop=True).then_inc(bank_filled, 1)
            for c in range(4):
                pe.matmul(take(q_a + c)[:, :], LW2[HD:P, c * P:(c + 1) * P], WA[HD:P, :],
                          start=True, stop=True).then_inc(bank_filled, 1)
            for c in range(4):
                pe.matmul(take(q_g + c)[:, :], G2[:, c * P:(c + 1) * P], GD,
                          start=True, stop=True).then_inc(bank_filled, 1)

            with pe.Fori(0, 3) as i:
                pe.wait_ge(w_full[0], i * 16 + (full[0] + 16))
                group(0, h, q_pair, i * 8)
                pe.wait_ge(w_full[1], i * 16 + (full[1] + 16))
                group(1, h, q_pair + 4, i * 8)
            full[0] += 48
            full[1] += 48

            for n, (q, src) in enumerate(((q_kk, SQA), (q_gq, SQB), (q_gk, SQC), (q_bon, BON))):
                if n < 3:
                    pe.wait_ge(sq_grp, n + 1)
                else:
                    pe.wait_ge(bonus_in, 4)
                for c in range(4):
                    pe.matmul(take(q + c)[:, :], HEADS2, src[:, c, :],
                              start=True, stop=True).then_inc(bank_filled, 1)
            pe.wait_ge(glog_ready, 1)
            o = take(q_cum)
            pe.matmul(o[:, 0:32], INCL, wide(GLOG), start=True, stop=True)
            pe.matmul(o[:, 32:64], ONES, wide(GLOG), start=True, stop=True).then_inc(bank_filled, 1)

            pe.wait_ge(l0_dve, 1)
            pe.wait_ge(l0_act, 1)

            def half(x, p, j):
                return x[p * HD:(p + 1) * HD, j, :]

            def head_products(banks, lhs, rhs, done):
                for j in range(PAIRS):
                    for p in range(2):
                        mm = pe.matmul(bank[banks[p]][:, j * P:(j + 1) * P], half(lhs, p, j),
                                       half(rhs, p, j), start=True, stop=True)
                mm.then_inc(done, 1)

            def turn(b, src, done):
                for j in range(PAIRS):
                    mm = pe.transpose(bank[b][:, j * P:(j + 1) * P], src[:, j, :], IDENT)
                mm.then_inc(done, 1)

            def turn_wide(b, src, done):
                for j in range(PAIRS):
                    mm = pe.transpose(bank[b][:, j * P:(j + 1) * P], src[:, j * P:(j + 1) * P], IDENT)
                mm.then_inc(done, 1)

            def by_state(b, lhs, state, more):
                for j in range(PAIRS):
                    mm = pe.matmul(bank[b][:, j * P:(j + 1) * P], lhs[:, j, :], state[:, j, :],
                                   start=(j == 0), stop=not more, skip_group_check=True)
                return mm

            def by_heads(b, mats, vals, first, last):
                for hh in range(NH):
                    cols = slice(hh * HD, (hh + 1) * HD)
                    mm = pe.matmul(bank[b][:, cols], mats[hh % 2][:, hh // 2, :], vals[:, cols],
                                   start=(first and hh == 0), stop=last, skip_group_check=True)
                return mm

            TOP, LOW = slice(0, HD), slice(HD, P)

            def below(b, mats, vals, rows, first):
                pe.sem_inc(below_begun, 1)
                for hh in range(NH):
                    cols = slice(hh * HD, (hh + 1) * HD)
                    mm = pe.matmul(bank[b][LOW, cols], mats[hh % 2][rows, hh // 2, LOW],
                                   vals[rows, cols], start=(first and hh == 0), stop=True,
                                   skip_group_check=True)
                return mm

            with pe.Fori(0, TT) as c:
                n = c + 1
                pe.wait_ge(e_gtri, n)
                for p in range(2):
                    mm = pe.matmul(bank[p][:, :], ONES, wide(GTRI[p]), start=True, stop=True)
                mm.then_inc(f_grow, 1)
                pe.wait_ge(e_copy, n)
                turn(2, KC, f_kt)
                turn(3, VGC, f_vg)
                turn(4, VRC, f_vr)
                head_products((5, 6), KC, KC, f_kk)
                pe.wait_ge(r_kt, n)
                head_products((7, 2), KC, QC, f_kq)
                pe.wait_ge(e_ba, n)
                pe.wait_ge(e_rk, n)
                pe.wait_ge(r_vg, n)
                pe.wait_ge(r_vr, n)
                head_products((3, 4), BD, AD, f_lt)
                pe.wait_ge(e_dsub, n)
                head_products((0, 1), KD, AD, f_mk)
                pe.wait_ge(r_kk, n)
                head_products((5, 6), KD, RD, f_rk)
                pe.wait_ge(r_kq, n)
                head_products((7, 2), BD, RD, f_rb)
                pe.wait_ge(r_lt, n)
                turn(3, KD, f_ktok)
                turn(4, BD, f_btok)
                pe.wait_ge(e_s0, n)
                pe.wait_ge(r_mk, n)
                by_state(0, AD, SR, True)
                by_heads(0, MK, VR, False, True).then_inc(f_x1, 1)
                by_state(1, KC, SG, False).then_inc(f_ks, 1)
                pe.wait_ge(r_x1, n)
                pe.wait_ge(r_ks, n)
                pe.wait_ge(r_rb, n)
                pe.wait_ge(r_btok, n)
                pe.sem_inc(inverse_begun, 1)
                for g in range(4):
                    pe.wait_ge((inv_q0, inv_q1)[g // 2], c * 2 + (g % 2 + 1))
                    for j in range(PAIRS):
                        mm = pe.transpose(bank[2 * g][:, j * P:(j + 1) * P], QI[g][:, j, :], IDENT)
                    mm.then_inc(inv_first, 1)
                with pe.Fori(0, LEVELS - 1) as lev:
                    def merged(g, sem_, per, more=0):
                        pe.wait_ge(sem_, c * per + (lev * 4 + (g + 1 + more)))

                    for g in range(4):
                        merged(g, inv_t, MERGES + 4)
                        for j in range(PAIRS):
                            mm = pe.matmul(bank[2 * g][:, j * P:(j + 1) * P], LT[g][:, j, :],
                                           TI[g][:, j, :], start=True, stop=True)
                        mm.then_inc(inv_x, 1)
                    for g in range(4):
                        merged(g, inv_xs, MERGES)
                        merged(g, inv_q, MERGES)
                        for j in range(PAIRS):
                            mm = pe.matmul(bank[2 * g][:, j * P:(j + 1) * P], QI[g][:, j, :],
                                           XM[g][:, j, :], start=True, stop=True)
                        mm.then_inc(inv_y, 1)
                    for g in range(4):
                        merged(g, inv_t, MERGES + 4, 4)
                        for j in range(PAIRS):
                            mm = pe.transpose(bank[2 * g + 1][:, j * P:(j + 1) * P], TI[g][:, j, :], IDENT)
                        mm.then_inc(inv_turned, 1)
                pe.wait_ge(inv_q, c * MERGES + (MERGES + 4))
                by_heads(0, QI[0:2], X1R, True, True).then_inc(f_u1, 1)
                by_heads(1, QI[2:4], VG, True, True).then_inc(f_y1, 1)
                by_state(4, QC, SG, False).then_inc(f_qs, 1)
                by_state(2, RD, SR, True)
                by_heads(2, RK, VR, False, False)
                pe.wait_ge(r_u1, n)
                below(5, LT[0:2], X1R, TOP, True).then_inc(f_zr, 1)
                pe.wait_ge(r_y1, n)
                below(6, LT[2:4], VG, TOP, True).then_inc(f_zg, 1)
                pe.wait_ge(r_zr, n)
                below(0, QI[0:2], X1R, LOW, False).then_inc(f_u, 1)
                pe.wait_ge(r_zg, n)
                below(1, QI[2:4], VG, LOW, False).then_inc(f_y, 1)
                pe.wait_ge(r_u, n)
                by_heads(2, RBM, UN, False, True).then_inc(f_or, 1)
                pe.wait_ge(r_y, n)
                by_heads(3, GRK, VN, True, True).then_inc(f_og, 1)
                for j in range(PAIRS):
                    cols = slice(j * P, (j + 1) * P)
                    pe.matmul(bank[5][:, cols], KTOK[:, cols], VR[:, cols], start=(j == 0),
                              stop=False, skip_group_check=True)
                    mm = pe.matmul(bank[5][:, cols], BTOK[:, cols], UN[:, cols], start=False,
                                   stop=True, skip_group_check=True)
                mm.then_inc(f_sr, 1)
                for j in range(PAIRS):
                    cols = slice(j * P, (j + 1) * P)
                    mm = pe.matmul(bank[6][:, cols], KGT[:, cols], VN[:, cols], start=True, stop=True)
                mm.then_inc(f_sg, 1)
                pe.wait_ge(e_on, n)
                turn_wide(7, OR, f_tr)
                pe.wait_ge(e_og, n)
                turn_wide(0, OG, f_tg)
                pe.wait_ge(r_tg, n)
                pe.wait_ge(e_state, n)

            def products(o, pairs, waits=None):
                n_ = len(pairs)
                for i_, (k, wh, wl, xh, xl) in enumerate(pairs):
                    if waits is not None:
                        waits[0](k)
                    pe.matmul(o, wh, xh, start=(i_ == 0), stop=False)
                    pe.matmul(o, wl, xh, start=False, stop=False)
                for i_, (k, wh, wl, xh, xl) in enumerate(pairs):
                    if waits is not None:
                        waits[1](k)
                    mm = pe.matmul(o, wh, xl, start=False, stop=(i_ == n_ - 1))
                return mm

            def split_unit(u, q, xh, xl, dyn_u=0, dyn_q=0, waits=None):
                pe.wait_ge(lo_ready, dyn_u + (u + 1))
                for b in range(2):
                    cols = slice(b * P, (b + 1) * P)
                    products(take(q + b, dyn_q)[:, :],
                             [(k, WH[:, u % 2, k, cols], WL[:, u % 2, k, cols], xh[:, k, :], xl[:, k, :])
                              for k in range(KT)], waits if b == 0 else None).then_inc(bank_filled, 1)

            def normed_split(n):
                return (lambda k: pe.wait_ge(h_hi, KT * (n - 1) + k + 1),
                        lambda k: pe.wait_ge(h_lo, KT * (n - 1) + k + 1))

            def mlp(l):
                with pe.Fori(0, 4) as i:
                    for v in range(4):
                        split_unit(u_mlp[l] + v, q_m1[l] + 2 * v, HH, HL, i * 8, i * 16,
                                   normed_split(2 * l + 1) if v == 0 else None)
                    hidden = (lambda k: pe.wait_ge(h1_ready, i * 8 + (32 * l + 4 + k + 1)),
                              lambda k: pe.wait_ge(h1_ready, i * 8 + (32 * l + 4 + k + 1)))
                    for v in range(4):
                        split_unit(u_mlp[l] + 4 + v, q_m2[l] + 2 * v, AH, AL, i * 8, i * 16,
                                   hidden if v == 0 else None)

            def projected(l, xh, xl, waits):
                for v in range(4):
                    split_unit(u_out[l] + v, q_out[l] + 2 * v, xh, xl, waits=waits if v == 0 else None)
                norm(2 * l + 1)
                mlp(l)

            projected(0, HH, HL, (lambda k: pe.wait_ge(mix_hi, 1 + k // 4),
                                  lambda k: pe.wait_ge(mix_lo, 1 + k // 4)))

            norm(2)
            split_unit(u_kv, q_k, HH, HL, waits=normed_split(2))
            u = u_kv + 1
            pe.wait_ge(lo_ready, u + 1)
            products(take(q_ik)[:, :], [(k, WH[:, u % 2, k, 0:P], WL[:, u % 2, k, 0:P], HH[:, k, :],
                                         HL[:, k, :]) for k in range(KT)]).then_inc(bank_filled, 1)

            def token_major(o, i, wh, wl):
                rows = slice(i * P, (i + 1) * P)
                return products(o, [(k, HH[:, k, rows], HL[:, k, rows], wh[:, k, :], wl[:, k, :])
                                    for k in range(KT)])

            for v in range(2):
                o = take(q_v + v)
                for i in range(2):
                    mm = token_major(o[:, i * VIW:(i + 1) * VIW], 2 * v + i, WH[:, u % 2, :, P:USLOT],
                                     WL[:, u % 2, :, P:USLOT])
                mm.then_inc(bank_filled, 1)
            for v in range(2):
                split_unit(u_iq + v, q_iq + 2 * v, HH, HL)

            def mv(v):
                u = u_mv + v
                pe.wait_ge(lo_ready, u + 1)
                for i in range(TT):
                    token_major(take(q_mv[v] + i)[:, 0:UW], i, WH[:, u % 2, :, 0:UW],
                                WL[:, u % 2, :, 0:UW])\
                        .then_inc(bank_filled, 1)

            pe.wait_ge(bank_read, q_ik + 1)
            pe.matmul(take(q_ikm)[:, :], HEADS2, L1[:, 20, :], start=True, stop=True).then_inc(bank_filled, 1)
            mv(0)
            pe.wait_ge(n_sq, 1)
            pe.matmul(take(q_ikv)[:, :], HEADS2, SQ1[0][:, 0, :], start=True, stop=True).then_inc(bank_filled, 1)
            mv(1)
            pe.wait_ge(n_used, 1)
            u = 0
            for i in range(1, TT):
                for hh in range(NH):
                    p, j = hh % 2, hh // 2
                    pe.matmul(take(q_idx + u)[:, 0:P * (i + 1)],
                              L1[p * HD:(p + 1) * HD, 16 + j, i * P:(i + 1) * P],
                              L1[p * HD:(p + 1) * HD, 20, 0:P * (i + 1)],
                              start=True, stop=True).then_inc(bank_filled, 1)
                    u += 1
            def head_sums(n, q, x):
                pe.wait_ge(n_sq, n)
                for t in range(x.shape[1]):
                    pe.matmul(take(q + t)[:, :], HEADS2, x[:, t, :], start=True, stop=True)\
                        .then_inc(bank_filled, 1)

            for v in range(2):
                split_unit(u_dq + v, q_dq + 2 * v, HH, HL)
            head_sums(2, q_k2n, SQK)
            for v in range(2):
                split_unit(u_mqk + v, q_mq + 2 * v, HH, HL)
            head_sums(3, q_dqn, SQ1[0])
            for v in range(2):
                split_unit(u_mqk + 2 + v, q_mk + 2 * v, HH, HL)
            head_sums(4, q_mqn, SQ1[1])
            head_sums(5, q_mkn, SQ1[0])
            pe.wait_ge(n_used, 5)
            pe.wait_ge(bank_read, q_mix)

            with pe.Fori(0, PAIRS) as b:
                def scores(w):
                    i, p, u = w // 2 % 4, w % 2, w // 8
                    if w % 8 == 0:
                        pe.wait_ge(at_stage, b * 2 + (u + 1))
                    pe.wait_ge(at_z, b * 16 + (8 + w + 1))
                    pe.matmul(bank[w % 4][:, 0:P * (i + 1)],
                              QS[p * HD:(p + 1) * HD, u, i * P:(i + 1) * P],
                              KS[p * HD:(p + 1) * HD, u, 0:P * (i + 1)],
                              start=True, stop=True).then_inc(at_qk, 1)

                def turned(w):
                    i = w // 2 % 4
                    pe.wait_ge(at_p, b * 16 + (w + 1))
                    pe.wait_ge(at_pt, b * 16 + (w + 1))
                    for s in range(i + 1):
                        mm = pe.transpose(bank[4 + w % 2][:, s * P:(s + 1) * P],
                                          ZB[:, w % 8, s * P:(s + 1) * P], IDENT)
                    mm.then_inc(at_t, 1)

                def values(w):
                    i, p, u = w // 2 % 4, w % 2, w % 8
                    if u == 0:
                        pe.wait_ge(at_on, b * 2 + 1)
                    pe.wait_ge(at_pt, b * 16 + (w + 3))
                    for s in range(i + 1):
                        v = VALL[:, s, bass.ds(b * 256 + (w // 8 * 128 + p * HD), HD)]
                        mm = pe.matmul(bank[6 + w // 8][:, u * HD:(u + 1) * HD],
                                       PTS[:, w % 3, s * P:(s + 1) * P], v,
                                       start=(s == 0), stop=(s == i))
                    mm.then_inc(at_o, 1)

                for w in range(4):
                    scores(w)
                for w in range(16):
                    if w + 4 < 16:
                        scores(w + 4)
                    if w >= 2:
                        values(w - 2)
                    turned(w)
                values(14)
                values(15)
            pe.wait_ge(at_on, 9)
            for k in range(KT):
                o = bank[(q_mix + k) % 8]
                for i in range(TT):
                    mm = pe.transpose(o[:, i * P:(i + 1) * P], ON[:, i, k * P:(k + 1) * P], IDENT)
                mm.then_inc(bank_filled, 1)
            projected(1, AH, AL, (lambda k: pe.wait_ge(mix_hi, 2 + k + 1),
                                  lambda k: pe.wait_ge(bank_read, q_mix + k + 1)))
            pe.wait_ge(bank_read, q_fin)
            for i in range(TT):
                for half_ in range(2):
                    o = take(q_fin + 2 * i + half_)
                    for b in range(4):
                        mm = pe.transpose(o[:, b * P:(b + 1) * P],
                                          XT[:, half_ * 4 + b, i * P:(i + 1) * P], IDENT)
                    mm.then_inc(bank_filled, 1)

        @block.scalar
        def _(act):
            t = Tally(act, act_step)

            def filled(q, dyn=0):
                act.wait_ge(bank_filled, dyn + (q + 1))

            def src(q):
                return bank[q % 8]

            def rows(dst, vec):
                act.dma_start(dst, vec).then_inc(dma_par, 16)

            act.dma_start(XIN[:, 2:4, :], x_rows[:, 2:4, :]).then_inc(dma_x, 16)
            rows(PR[0:16, :], a["norm1_g"].rearrange("l (c p) -> (l c) p", p=P))
            rows(PR[16:32, :], a["norm2_g"].rearrange("l (c p) -> (l c) p", p=P))
            r = 32
            for name in ("rwkv_mu", "rwkv_w0", "rwkv_a0", "rwkv_k_k", "rwkv_k_a", "rwkv_r_k",
                         "rwkv_lnx_w", "rwkv_lnx_b"):
                v = a[name]
                v = v.rearrange("o (c a) n -> (o c) (a n)", a=2) if name == "rwkv_r_k" else \
                    v.rearrange("o (c p) -> (o c) p", p=P)
                rows(PR[r:r + v.shape[0], :], v)
                r += v.shape[0]
            rows(PR[74:122, :], a["gdn_conv_w"][0].rearrange("j (b p) -> (j b) p", p=P))
            for i, name in enumerate(PAR64):
                rows(PR2[i:i + 1, :].rearrange("p (h d) -> p h d", h=2),
                     a[name].unsqueeze(1).broadcast_to([1, 2, HD]))
            for dst, vec in ((ALOG, a["gdn_a_log"].broadcast_to([P, NH])),
                             (DTB, a["gdn_dt_bias"].broadcast_to([P, NH])),
                             (LW2[0:HD, :], a["rwkv_w2"][0]), (LW2[HD:P, :], a["rwkv_a2"][0]),
                             (G2, a["rwkv_g2"][0])):
                act.dma_start(dst, vec).then_inc(dma_late, 16)

            def norm(n, ready, between=lambda k: None):
                for k in range(KT):
                    act.wait_ge(bank_read, ready + k + 1)
                    act.activation(SQ[n][:, k, :], XT[:, k, :], ACT.Square).then_inc(squares, 1)
                    between(k)
                filled(q_norm[n])
                act.wait_ge(bank_read, q_norm[n])
                act.activation(RS[n], src(q_norm[n])[:, :], ACT.Ln, bias=RMS_EPS, scale=1.0 / D)\
                   .then_inc(bank_read, 1)
                act.wait_ge(bank_read, q_norm[n] + 1)
                act.activation(RS[n], RS[n], ACT.Exp, scale=-0.5).then_inc(rms, 1)

            def weight_hi(u, dyn=0, q_done=None, dyn_q=0):
                act.wait_ge(raw_full[u % 2], dyn + raw_count(u))
                if q_done is not None:
                    filled(q_done, dyn_q)
                w = unit_cols(u)
                act.activation(WH[:, u % 2, :, 0:w], RAW[:, u % 2, :, 0:w], ACT.Copy).then_inc(hi_ready, 1)

            def h_split(n):
                for k in range(KT):
                    act.wait_ge(h_ready, KT * n + k + 1)
                    act.activation(HH[:, k, :], SQ[n][:, k, :], ACT.Copy).then_inc(h_hi, 1)

            norm(0, q_x)

            act.wait_ge(pads_zero, 1)
            for b in range(2):
                filled(q_lora + b)
                act.activation(STAGE[0][:, b, 3:3 + W], src(q_lora + b)[:, :], ACT.Copy)\
                   .then_inc(bank_read, 1)
            filled(q_ab)
            act.activation(wide(AB), src(q_ab)[:, 0:64], ACT.Copy).then_inc(bank_read, 1)
            for b in range(4):
                filled(q_z + b)
                act.activation(Z[:, b, :], src(q_z + b)[:, :], ACT.Silu).then_inc(bank_read, 1)
            act.wait_ge(lora_shifted, 2)
            act.activation(WA[0:HD, :], WA[0:HD, :], ACT.Tanh).then_inc(lora_act, 1)
            act.activation(GD, GD, ACT.Sigmoid).then_inc(lora_act, 1)
            act.wait_ge(bank_read, q_ab + 1)
            act.activation(BETA, AB[:, :, 0:NH], ACT.Sigmoid)
            for c in range(4):
                filled(q_w + c)
                act.activation(BON[:, c, :], src(q_w + c)[:, :], ACT.Sigmoid, bias=pc("w0", c))\
                   .then_inc(bank_read, 1)
            for c in range(4):
                filled(q_a + c)
                act.activation(B[:, c, :], src(q_a + c)[:, :], ACT.Sigmoid, bias=pc("a0", c))\
                   .then_inc(bank_read, 1)
            for c in range(4):
                filled(q_g + c)
                act.activation(G[:, c, :], src(q_g + c)[:, :], ACT.Copy).then_inc(bank_read, 1)

            act.wait_ge(gate_in, 1)
            t.link(act.activation(wide(GLOG), wide(GTMP), ACT.Abs))
            t.link(act.activation(wide(GLOG), wide(GLOG), ACT.Exp, scale=-1.0))
            act.wait_ge(dma_late, 16 * 5)
            act.activation(NEA, ALOG, ACT.Exp)
            act.activation(wide(GLOG), wide(GLOG), ACT.Ln, bias=1.0).then_inc(gate_ln, 1)

            with act.Fori(0, 3) as i:
                for s in range(2):
                    for b in range(4):
                        filled(q_pair + 4 * s + b, i * 8)
                        if s == 0:
                            act.wait_ge(stage_used, i * 4 + (b + 1))
                        act.activation(STAGE[s][:, b, 3:3 + W], src(q_pair + 4 * s + b)[:, :],
                                       ACT.Copy).then_inc(bank_read, 1)
                for b in range(4):
                    act.wait_ge(conv_out, i * 4 + (b + 1))
                    act.activation(GQKV[:, bass.ds(i * 4 + b, 1), :].rearrange("p a w -> p (a w)"),
                                   CONV[:, b, :], ACT.Silu).then_inc(conv_used, 1)

            act.wait_ge(conv_used, 4 + 12)
            act.wait_ge(stage_used, 4 + 12)
            norms = ((q_kk, KK, SQA), (q_gq, GQ, SQB), (q_gk, GK, SQC))
            act.wait_ge(kk_ready, 4)
            for q, x, sq in norms:
                act.activation(wide(sq), wide(x), ACT.Square).then_inc(sq_grp, 1)
            for q, x, sq in norms:
                for c in range(4):
                    filled(q + c)
                    act.activation(sq[:, c, :], src(q + c)[:, :], ACT.Ln, bias=1e-6)\
                       .then_inc(bank_read, 1)
                act.wait_ge(bank_read, q + 4)
                act.activation(wide(sq), wide(sq), ACT.Exp, scale=-0.5).then_inc(rs_grp, 1)
            act.wait_ge(gcum_ready, 1)
            act.activation(wide(EG), wide(GCUM), ACT.Exp)
            act.activation(wide(EREST), wide(EREST), ACT.Exp)
            for p in range(2):
                part = slice(p * HD, (p + 1) * HD)
                last = act.activation(
                    ESTATE[part, :, :],
                    src(q_cum)[part, 32:64].rearrange("p (c j q) -> p c j q", c=TT, q=2)[:, :, :, p],
                    ACT.Exp)
            last.then_inc(l0_act, 1)

            act.wait_ge(l0_dve, 1)
            act.sem_inc(inv_q, 4)
            with act.Fori(0, TT) as c:
                n = c + 1
                act.wait_ge(e_diff, n)
                act.activation(wide(KD), wide(RD), ACT.Exp, scale=-1.0)
                with t.loop(c, 1, TT):
                    t.link(act.activation(wide(BD), wide(RD), ACT.Exp, scale=-1.0))
                act.activation(wide(RD), wide(RD), ACT.Exp)
                act.activation(wide(AD), wide(AD), ACT.Exp)
                act.activation(ESM, SM, ACT.Exp).then_inc(e_exp, 1)
                act.wait_ge(f_vg, n)
                act.activation(VG, bank[3][:, :], ACT.Copy).then_inc(r_vg, 1)
                act.wait_ge(f_vr, n)
                act.activation(VR, bank[4][:, :], ACT.Copy).then_inc(r_vr, 1)
                act.wait_ge(e_dsub, n)
                for p in range(2):
                    last = act.activation(wide(DT[p]), wide(DT[p]), ACT.Exp)
                last.then_inc(e_dt, 1)
                act.wait_ge(f_lt, n)
                for p in range(2):
                    last = act.activation(wide(LT[p]), bank[3 + p][:, :], ACT.Copy)
                last.then_inc(r_lt, 1)
                act.wait_ge(f_ktok, n)
                act.activation(KTOK, bank[3][:, :], ACT.Copy).then_inc(r_ktok, 1)
                act.wait_ge(f_btok, n)
                act.activation(BTOK, bank[4][:, :], ACT.Copy).then_inc(r_btok, 1)
                act.wait_ge(f_x1, n)
                act.activation(X1R, bank[0][:, :], ACT.Copy).then_inc(r_x1, 1)
                with act.Fori(0, LEVELS - 1) as lev:
                    for g in range(4):
                        act.wait_ge(inv_turned, c * MERGES + (lev * 4 + (g + 1)))
                        act.activation(wide(QI[g]), bank[2 * g + 1][:, :], ACT.Copy).then_inc(inv_q, 1)
                act.wait_ge(f_u1, n)
                act.activation(X1R[0:HD, :], bank[0][0:HD, :], ACT.Copy).then_inc(r_u1, 1)
                act.wait_ge(f_zr, n)
                act.activation(X1R[HD:P, :], bank[5][HD:P, :], ACT.Copy, scale=-1.0).then_inc(r_zr, 1)
                act.wait_ge(f_u, n)
                act.activation(UN, bank[0][:, :], ACT.Copy, scale=-1.0).then_inc(r_u, 1)
                for g, eps in ((0, GN_EPS), (1, RMS_EPS)):
                    cols = slice(g * NH, (g + 1) * NH)
                    act.wait_ge(e_var, 2 * c + (g + 1))
                    act.activation(RSTD[:, cols], VAR[:, cols], ACT.Ln, bias=eps, scale=1.0 / HD)\
                       .then_inc(e_ln, 1)
                    act.wait_ge(e_ln, 2 * c + (g + 1))
                    act.activation(RSTD[:, cols], RSTD[:, cols], ACT.Exp, scale=-0.5)\
                       .then_inc(e_rstd, 1)
                here = bass.ds(c * P, P)
                act.wait_ge(f_tr, n)
                for j in range(4):
                    last = act.activation(R[:, j, here], bank[7][:, j * P:(j + 1) * P], ACT.Identity,
                                          bias=pc("lnx_b", j), scale=pc("lnx_w", j))
                last.then_inc(r_tr, 1)
                act.wait_ge(f_tg, n)
                act.activation(GQ[:, :, here], bank[0][:, :].rearrange("p (j t) -> p j t", j=4),
                               ACT.Copy, scale=pc2(GDNN)).then_inc(r_tg, 1)

            def norm_and_weights(l, n):
                def between(k):
                    if k % 2 == 1:
                        weight_hi(u_out[l] + k // 2 + 2, q_done=q_out[l] + k)

                norm(n, q_out[l], between)
                h_split(n)

            def mlp(l):
                def quarter(i, units):
                    for v in range(8):
                        if v < 4:
                            for b in (2 * v, 2 * v + 1):
                                if b == 0:
                                    act.wait_ge(bank_read, i * 16 + q_m1[l])
                                filled(q_m1[l] + b, i * 16)
                                act.wait_ge(h1_ready, i * 8 + (32 * l + b + 1))
                                act.activation(SQT[:, b % 4, :], src(q_m1[l] + b)[:, :], ACT.Relu)\
                                   .then_inc(bank_read, 1)
                        if v < units:
                            weight_hi(u_mlp[l] + 2 + v, i * 64, q_m1[l] + 2 * v + 1, i * 16)

                with act.Fori(0, 3) as i:
                    quarter(i, 8)
                quarter(3, 6)

            act.wait_ge(e_state, TT)
            weight_hi(0)
            act.wait_ge(mix_ready, 1)
            act.activation(HH[:, 0:4, :], R, ACT.Copy).then_inc(mix_hi, 1)
            act.wait_ge(mix_ready, 2)
            act.activation(HH[:, 4:8, :], GQ, ACT.Copy).then_inc(mix_hi, 1)
            weight_hi(1)
            norm_and_weights(0, 1)
            mlp(0)
            norm(2, q_norm[2] - 8,
                 lambda k: weight_hi(u_kv + (k - 5) // 2, q_done=q_norm[2] - 8 + k) if k in (5, 7) else None)
            h_split(2)

            for q, tile in ((q_k, 8), (q_k + 1, 10), (q_ik, 20)):
                filled(q)
                act.activation(L1[:, tile, :], src(q)[:, :], ACT.Copy).then_inc(bank_read, 1)
                if q == q_k + 1:
                    weight_hi(u_iq, q_done=q)
            for v in range(2):
                filled(q_v + v)
                for i in range(2):
                    vin = src(q_v + v)[:, i * VIW:i * VIW + P].rearrange("p (g d) -> p g d", g=2)
                    act.activation(VALL[:, 2 * v + i, 0:512].rearrange("p (g r d) -> p g r d", g=2, r=4),
                                   vin.unsqueeze(2).broadcast_to([P, 2, 4, HD]), ACT.Copy)
                act.activation(IW[:, 2 * v:2 * v + 2, :],
                               src(q_v + v)[:, 0:2 * VIW].rearrange("p (i c) -> p i c", i=2)[:, :, P:VIW],
                               ACT.Copy, scale=float(NH) ** -0.5).then_inc(bank_read, 1)
            weight_hi(u_iq + 1, q_done=q_v + 1)

            def evacuate(q, tile):
                filled(q)
                act.activation(L1[:, tile, :], src(q)[:, :], ACT.Copy).then_inc(bank_read, 1)

            for v in range(2):
                for b in range(2):
                    evacuate(q_iq + 2 * v + b, 16 + 2 * v + b)
                weight_hi(u_mv + v, q_done=q_iq + 2 * v + 1)
            act.wait_ge(ik_centred, 1)
            act.activation(SQ1[0][:, 0, :], L1[:, 20, :], ACT.Square).then_inc(n_sq, 1)

            def mv(v):
                act.wait_ge(bank_read, q_mv[v])
                for i in range(TT):
                    filled(q_mv[v] + i)
                    act.activation(VALL[:, i, 512 + v * UW:512 + (v + 1) * UW],
                                   src(q_mv[v] + i)[:, 0:UW], ACT.Copy).then_inc(bank_read, 1)
                weight_hi(u_dq + v, q_done=q_mv[v] + 3)

            def inverse_rms(q, x):
                for c in range(x.shape[1]):
                    filled(q + c)
                    act.activation(x[:, c, :], src(q + c)[:, :], ACT.Ln, bias=RMS_EPS,
                                   scale=1.0 / HD).then_inc(bank_read, 1)
                act.wait_ge(bank_read, q + x.shape[1])
                act.activation(x, x, ACT.Exp, scale=-0.5).then_inc(n_rs, 1)

            mv(0)
            inverse_rms(q_ikv, SQ1[0][:, 0:1, :])
            mv(1)
            u = 0
            for i in range(1, TT):
                for hh in range(NH):
                    filled(q_idx + u)
                    if u >= 4:
                        act.wait_ge(idx_acc, u - 3)
                    act.activation(RT[:, u % 4, 0:P * (i + 1)], src(q_idx + u)[:, 0:P * (i + 1)],
                                   ACT.Relu, scale=float(HD) ** -0.5).then_inc(bank_read, 1)
                    u += 1
            act.activation(SQK, L1[:, 8:12:2, :], ACT.Square).then_inc(n_sq, 1)

            def project(u0, q0, tile):
                for v in range(2):
                    for b in range(2):
                        evacuate(q0 + 2 * v + b, tile + 2 * v + b)
                    weight_hi(u0 + 2 + v, q_done=q0 + 2 * v + 1)

            def squares_of(x, q_last, sq):
                act.wait_ge(bank_read, q_last + 1)
                act.activation(sq, x, ACT.Square).then_inc(n_sq, 1)

            project(u_dq, q_dq, 0)
            act.wait_ge(idx_acc, u)
            squares_of(L1[:, 0:4, :], q_dq + 3, SQ1[0])
            inverse_rms(q_k2n, SQK)
            project(u_mqk, q_mq, 4)
            squares_of(L1[:, 4:8, :], q_mq + 3, SQ1[1])
            inverse_rms(q_dqn, SQ1[0])
            project(u_mqk + 2, q_mk, 12)
            act.wait_ge(n_used, 3)
            squares_of(L1[:, 12:16, :], q_mk + 3, SQ1[0])
            inverse_rms(q_mqn, SQ1[1])
            inverse_rms(q_mkn, SQ1[0])

            act.wait_ge(n_used, 5)
            act.sem_inc(at_pt, 2)
            with act.Fori(0, PAIRS) as b:
                def probs(w):
                    wdt = P * (w // 2 % 4 + 1)
                    act.wait_ge(at_mx, b * 16 + (w + 1))
                    if w == 0:
                        act.wait_ge(at_on, b * 2 + 1)
                    act.activation(ZB[:, w % 8, 0:wdt], ZB[:, w % 8, 0:wdt], ACT.Exp,
                                   bias=NMX[:, w:w + 1], accum_out=RSUM[:, w:w + 1])\
                       .then_inc(at_p, 1)

                def out_turned(w):
                    wdt = P * (w // 2 % 4 + 1)
                    act.wait_ge(at_t, b * 16 + (w + 1))
                    if w >= 3:
                        act.wait_ge(at_o, b * 16 + (w - 2))
                    act.activation(PTS[:, w % 3, 0:wdt], bank[4 + w % 2][:, 0:wdt], ACT.Copy)\
                       .then_inc(at_pt, 1)

                for w in range(16):
                    probs(w)
                    if w >= 1:
                        out_turned(w - 1)
                out_turned(15)
            for k in range(KT):
                filled(q_mix + k)
                act.activation(AH[:, k, :], src(q_mix + k)[:, :], ACT.Copy).then_inc(mix_hi, 1)
            norm_and_weights(1, 3)
            mlp(1)
            for i in range(2 * TT):
                filled(q_fin + i)
                act.activation(OUTT[:, i // 2, (i % 2) * 512:(i % 2 + 1) * 512],
                               src(q_fin + i)[:, :], ACT.Copy).then_inc(bank_read, 1)

        @block.vector
        def _(dve):
            t = Tally(dve, dve_step)
            mul, add, sub = ALU.mult, ALU.add, ALU.subtract

            def filled(q, dyn=0):
                dve.wait_ge(bank_filled, dyn + (q + 1))

            def src(q):
                return bank[q % 8]

            dve.sem_inc(stage_used, 4)
            dve.sem_inc(h1_ready, 4)
            for k in range(KT):
                filled(q_x + k)
                dve.tensor_copy(XT[:, k, :], src(q_x + k)[:, :]).then_inc(bank_read, 1)
            filled(q_par)
            dve.tensor_copy(PC[:, 0:NPC], src(q_par)[:, 0:NPC]).then_inc(bank_read, 1)
            filled(q_par + 1)
            dve.tensor_copy(PC2[:, 0:7], src(q_par + 1)[:, 0:7]).then_inc(bank_read, 1)
            dve.wait_ge(bank_read, q_par + 2)
            dve.tensor_scalar(OMKA, PC[:, at["k_a"]:at["k_a"] + 4], -1.0, 1.0, mul, add)
            for i, col in enumerate((DQN, MQN)):
                dve.tensor_scalar(QW[:, i:i + 1], pc2(col), float(HD) ** -0.5, None, mul)

            def norm(n):
                dst = HT if n == 0 else SQ[n]
                dve.wait_ge(rms, n + 1)
                for k in range(KT):
                    g = pc("norm1" if n % 2 == 0 else "norm2", (n // 2) * KT + k)
                    dve.scalar_tensor_tensor(out=dst[:, k, :], in0=XT[:, k, :], scalar=g, in1=RS[n],
                                             op0=mul, op1=mul).then_inc(h_ready, 1)
                if n > 0:
                    for k in range(KT):
                        dve.wait_ge(h_hi, KT * (n - 1) + k + 1)
                        dve.tensor_tensor(HL[:, k, :], dst[:, k, :], as_f32(HH[:, k, :]), sub)\
                           .then_inc(h_lo, 1)

            norm(0)

            def shifted(dst, stage, mu):
                t.link(dve.tensor_tensor(TMPD, stage[:, 2:2 + W], stage[:, 3:3 + W], sub))
                return dve.scalar_tensor_tensor(out=dst, in0=TMPD, scalar=mu, in1=stage[:, 3:3 + W],
                                                op0=mul, op1=add)

            for b, dst in enumerate((WA, GD)):
                dve.wait_ge(bank_read, q_lora + b + 1)
                shifted(dst, STAGE[0][:, b, :], pc("mu", 12 + b)).then_inc(lora_shifted, 1)
                dve.wait_ge(lora_shifted, b + 1)
            dve.sem_inc(conv_used, 4)
            dve.wait_ge(dma_late, 16 * 5)
            dve.wait_ge(bank_read, q_ab + 1)
            dve.tensor_tensor(GTMP, AB[:, :, NH:2 * NH], DTB.unsqueeze(1).broadcast_to([P, TT, NH]),
                              add).then_inc(gate_in, 1)
            t.link(dve.memset(CUM[:, :, :, 0:1].rearrange("p c k o -> p (c k) o"), 0.0))
            for c in range(4):
                dve.wait_ge(bank_read, q_w + c + 1)
                t.link(dve.tensor_scalar(CUM[:, c, :, 1:CW],
                                         BON[:, c, :].rearrange("p (k t) -> p k t", k=4),
                                         -float(np.exp(-0.5)), None, mul))
                cum = CUM[:, c, :, :].rearrange("p k t -> p (k t)")
                t.link(dve.tensor_tensor_scan(cum, SCANM, cum, 0.0, mul, add))

            dve.wait_ge(gate_ln, 1)
            t.link(dve.scalar_tensor_tensor(out=wide(GTMP), in0=wide(GTMP), scalar=0.0, in1=wide(GLOG),
                                            op0=ALU.max, op1=add))
            dve.scalar_tensor_tensor(out=GLOG, in0=GTMP, scalar=-1.0,
                                     in1=NEA.unsqueeze(1).broadcast_to([P, TT, NH]),
                                     op0=mul, op1=mul).then_inc(glog_ready, 1)

            with dve.Fori(0, 3) as i:
                with t.loop(i, 4 + 12, 3):
                    for b in range(4):
                        dve.wait_ge(bank_read, i * 8 + (q_pair + b + 1))
                        mu = PC[:, bass.ds(i * 4 + (at["mu"] + b), 1)]
                        dst = RKV[:, bass.ds(i * 4 + b, 1), :].rearrange("p a w -> p (a w)")
                        shifted(dst, STAGE[0][:, b, :], mu).then_inc(stage_used, 1)
                        dve.wait_ge(stage_used, i * 4 + (4 + b + 1))
                    for b in range(4):
                        dve.wait_ge(bank_read, i * 8 + (q_pair + 4 + b + 1))
                        dve.wait_ge(conv_used, i * 4 + (b + 1))
                        for tap in range(4):
                            wgt = PC[:, bass.ds(i * 4 + (at["conv"] + 12 * tap + b), 1)]
                            x = STAGE[1][:, b, tap:tap + W]
                            if tap == 0:
                                ins = dve.tensor_scalar(CONV[:, b, :], x, wgt, None, mul)
                            else:
                                ins = dve.scalar_tensor_tensor(out=CONV[:, b, :], in0=x, scalar=wgt,
                                                               in1=CONV[:, b, :], op0=mul, op1=add)
                            if tap < 3:
                                t.link(ins)
                            else:
                                ins.then_inc(conv_out, 1)
                        dve.wait_ge(conv_out, i * 4 + (b + 1))
            for c in range(4):
                dve.tensor_scalar(KK[:, c, :], K[:, c, :], pc("k_k", c), None, mul).then_inc(kk_ready, 1)
            dve.wait_ge(kk_ready, 4)
            for c in range(4):
                t.link(dve.tensor_scalar(TMPD, B[:, c, :], pc("k_a", c), OMKA[:, c:c + 1], mul, add))
                t.link(dve.tensor_tensor(K[:, c, :], K[:, c, :], TMPD, mul))
            for c in range(4):
                dve.scalar_tensor_tensor(out=BON[:, c, :], in0=R[:, c, :], scalar=pc("r_k", c),
                                         in1=K[:, c, :], op0=mul, op1=mul).then_inc(bonus_in, 1)
            dve.wait_ge(rs_grp, 1)
            t.link(dve.tensor_tensor(wide(KK), wide(KK), wide(SQA), mul))
            t.step(dve.tensor_tensor(wide(B), wide(KK), wide(B), mul))
            dve.wait_ge(rs_grp, 2)
            t.step(dve.scalar_tensor_tensor(out=wide(GQ), in0=wide(GQ), scalar=float(HD) ** -0.5,
                                            in1=wide(SQB), op0=mul, op1=mul))
            dve.wait_ge(rs_grp, 3)
            t.link(dve.tensor_tensor(wide(GK), wide(GK), wide(SQC), mul))
            for c in range(4):
                filled(q_bon + c)
                dve.tensor_tensor(BON[:, c, :], src(q_bon + c)[:, :], V[:, c, :], mul)\
                   .then_inc(bank_read, 1)
            filled(q_cum)
            t.link(dve.tensor_copy(wide(GCUM), src(q_cum)[:, 0:32]))
            dve.tensor_tensor(wide(EREST), src(q_cum)[:, 32:64], wide(GCUM), sub).then_inc(gcum_ready, 1)
            dve.wait_ge(l0_act, 1)
            dve.wait_ge(gcum_ready, 1)
            dve.tensor_copy(VAR[:, 0:1], PC[:, 0:1]).then_inc(l0_dve, 1)
            dve.sem_inc(bank_read, 1)

            def bc(x, n=P):
                return x.unsqueeze(2).broadcast_to([P, x.shape[1], n])

            def by_parity(x, p):
                return x.rearrange("p o (j q) -> p (o j) q", q=2)[:, :, p]

            def bank4(b):
                return bank[b][:, :].rearrange("p (j t) -> p j t", j=4)

            def heads(x):
                return x.rearrange("p (h d) -> p h d", h=NH)

            def mask4(m):
                return m.unsqueeze(1).broadcast_to([P, 4, P])

            dve.wait_ge(l0_dve, 1)
            with dve.Fori(0, TT) as c:
                n = c + 1
                here = bass.ds(c * P, P)
                row = bass.ds(c, 1)

                def row_of(x):
                    return x[:, row, :].rearrange("p a h -> p (a h)")

                with t.loop(c, DVE_CHUNK, TT):
                    mid = CUM[:, :, row, P // 2:P // 2 + 1].rearrange("p c k o -> p c (k o)")
                    chunk_cum = CUM[:, :, row, :].rearrange("p c k t -> p c (k t)")
                    midb = mid.broadcast_to([P, 4, P])
                    t.link(dve.tensor_tensor(RD, chunk_cum[:, :, 1:CW], midb, sub))
                    dve.tensor_tensor(AD, chunk_cum[:, :, 0:P], midb, sub)
                    dve.tensor_copy(SM[:, 0:4].unsqueeze(2), mid)
                    dve.tensor_copy(SM[:, 4:8].unsqueeze(2), RD[:, :, P - 1:P]).then_inc(e_diff, 1)
                    dve.wait_ge(f_grow, n)
                    for p in range(2):
                        gs = by_parity(GCUM[:, row, :], p)
                        t.step(dve.tensor_tensor(DT[p], bank4(p), bc(gs), sub))
                    t.settle()
                    for p in range(2):
                        ins = dve.tensor_scalar(wide(DT[p]), wide(DT[p]), 0.0, None, ALU.min)
                    ins.then_inc(e_dsub, 1)
                    dve.wait_ge(f_kt, n)
                    dve.tensor_tensor(heads(KGT), heads(bank[2][:, :]), bc(row_of(EREST), HD), mul)\
                       .then_inc(r_kt, 1)
                    dve.wait_ge(e_exp, n)
                    dve.tensor_tensor(RD, RD, R[:, :, here], mul)
                    dve.tensor_tensor(KD, KD, K[:, :, here], mul).then_inc(e_rk, 1)
                    dve.tensor_tensor(SR, SR, bc(ESM[:, 0:4]), mul).then_inc(e_s0, 1)
                    dve.wait_ge(e_dt, n)
                    for p in range(2):
                        t.step(dve.tensor_tensor(GRK[p], DT[p], mask4(INCL), mul))
                    t.settle()
                    dve.wait_ge(e_dmask, n)
                    dve.wait_ge(f_kk, n)
                    for p in range(2):
                        ins = dve.tensor_tensor(LT[2 + p], bank4(5 + p), LT[2 + p], mul)
                    ins.then_inc(r_kk, 1)
                    dve.wait_ge(f_kq, n)
                    for p in range(2):
                        ins = dve.tensor_tensor(GRK[p], bank4((7, 2)[p]), GRK[p], mul)
                    ins.then_inc(r_kq, 1)
                    for f, dst, banks, m, r_ in ((f_mk, MK, (0, 1), STRICT, r_mk),
                                                 (f_rk, RK, (5, 6), INCL, r_rk),
                                                 (f_rb, RBM, (7, 2), INCL, r_rb)):
                        dve.wait_ge(f, n)
                        for p in range(2):
                            ins = dve.tensor_tensor(dst[p], bank4(banks[p]), mask4(m), mul)
                        ins.then_inc(r_, 1)
                    for g in range(2, 4):
                        t.step(dve.tensor_tensor(QI[g], LT[g], mask4(MERGE[:, 0, :]), mul))
                    t.settle()
                    for g in range(2, 4):
                        dve.tensor_tensor(QI[g], QI[g], mask4(IDENT), add).then_inc(inv_q1, 1)
                    dve.wait_ge(f_ks, n)
                    dve.wait_ge(r_vg, n)
                    t.link(dve.tensor_tensor(heads(TMPK), heads(bank[1][:, :]), bc(row_of(EG), HD), mul))
                    dve.tensor_tensor(VG, VG, TMPK, sub).then_inc(r_ks, 1)
                    for g in range(4):
                        dve.wait_ge(inv_first, c * 4 + (g + 1))
                        dve.tensor_copy(TI[g], bank4(2 * g)).then_inc(inv_t, 1)
                    with dve.Fori(0, LEVELS - 1) as lev:
                        for g in range(4):
                            dve.wait_ge(inv_x, c * MERGES + (lev * 4 + (g + 1)))
                            m = MERGE[:, bass.ds(lev + 1, 1), :].broadcast_to([P, 4, P])
                            dve.tensor_tensor(XM[g], bank4(2 * g), m, mul).then_inc(inv_xs, 1)
                        for g in range(4):
                            dve.wait_ge(inv_y, c * MERGES + (lev * 4 + (g + 1)))
                            dve.tensor_tensor(TI[g], TI[g], bank4(2 * g), sub).then_inc(inv_t, 1)
                    dve.wait_ge(f_y1, n)
                    dve.tensor_copy(VG[0:HD, :], bank[1][0:HD, :]).then_inc(r_y1, 1)
                    dve.wait_ge(f_zg, n)
                    dve.tensor_scalar(VG[HD:P, :], bank[6][HD:P, :], -1.0, None, mul).then_inc(r_zg, 1)
                    dve.wait_ge(f_y, n)
                    dve.tensor_tensor(heads(VN), heads(bank[1][:, :]), bc(row_of(BETA), HD), mul)\
                       .then_inc(r_y, 1)
                    dve.wait_ge(f_or, n)
                    o_r = heads(bank[2][:, :])
                    t.link(dve.tensor_reduce(NMEAN, o_r, AX.X, add, negate=True))
                    t.link(dve.tensor_scalar(NMEAN, NMEAN, 1.0 / HD, None, mul))
                    t.link(dve.tensor_tensor(heads(OR), o_r, bc(NMEAN, HD), add))
                    t.link(dve.tensor_tensor(OSQ, OR, OR, mul))
                    dve.tensor_reduce(VAR[:, 0:NH], heads(OSQ), AX.X, add).then_inc(e_var, 1)
                    dve.wait_ge(f_og, n)
                    dve.wait_ge(f_qs, n)
                    t.link(dve.tensor_tensor(heads(TMPG), heads(bank[4][:, :]), bc(row_of(EG), HD), mul))
                    t.link(dve.tensor_tensor(OG, TMPG, bank[3][:, :], add))
                    t.link(dve.tensor_tensor(OSQG, OG, OG, mul))
                    dve.tensor_reduce(VAR[:, NH:2 * NH], heads(OSQG), AX.X, add).then_inc(e_var, 1)
                    dve.wait_ge(e_rstd, 2 * c + 1)
                    dve.tensor_tensor(heads(OR), heads(OR), bc(RSTD[:, 0:NH], HD), mul).then_inc(e_on, 1)
                    dve.wait_ge(e_rstd, 2 * c + 2)
                    dve.tensor_tensor(heads(OG), heads(OG), bc(RSTD[:, NH:2 * NH], HD), mul).then_inc(e_og, 1)
                    dve.wait_ge(f_sr, n)
                    t.link(dve.tensor_tensor(TMPS, bank4(5), mask4(HEADS2), mul))
                    t.link(dve.tensor_tensor(SR, SR, TMPS, add))
                    t.link(dve.tensor_tensor(SR, SR, bc(ESM[:, 4:8]), mul))
                    dve.wait_ge(f_sg, n)
                    t.link(dve.tensor_tensor(TMPS, bank4(6), mask4(HEADS2), mul))
                    t.link(dve.tensor_tensor(SG, SG, bc(row_of(ESTATE)), mul))
                    dve.tensor_tensor(SG, SG, TMPS, add).then_inc(e_state, 1)
                    dve.wait_ge(e_state, n)
            dve.wait_ge(r_tg, TT)
            t.link(dve.tensor_tensor(wide(R), wide(R), wide(BON), add))
            dve.tensor_tensor(wide(R), wide(R), wide(G), mul).then_inc(mix_ready, 1)
            dve.tensor_tensor(wide(GQ), wide(GQ), wide(Z), mul).then_inc(mix_ready, 1)
            for i, x in enumerate((R, GQ)):
                k = slice(4 * i, 4 * i + 4)
                dve.wait_ge(mix_hi, i + 1)
                dve.tensor_tensor(HL[:, k, :], x, as_f32(HH[:, k, :]), sub).then_inc(mix_lo, 1)

            def residual(q):
                for k in range(KT):
                    filled(q + k)
                    dve.tensor_tensor(XT[:, k, :], XT[:, k, :], src(q + k)[:, :], add).then_inc(bank_read, 1)

            def mlp(l):
                with dve.Fori(0, 4) as i, t.loop(i, 16, 4):
                    for b in range(8):
                        dve.wait_ge(bank_read, i * 16 + (q_m1[l] + b + 1))
                        sq = SQT[:, b % 4, :]
                        t.link(dve.tensor_tensor(sq, sq, sq, mul))
                        t.link(dve.tensor_copy(AH[:, b, :], sq))
                        dve.tensor_tensor(AL[:, b, :], sq, as_f32(AH[:, b, :]), sub).then_inc(h1_ready, 1)
                    for k in range(KT):
                        filled(q_m2[l] + k, i * 16)
                        dve.tensor_tensor(XT[:, k, :], XT[:, k, :], src(q_m2[l] + k)[:, :], add)\
                           .then_inc(bank_read, 1)

            residual(q_out[0])
            norm(1)
            mlp(0)
            norm(2)

            IK = L1[:, 20, :]
            filled(q_ikm)
            dve.wait_ge(bank_read, q_ikm)
            dve.scalar_tensor_tensor(out=IK, in0=src(q_ikm)[:, :], scalar=-1.0 / HD, in1=IK,
                                     op0=mul, op1=add).then_inc(ik_centred, 1)
            dve.wait_ge(ik_centred, 1)
            dve.sem_inc(bank_read, 1)
            dve.wait_ge(n_rs, 1)
            t.link(dve.scalar_tensor_tensor(out=IK, in0=IK, scalar=pc2(LNW), in1=SQ1[0][:, 0, :],
                                            op0=mul, op1=mul))
            dve.tensor_scalar(IK, IK, pc2(LNB), None, add).then_inc(n_used, 1)
            u = 0
            for i in range(1, TT):
                for hh in range(NH):
                    wdt = P * (i + 1)
                    dve.wait_ge(bank_read, q_idx + u + 1)
                    wgt = IW[:, i, hh:hh + 1]
                    s = SCORE[:, i - 1, 0:wdt]
                    if hh == 0:
                        dve.tensor_scalar(s, RT[:, u % 4, 0:wdt], wgt, None, mul).then_inc(idx_acc, 1)
                    else:
                        dve.scalar_tensor_tensor(out=s, in0=RT[:, u % 4, 0:wdt], scalar=wgt, in1=s,
                                                 op0=mul, op1=add).then_inc(idx_acc, 1)
                    u += 1
                    dve.wait_ge(idx_acc, u)
            rounds = TOPK // 8
            scores = [SCORE[:, i - 1, 0:P * (i + 1)] for i in range(1, TT)]
            dve.wait_ge(idx_masked, TT - 1)
            with dve.Fori(0, rounds) as r:
                with t.loop(r, 2 * (TT - 1), rounds):
                    for i, sc in enumerate(scores):
                        t.step(dve.max(M8[:, i, :], sc))
                    t.settle()
                    dve.sem_inc(topk_rounds, 1)
                    for i, sc in enumerate(scores):
                        t.step(dve.match_replace(sc, M8[:, i, :], sc, TAKEN))
                    t.settle()
            dve.wait_ge(dist_ready, 1)
            for i in range(TT):
                wdt = P * (i + 1)
                d = DIST[:, W - wdt:W]
                lo = bias_off(i)
                t.step(dve.tensor_copy(BIAS[:, 1, lo:lo + wdt], d))
                if i == 0:
                    t.step(dve.tensor_copy(BIAS[:, 0, lo:lo + wdt], d))
                else:
                    s = SCORE[:, i - 1, 0:wdt]
                    t.link(dve.tensor_scalar(s, s, 0.5 * (CAUSAL_FILL + TAKEN), FAR, ALU.is_gt, mul))
                    t.step(dve.tensor_tensor(BIAS[:, 0, lo:lo + wdt], s, d, ALU.max))
            t.settle()

            dve.wait_ge(n_rs, 2)
            for g in range(2):
                t.step(dve.scalar_tensor_tensor(out=L1[:, 9 + 2 * g, :], in0=L1[:, 8 + 2 * g, :],
                                                scalar=pc2(DKN), in1=SQK[:, g, :], op0=mul, op1=mul))
            t.settle()
            for g in range(2):
                ins = dve.tensor_copy(L1[:, 8 + 2 * g, :], L1[:, 9 + 2 * g, :])
            ins.then_inc(n_used, 1)
            for n, (lo, wgt, rs) in enumerate(((0, QW[:, 0:1], SQ1[0]), (4, QW[:, 1:2], SQ1[1]),
                                               (12, pc2(MKN), SQ1[0]))):
                dve.wait_ge(n_rs, n + 3)
                dve.scalar_tensor_tensor(out=wide(L1[:, lo:lo + 4, :]), in0=wide(L1[:, lo:lo + 4, :]),
                                         scalar=wgt, in1=wide(rs), op0=mul, op1=mul).then_inc(n_used, 1)

            dve.sem_inc(at_z, 12)
            dve.sem_inc(at_on, 1)
            with dve.Fori(0, 2) as ty:
                with dve.Fori(0, 2) as jj:
                    pass16 = ty * 32 + jj * 16

                    def score(w):
                        i, p = w // 2 % 4, w % 2
                        wdt = P * (i + 1)
                        z = ZB[:, w % 8, 0:wdt]
                        dve.wait_ge(at_qk, pass16 + (w + 1))
                        if w >= 8:
                            dve.wait_ge(at_t, pass16 + (w - 7))
                        elif w == 0:
                            dve.wait_ge(at_on, ty * 4 + jj * 2 + 1)
                        slope = SLOPE[:, bass.ds(ty * 8 + jj * 4 + (w // 8 * 2 + p), 1)]
                        dist = BIAS[:, bass.ds(ty, 1), bias_off(i):bias_off(i) + wdt]\
                            .rearrange("p a w -> p (a w)")
                        dve.scalar_tensor_tensor(out=z, in0=dist, scalar=slope,
                                                 in1=bank[w % 4][:, 0:wdt], op0=mul, op1=add)\
                           .then_inc(at_z, 1)
                        dve.wait_ge(at_z, pass16 + (12 + w + 1))
                        dve.tensor_reduce(NMX[:, w:w + 1], z, AX.X, ALU.max, negate=True)\
                           .then_inc(at_mx, 1)

                    def rows_out(pair):
                        cols = slice(8 * pair, 8 * pair + 8)
                        dve.wait_ge(at_p, pass16 + (8 * pair + 8))
                        t.link(dve.reciprocal(RINV[:, cols], RSUM[:, cols]))
                        dve.wait_ge(at_o, pass16 + (8 * pair + 8))
                        dst = ON[:, :, bass.ds(ty * 512 + jj * 256 + pair * 128, 128)]\
                            .rearrange("p i (q d) -> p i q d", q=2)
                        dve.tensor_tensor(dst, bank[6 + pair][:, :].rearrange("p (i q d) -> p i q d", i=4, q=2),
                                          RINV[:, cols].rearrange("p (i q) -> p i q", i=4).unsqueeze(3)
                                          .broadcast_to([P, 4, 2, HD]), mul).then_inc(at_on, 1)

                    with t.loop(ty, 4, 2), t.loop(jj, 2, 2):
                        for w in range(16):
                            score(w)
                            if w == 12:
                                rows_out(0)
                        rows_out(1)
            for k in range(KT):
                dve.wait_ge(mix_hi, 2 + k + 1)
                dve.tensor_tensor(AL[:, k, :], src(q_mix + k)[:, :], as_f32(AH[:, k, :]), sub)\
                   .then_inc(bank_read, 1)
            residual(q_out[1])
            norm(3)
            mlp(1)

        @block.gpsimd
        def _(pool):
            t = Tally(pool, pool_step)
            mul = ALU.mult

            def select(x, base, pattern, cm, fill, op=ALU.is_ge):
                t.link(pool.affine_select(out=x, in_=x, pattern=pattern, compare_op=op, fill=fill,
                                          base=base, channel_multiplier=cm))

            t.step(pool.memset(IDENT, 0.0))
            t.step(pool.memset(ONES, 1.0))
            t.step(pool.memset(INCL, 1.0))
            t.step(pool.memset(STRICT, 1.0))
            t.step(pool.memset(HEADS2, 0.0))
            t.step(pool.memset(wide(MERGE), 0.0))
            t.step(pool.memset(SCANM, 1.0))
            t.settle()
            select(IDENT, 0, [[-1, P]], 1, 1.0, ALU.not_equal)
            select(INCL, 0, [[1, P]], -1, 0.0)
            select(STRICT, -1, [[1, P]], -1, 0.0)
            for p in range(2):
                t.link(pool.memset(HEADS2[p * HD:(p + 1) * HD, p * HD:(p + 1) * HD], 1.0))
            t.link(pool.memset(SCANM.rearrange("p (k t) -> p k t", k=4)[:, :, 0:1], 0.0))
            first = MERGE[:, 0, :].rearrange("p (n q) -> p n q", q=2)[:, :, 1]
            t.link(pool.memset(first, -1.0))
            select(first, 0, [[-2, P // 2]], 1, 0.0, ALU.is_equal)
            for lev in range(1, LEVELS):
                b = 1 << lev
                low = MERGE[:, lev, :].rearrange("p (n q w) -> p n q w", q=2, w=b)[:, :, 0, :]
                t.link(pool.memset(low, 1.0))
                select(low, -b, [[-2 * b, P // (2 * b)], [0, b]], 1, 0.0)
                select(low, 2 * b - 1, [[2 * b, P // (2 * b)], [0, b]], -1, 0.0)
            for g in range(16):
                col = (g % 2) * NH + g // 2
                t.step(pool.memset(SLOPE[:, col:col + 1], -float(np.float32(2.0) ** np.float32(-0.5 * (g + 1)))))
            t.settle()
            pool.memset(wide(M8), 0.0).then_inc(consts, 1)
            for s in range(2):
                t.step(pool.memset(STAGE[s][:, :, 0:3], 0.0))
            t.settle()
            pool.memset(NMX, 0.0).then_inc(pads_zero, 1)

            pool.wait_ge(l0_dve, 1)
            pool.memset(wide(SR), 0.0)
            pool.memset(wide(SG), 0.0)
            with pool.Fori(0, TT) as c:
                n = c + 1
                here = bass.ds(c * P, P)
                row = bass.ds(c, 1)

                def by_parity(x, p):
                    return x[:, row, :].rearrange("p o (j q) -> p (o j) q", q=2)[:, :, p]\
                        .unsqueeze(2).broadcast_to([P, 4, P])

                for p in range(2):
                    ins = pool.tensor_tensor(GTRI[p], INCL.unsqueeze(1).broadcast_to([P, 4, P]),
                                             by_parity(GLOG, p), mul)
                ins.then_inc(e_gtri, 1)
                pool.tensor_copy(KC, GK[:, :, here])
                pool.tensor_copy(QC, GQ[:, :, here])
                pool.tensor_copy(VGC, GV[:, :, here])
                pool.tensor_copy(VRC, V[:, :, here]).then_inc(e_copy, 1)
                pool.wait_ge(e_exp, n)
                pool.tensor_tensor(BD, BD, B[:, :, here], mul)
                pool.tensor_tensor(AD, AD, KK[:, :, here], mul).then_inc(e_ba, 1)
                pool.wait_ge(e_dt, n)
                for p in range(2):
                    ins = pool.tensor_tensor(LT[2 + p], DT[p], by_parity(BETA, p), mul)
                ins.then_inc(e_dmask, 1)
                pool.wait_ge(r_lt, n)
                with t.loop(c, 2, TT):
                    for g in range(2):
                        t.link(pool.tensor_tensor(QI[g], LT[g], MERGE[:, 0:1, :].broadcast_to([P, 4, P]), mul))
                        pool.tensor_tensor(QI[g], QI[g], IDENT.unsqueeze(1).broadcast_to([P, 4, P]),
                                           ALU.add).then_inc(inv_q0, 1)
                pool.wait_ge(f_y, n)
                pool.wait_ge(f_qs, n)

            def weight_lo(u, dyn=0):
                pool.wait_ge(hi_ready, dyn + (u + 1))
                w = unit_cols(u)
                pool.tensor_tensor(WL[:, u % 2, :, 0:w], RAW[:, u % 2, :, 0:w],
                                   as_f32(WH[:, u % 2, :, 0:w]), ALU.subtract)\
                    .then_inc(lo_ready, 1)

            def weights(first, last):
                with pool.Fori(0, (last - first) // 2) as i:
                    weight_lo(first, i * 2)
                    weight_lo(first + 1, i * 2)

            weights(0, 2)
            weights(2, u_kv)
            t.link(pool.iota(DIST.bitcast(I32), [[-1, W]], base=W - P, channel_multiplier=1))
            t.link(pool.tensor_copy(DIST, DIST.bitcast(I32)))
            pool.affine_select(out=DIST, in_=DIST, pattern=[[-1, W]], compare_op=ALU.is_ge, fill=FAR,
                               base=W - P, channel_multiplier=1).then_inc(dist_ready, 1)
            weight_lo(u_kv)
            weight_lo(u_kv + 1)
            weights(u_kv + 2, u_mqk)
            for i in range(1, TT):
                pool.wait_ge(idx_acc, NH * i)
                d = SCORE[:, i - 1, P * i:P * (i + 1)]
                pool.affine_select(out=d, in_=d, pattern=[[-1, P]], compare_op=ALU.is_ge,
                                   fill=CAUSAL_FILL, base=0, channel_multiplier=1).then_inc(idx_masked, 1)
            weights(u_mqk, u_out[1] + 2)
            def stage(pair, u):
                q = L1[:, bass.ds(pair, 1), :].rearrange("p a w -> p (a w)")
                k = L1[:, bass.ds(pair + 8, 1), :].rearrange("p a w -> p (a w)")
                pool.tensor_copy(QS[:, u, :], q)
                pool.tensor_copy(KS[:, u, :], k).then_inc(at_stage, 1)

            pool.wait_ge(n_used, 3)
            for u in range(2):
                stage(u, u)
            pool.wait_ge(n_used, 5)
            with pool.Fori(1, PAIRS) as b:
                for u in range(2):
                    pool.wait_ge(at_z, b * 16 + (4 + 8 * u))
                    stage(b * 2 + u, u)
            weights(u_out[1] + 2, u_mlp[1] + 32)


PAR64 = ("gdn_norm_w", "dsa_q_norm", "dsa_k_norm", "idx_k_ln_w", "idx_k_ln_b", "moba_q_norm",
         "moba_k_norm")
N_PAR = 2 + 8 + 1 + len(PAR64)
DVE_CHUNK = 20

_INS = ("x norm1_g norm2_g mlp_w1 mlp_w2 ev_w_in ev_w_out rwkv_mu rwkv_w0 rwkv_w2 rwkv_a0 rwkv_a2 "
        "rwkv_g2 rwkv_k_k rwkv_k_a rwkv_r_k rwkv_lnx_w rwkv_lnx_b gdn_conv_w gdn_a_log gdn_dt_bias "
        "gdn_norm_w od_w_in od_w_out dsa_q_norm dsa_k_norm idx_k_ln_w idx_k_ln_b moba_q_norm "
        "moba_k_norm").split()


def kernel(**inputs):
    import concourse.bacc as _bacc
    from concourse.bass_utils import run_bass_kernel_spmd as _run

    nc = _bacc.Bacc("TRN2", target_bir_lowering=False, num_devices=1)
    arrays, aps = {}, {}
    for name in _INS:
        x = np.ascontiguousarray(inputs[name])
        arrays[f"in_{name}_dram"] = x
        aps[name] = nc.dram_tensor(f"in_{name}_dram", x.shape, mybir.dt.from_np(x.dtype),
                                   kind="ExternalInput").ap()
    out = nc.dram_tensor("out_0_dram", (1, SEQ, D), F32, kind="ExternalOutput").ap()
    trunk_kernel(nc, aps, out)
    r = _run(nc, [arrays], core_ids=[0])
    return r.results[0]["out_0_dram"]
```
